# Optimizing a Trainium2 kernel written in Bass

```python
import math
import jax, jax.numpy as jnp
from jax import lax
import numpy as np

D_MODEL = 1024
BATCH = 1
SEQ = 256
DEPTH = 1

HEAD_DIM = 64
RWKV_HEADS = 6
RWKV_W = RWKV_HEADS * HEAD_DIM
D_DECAY_LORA = 64
D_AAA_LORA = 64
D_GATE_LORA = 128
RWKV_SPLITS = (RWKV_W, RWKV_W, RWKV_W, D_DECAY_LORA, D_AAA_LORA, D_GATE_LORA)
RWKV_COLS = sum(RWKV_SPLITS)
GN_EPS = 64e-5
NSA_Q_HEADS = 6
NSA_KV_GROUPS = 2
NSA_Q_PER_KV = NSA_Q_HEADS // NSA_KV_GROUPS
NSA_W = NSA_Q_HEADS * HEAD_DIM
NSA_KV_W = NSA_KV_GROUPS * HEAD_DIM
NSA_N_BRANCH = 3
NSA_SPLITS = (NSA_W,) + (NSA_KV_W,) * 6 + (NSA_Q_HEADS * NSA_N_BRANCH,)
NSA_COLS = sum(NSA_SPLITS)
CMP_LEN = 32
CMP_STRIDE = 16
CMP_HIDDEN = 128
SEL_LEN = 64
SEL_TOPK = 16
WINDOW = 512
Q_BLOCK = 64
FORCED_BONUS = 1e3
NEG_INF = -1e30
S5_GROUPS = 16
S5_CH = 16
S5_W = S5_GROUPS * S5_CH
S5_STATE = 64
DT_MIN = 0.001
DT_MAX = 0.1
D_MIX = RWKV_W + NSA_W + S5_W
N_IN = RWKV_COLS + NSA_COLS + S5_W
D_FF = 2816
CONV_W = 3
PLE_DIM = 256
NORM_EPS = 1e-6


def _split(z, sizes):
    cuts = [int(c) for c in np.cumsum(sizes)[:-1]]
    return jnp.split(z, cuts, axis=-1)

def rms_norm(x, g):
    xf = x.astype(jnp.float32)
    y = xf * lax.rsqrt(jnp.mean(xf * xf, axis=-1, keepdims=True) + NORM_EPS)
    return (y * g.astype(jnp.float32)).astype(x.dtype)

def masked_softmax(s, mask):
    s = jnp.where(mask, s, NEG_INF)
    return jnp.where(mask, jax.nn.softmax(s, axis=-1), 0.0)

def alibi_slopes(n):
    def pow2(m):
        start = 2.0 ** (-8.0 / m)
        return [start ** (i + 1) for i in range(m)]
    if math.log2(n).is_integer():
        return pow2(n)
    c = 2 ** math.floor(math.log2(n))
    return pow2(c) + pow2(2 * c)[0::2][: n - c]

def token_shift(z, mu):
    prev = jnp.pad(z, ((0, 0), (1, 0), (0, 0)))[:, :-1]
    return z + (prev - z) * mu

def rwkv7_mixer(z, w0, w2, a0, a2, g2, k_k, k_a, r_k, gn_w, gn_b):
    B, T, _ = z.shape
    H, N = RWKV_HEADS, HEAD_DIM
    z = z.astype(jnp.float32)
    r, k, v, wl, al, gl = _split(z, RWKV_SPLITS)
    w = -jax.nn.softplus(-(w0 + jnp.tanh(wl) @ w2)) - 0.5
    a = jax.nn.sigmoid(a0 + al @ a2)
    g = jax.nn.sigmoid(gl) @ g2
    heads = lambda t: t.reshape(B, T, H, N)
    kk = heads(k * k_k)
    kk = kk / jnp.maximum(jnp.sqrt(jnp.sum(kk * kk, axis=-1, keepdims=True)), 1e-12)
    k = k * (1.0 + (a - 1.0) * k_a)
    decay = jnp.exp(-jnp.exp(w))
    r_h, k_h, v_h, a_h, d_h = (heads(t) for t in (r, k, v, a, decay))

    def step(S, inp):
        r_t, d_t, k_t, v_t, kk_t, a_t = inp
        sa = jnp.einsum('bhij,bhj->bhi', S, -kk_t)
        S = S * d_t[:, :, None, :] + sa[..., None] * (kk_t * a_t)[:, :, None, :] + v_t[..., None] * k_t[:, :, None, :]
        return S, jnp.einsum('bhij,bhj->bhi', S, r_t)

    tm = lambda t: jnp.moveaxis(t, 1, 0)
    S0 = jnp.zeros((B, H, N, N), jnp.float32)
    _, o = lax.scan(step, S0, tuple(tm(t) for t in (r_h, d_h, k_h, v_h, kk, a_h)))
    o = jnp.moveaxis(o, 0, 1)
    mu = jnp.mean(o, axis=-1, keepdims=True)
    var = jnp.mean(jnp.square(o - mu), axis=-1, keepdims=True)
    o = ((o - mu) * lax.rsqrt(var + GN_EPS)).reshape(B, T, RWKV_W) * gn_w + gn_b
    bonus = jnp.sum(r_h * k_h * r_k.reshape(H, N), axis=-1, keepdims=True) * v_h
    return (o + bonus.reshape(B, T, RWKV_W)) * g

def nsa_mixer(z, pe_k, pe_v, w1_k, w2_k, w1_v, w2_v):
    B, T, _ = z.shape
    G, R, Dh = NSA_KV_GROUPS, NSA_Q_PER_KV, HEAD_DIM
    f32 = jnp.float32
    z = z.astype(f32)
    q, kc, vc, ks, vs, kw, vw, gl = _split(z, NSA_SPLITS)
    kv_heads = lambda t: t.reshape(B, T, G, Dh).transpose(0, 2, 1, 3)
    kc, vc, ks, vs, kw, vw = (kv_heads(t) for t in (kc, vc, ks, vs, kw, vw))

    n_cmp = (T - CMP_LEN) // CMP_STRIDE + 1
    cmp_start = jnp.arange(n_cmp) * CMP_STRIDE
    cmp_end = cmp_start + CMP_LEN - 1
    cmp_idx = cmp_start[:, None] + jnp.arange(CMP_LEN)[None, :]

    def compress(t, pe, w1, w2):
        blocks = (t[:, :, cmp_idx] + pe.astype(f32)).reshape(B, G, n_cmp, CMP_LEN * Dh)
        return jax.nn.gelu(blocks @ w1.astype(f32)) @ w2.astype(f32)

    k_cmp = compress(kc, pe_k, w1_k, w2_k)
    v_cmp = compress(vc, pe_v, w1_v, w2_v)

    n_sel = T // SEL_LEN
    k_top = min(SEL_TOPK, n_sel)
    ks_blk = ks.reshape(B, G, n_sel, SEL_LEN, Dh)
    vs_blk = vs.reshape(B, G, n_sel, SEL_LEN, Dh)
    blk_ids = jnp.arange(n_sel)
    blk_start = blk_ids * SEL_LEN
    overlap = ((cmp_start[:, None] < blk_start[None, :] + SEL_LEN)
               & (cmp_end[:, None] >= blk_start[None, :])).astype(f32)
    gather_blocks = jax.vmap(jax.vmap(lambda blk, sel: blk[sel]))

    win_len = WINDOW + Q_BLOCK - 1
    kw_pad = jnp.pad(kw, ((0, 0), (0, 0), (WINDOW, 0), (0, 0)))
    vw_pad = jnp.pad(vw, ((0, 0), (0, 0), (WINDOW, 0), (0, 0)))

    slopes = jnp.asarray(alibi_slopes(NSA_Q_HEADS), f32).reshape(G, R)[None, :, :, None, None]
    scale = HEAD_DIM ** -0.5
    n_qb = T // Q_BLOCK
    q_blocks = q.reshape(B, n_qb, Q_BLOCK, G, R, Dh).transpose(1, 0, 3, 4, 2, 5)
    g_blocks = jax.nn.sigmoid(gl).reshape(B, n_qb, Q_BLOCK, G, R, NSA_N_BRANCH).transpose(1, 0, 3, 4, 2, 5)

    def query_block(args):
        qb, gb, bi = args
        t0 = bi * Q_BLOCK
        t = t0 + jnp.arange(Q_BLOCK)
        d_c = t[:, None] - cmp_end[None, :]
        s_c = jnp.einsum('bgrqd,bgnd->bgrqn', qb, k_cmp) * scale - slopes * jnp.abs(d_c).astype(f32)
        p_c = masked_softmax(s_c, d_c >= 0)
        o_c = jnp.einsum('bgrqn,bgnd->bgrqd', p_c, v_cmp)
        imp = jnp.einsum('bgrqn,nj->bgqj', p_c, overlap)
        cur = t // SEL_LEN
        valid = blk_start[None, :] <= t[:, None]
        forced = (blk_ids[None, :] == 0) | (blk_ids[None, :] == cur[:, None]) | (blk_ids[None, :] == cur[:, None] - 1)
        score = jnp.where(valid, imp + FORCED_BONUS * forced.astype(f32), -jnp.inf)
        _, sel = lax.top_k(score, k_top)
        k_sel = gather_blocks(ks_blk, sel)
        v_sel = gather_blocks(vs_blk, sel)
        pos = sel[..., None] * SEL_LEN + jnp.arange(SEL_LEN)
        d_s = (t[:, None, None] - pos)[:, :, None]
        s_s = jnp.einsum('bgrqd,bgqnld->bgrqnl', qb, k_sel) * scale - slopes[..., None] * jnp.abs(d_s).astype(f32)
        p_s = masked_softmax(s_s.reshape(B, G, R, Q_BLOCK, k_top * SEL_LEN),
                             (d_s >= 0).reshape(B, G, 1, Q_BLOCK, k_top * SEL_LEN))
        o_s = jnp.einsum('bgrqnl,bgqnld->bgrqd', p_s.reshape(s_s.shape), v_sel)
        k_win = lax.dynamic_slice_in_dim(kw_pad, t0 + 1, win_len, axis=2)
        v_win = lax.dynamic_slice_in_dim(vw_pad, t0 + 1, win_len, axis=2)
        pos_w = t0 - WINDOW + 1 + jnp.arange(win_len)
        d_w = t[:, None] - pos_w[None, :]
        mask_w = (d_w >= 0) & (d_w < WINDOW) & (pos_w[None, :] >= 0)
        s_w = jnp.einsum('bgrqd,bgkd->bgrqk', qb, k_win) * scale - slopes * jnp.abs(d_w).astype(f32)
        o_w = jnp.einsum('bgrqk,bgkd->bgrqd', masked_softmax(s_w, mask_w), v_win)
        return gb[..., 0:1] * o_c + gb[..., 1:2] * o_s + gb[..., 2:3] * o_w

    o = lax.map(query_block, (q_blocks, g_blocks, jnp.arange(n_qb)))
    return o.transpose(1, 0, 4, 2, 3, 5).reshape(B, T, NSA_W)

def _complex_linear_combine(e1, e2):
    a1r, a1i, b1r, b1i = e1
    a2r, a2i, b2r, b2i = e2
    return (a1r * a2r - a1i * a2i, a1r * a2i + a1i * a2r,
            a2r * b1r - a2i * b1i + b2r, a2r * b1i + a2i * b1r + b2i)

def s5_mixer(u, lam_re, lam_im, log_dt, b_re, b_im, c_re, c_im, d_skip, w_glu):
    B, T, _ = u.shape
    f32 = jnp.float32
    u = u.astype(f32).reshape(B, T, S5_GROUPS, S5_CH)
    lam_re, lam_im = lam_re.astype(f32), lam_im.astype(f32)
    b_re, b_im, c_re, c_im = (t.astype(f32) for t in (b_re, b_im, c_re, c_im))
    dt = jnp.exp(log_dt.astype(f32))[:, None]
    mag = jnp.exp(lam_re * dt)
    ab_re, ab_im = mag * jnp.cos(lam_im * dt), mag * jnp.sin(lam_im * dt)
    den = lam_re * lam_re + lam_im * lam_im
    f_re = ((ab_re - 1.0) * lam_re + ab_im * lam_im) / den
    f_im = (ab_im * lam_re - (ab_re - 1.0) * lam_im) / den
    bb_re = f_re[..., None] * b_re - f_im[..., None] * b_im
    bb_im = f_re[..., None] * b_im + f_im[..., None] * b_re
    bu_re = jnp.einsum('gpc,btgc->btgp', bb_re, u)
    bu_im = jnp.einsum('gpc,btgc->btgp', bb_im, u)
    a_re = jnp.broadcast_to(ab_re, bu_re.shape)
    a_im = jnp.broadcast_to(ab_im, bu_im.shape)
    _, _, s_re, s_im = lax.associative_scan(_complex_linear_combine, (a_re, a_im, bu_re, bu_im), axis=1)
    y = (jnp.einsum('gcp,btgp->btgc', c_re, s_re) - jnp.einsum('gcp,btgp->btgc', c_im, s_im)
         + d_skip.astype(f32).reshape(S5_GROUPS, S5_CH) * u)
    y = jax.nn.gelu(y.reshape(B, T, S5_W))
    val, gate = jnp.split(y @ w_glu, 2, axis=-1)
    return val * jax.nn.sigmoid(gate)

def conv_ffn(x, w_up, conv_w, conv_b, w_down):
    hu = x @ w_up
    c = hu.shape[-1]
    hu = lax.conv_general_dilated(hu, conv_w[:, None, :], window_strides=(1,), padding=[(CONV_W - 1, 0)],
                                  dimension_numbers=('NWC', 'WIO', 'NWC'), feature_group_count=c) + conv_b
    gate, up = jnp.split(hu, 2, axis=-1)
    return (jax.nn.gelu(gate, approximate=True) * up) @ w_down

def first_inputs(seed: int = 0) -> dict:
    key = jax.random.key(seed)
    keys = iter(jax.random.split(key, 48))
    f32 = jnp.float32

    def nrm(shape, scale):
        return scale * jax.random.normal(next(keys), shape, f32)

    def gain(shape):
        return 1.0 + 0.02 * jax.random.normal(next(keys), shape, f32)

    def unif(shape, lo, hi):
        return jax.random.uniform(next(keys), shape, f32, lo, hi)

    L = DEPTH
    n = jnp.arange(S5_STATE, dtype=f32)
    return {
        'x': nrm((BATCH, SEQ, D_MODEL), 1.0),
        'p': nrm((DEPTH, BATCH, SEQ, PLE_DIM), 1.0),
        'pre_mix_norm': gain((L, D_MODEL)),
        'post_mix_norm': gain((L, D_MODEL)),
        'pre_ffn_norm': gain((L, D_MODEL)),
        'post_ffn_norm': gain((L, D_MODEL)),
        'w_in': nrm((L, D_MODEL, N_IN), D_MODEL ** -0.5),
        'w_out': nrm((L, D_MIX, D_MODEL), D_MIX ** -0.5),
        'shift_mu': unif((L, RWKV_COLS), 0.0, 1.0),
        'rw_w0': unif((L, RWKV_W), -5.0, -1.0),
        'rw_w2': nrm((L, D_DECAY_LORA, RWKV_W), 0.1),
        'rw_a0': nrm((L, RWKV_W), 0.1),
        'rw_a2': nrm((L, D_AAA_LORA, RWKV_W), 0.3 * D_AAA_LORA ** -0.5),
        'rw_g2': nrm((L, D_GATE_LORA, RWKV_W), D_GATE_LORA ** -0.5),
        'rw_k_k': 0.85 + nrm((L, RWKV_W), 0.02),
        'rw_k_a': gain((L, RWKV_W)),
        'rw_r_k': nrm((L, RWKV_W), 0.1),
        'rw_gn_w': gain((L, RWKV_W)),
        'rw_gn_b': nrm((L, RWKV_W), 0.02),
        'cmp_pe_k': nrm((L, CMP_LEN, HEAD_DIM), 0.02),
        'cmp_pe_v': nrm((L, CMP_LEN, HEAD_DIM), 0.02),
        'cmp_w1_k': nrm((L, CMP_LEN * HEAD_DIM, CMP_HIDDEN), (CMP_LEN * HEAD_DIM) ** -0.5),
        'cmp_w2_k': nrm((L, CMP_HIDDEN, HEAD_DIM), CMP_HIDDEN ** -0.5),
        'cmp_w1_v': nrm((L, CMP_LEN * HEAD_DIM, CMP_HIDDEN), (CMP_LEN * HEAD_DIM) ** -0.5),
        'cmp_w2_v': nrm((L, CMP_HIDDEN, HEAD_DIM), CMP_HIDDEN ** -0.5),
        's5_lam_re': -0.5 + nrm((L, S5_GROUPS, S5_STATE), 0.01),
        's5_lam_im': math.pi * n + nrm((L, S5_GROUPS, S5_STATE), 0.01),
        's5_log_dt': unif((L, S5_GROUPS), math.log(DT_MIN), math.log(DT_MAX)),
        's5_b_re': nrm((L, S5_GROUPS, S5_STATE, S5_CH), (2 * S5_CH) ** -0.5),
        's5_b_im': nrm((L, S5_GROUPS, S5_STATE, S5_CH), (2 * S5_CH) ** -0.5),
        's5_c_re': nrm((L, S5_GROUPS, S5_CH, S5_STATE), (2 * S5_STATE) ** -0.5),
        's5_c_im': nrm((L, S5_GROUPS, S5_CH, S5_STATE), (2 * S5_STATE) ** -0.5),
        's5_d': nrm((L, S5_W), 1.0),
        's5_w_glu': nrm((L, S5_W, 2 * S5_W), S5_W ** -0.5),
        'w_up': nrm((L, D_MODEL, 2 * D_FF), D_MODEL ** -0.5),
        'conv_w': nrm((L, CONV_W, 2 * D_FF), CONV_W ** -0.5),
        'conv_b': nrm((L, 2 * D_FF), 0.02),
        'w_down': nrm((L, D_FF, D_MODEL), D_FF ** -0.5),
        'w_ple': nrm((L, PLE_DIM, D_MODEL), PLE_DIM ** -0.5),
        'ple_norm': gain((L, D_MODEL)),
        'w_ple_gate': nrm((L, D_MODEL, D_MODEL), D_MODEL ** -0.5),
    }

def first_block(x, p, pre_mix_norm, post_mix_norm, pre_ffn_norm, post_ffn_norm, w_in, w_out,
              shift_mu, rw_w0, rw_w2, rw_a0, rw_a2, rw_g2, rw_k_k, rw_k_a, rw_r_k, rw_gn_w, rw_gn_b,
              cmp_pe_k, cmp_pe_v, cmp_w1_k, cmp_w2_k, cmp_w1_v, cmp_w2_v,
              s5_lam_re, s5_lam_im, s5_log_dt, s5_b_re, s5_b_im, s5_c_re, s5_c_im, s5_d, s5_w_glu,
              w_up, conv_w, conv_b, w_down, w_ple, ple_norm, w_ple_gate):
    h = x
    for i in range(DEPTH):
        z = rms_norm(h, pre_mix_norm[i]) @ w_in[i]
        z_rw, z_nsa, z_s5 = _split(z, (RWKV_COLS, NSA_COLS, S5_W))
        o_rw = rwkv7_mixer(token_shift(z_rw, shift_mu[i]), rw_w0[i], rw_w2[i], rw_a0[i], rw_a2[i], rw_g2[i],
                           rw_k_k[i], rw_k_a[i], rw_r_k[i], rw_gn_w[i], rw_gn_b[i])
        o_nsa = nsa_mixer(z_nsa, cmp_pe_k[i], cmp_pe_v[i], cmp_w1_k[i], cmp_w2_k[i], cmp_w1_v[i], cmp_w2_v[i])
        o_s5 = s5_mixer(z_s5, s5_lam_re[i], s5_lam_im[i], s5_log_dt[i], s5_b_re[i], s5_b_im[i],
                        s5_c_re[i], s5_c_im[i], s5_d[i], s5_w_glu[i])
        mix = jnp.concatenate([o_rw, o_nsa, o_s5], axis=-1).astype(h.dtype) @ w_out[i]
        h = h + rms_norm(mix, post_mix_norm[i])
        f = conv_ffn(rms_norm(h, pre_ffn_norm[i]), w_up[i], conv_w[i], conv_b[i], w_down[i])
        h = h + rms_norm(f, post_ffn_norm[i])
        e = rms_norm(p[i] @ w_ple[i], ple_norm[i])
        gate = jax.nn.sigmoid((h @ w_ple_gate[i]).astype(jnp.float32)).astype(h.dtype)
        h = h + gate * e
    return h


DEPTH_2 = 2

N_POOL_LAYERS = DEPTH_2 // 2
N_ATTN_LAYERS = DEPTH_2 - N_POOL_LAYERS
POOL_WINDOWS = (2, 4, 8, 16)
N_POOL_GROUPS = len(POOL_WINDOWS)
POOL_GROUP_DIM = D_MODEL // N_POOL_GROUPS
BRANCHES = ((128, 1), (512, 4), (2048, 16))
N_BRANCHES = len(BRANCHES)
N_HEADS = D_MODEL // HEAD_DIM
D_ATTN = N_HEADS * HEAD_DIM
ATTN_BLOCK = 128
CONV_WIDTH = 3
EPS = 1e-6
ADA_SCALE = 0.5


def _rmsnorm(x, g):
    x32 = x.astype(jnp.float32)
    y = x32 * lax.rsqrt(jnp.mean(x32 * x32, axis=-1, keepdims=True) + EPS)
    return (y * g.astype(jnp.float32)).astype(x.dtype)

def _modulate(h, shift, scale):
    return h * (1 + scale[:, None, :]) + shift[:, None, :]

def _alibi_slopes(n):
    def pow2(m):
        start = 2.0 ** (-(2.0 ** -(math.log2(m) - 3)))
        return [start ** (i + 1) for i in range(m)]
    if math.log2(n).is_integer():
        s = pow2(n)
    else:
        c = 2 ** math.floor(math.log2(n))
        s = pow2(c) + pow2(2 * c)[0::2][: n - c]
    s = np.asarray(s, dtype=np.float32)
    return -np.sort(-s)

def _pool_mixer(h, w_in, w_grp, scale, w_out):
    b, s, _ = h.shape
    u = (h @ w_in).reshape(b, s, N_POOL_GROUPS, POOL_GROUP_DIM)
    u32 = u.astype(jnp.float32)
    csum = jnp.cumsum(u32, axis=1)
    t = jnp.arange(s)
    outs = []
    for g, w in enumerate(POOL_WINDOWS):
        cs = csum[:, :, g]
        lag = jnp.pad(cs, ((0, 0), (w, 0), (0, 0)))[:, :s]
        count = jnp.minimum(t + 1, w).astype(jnp.float32)[None, :, None]
        pooled = (cs - lag) / count - u32[:, :, g]
        outs.append(jnp.einsum('bsc,cd->bsd', pooled.astype(h.dtype), w_grp[g]))
    y = jnp.concatenate(outs, axis=-1) * scale
    return y @ w_out

def _causal_dwconv(a, w, bias):
    s = a.shape[1]
    ap = jnp.pad(a, ((0, 0), (CONV_WIDTH - 1, 0), (0, 0)))
    y = bias
    for k in range(CONV_WIDTH):
        y = y + ap[:, k:k + s] * w[k]
    return y

def _conv_ffn(h, w_up, conv_w, conv_b, w_down):
    a, v = jnp.split(h @ w_up, 2, axis=-1)
    a = _causal_dwconv(a, conv_w, conv_b)
    return (jax.nn.silu(a) * v) @ w_down

def _dilated_branch(q, k, v, window, dilation, slopes):
    b, s, h, dh = q.shape
    n_steps = window // dilation
    blk = max(ATTN_BLOCK, n_steps)
    sub_len = s // dilation
    nb = -(-sub_len // blk)
    sub_pad = nb * blk

    def to_sub(t):
        t = t.reshape(b, sub_len, dilation, h, dh).transpose(0, 2, 1, 3, 4).reshape(b * dilation, sub_len, h, dh)
        return jnp.pad(t, ((0, 0), (0, sub_pad - sub_len), (0, 0), (0, 0)))

    def with_prev(t):
        tb = t.reshape(-1, nb, blk, h, dh)
        prev = jnp.pad(tb, ((0, 0), (1, 0), (0, 0), (0, 0), (0, 0)))[:, :nb]
        return jnp.concatenate([prev, tb], axis=2)

    qb = to_sub(q).reshape(-1, nb, blk, h, dh)
    kb = with_prev(to_sub(k))
    vb = with_prev(to_sub(v))

    scores = jnp.einsum('bnqhd,bnkhd->bnhqk', qb, kb).astype(jnp.float32) * (dh ** -0.5)
    qi = jnp.arange(blk)[:, None] + blk
    ki = jnp.arange(2 * blk)[None, :]
    delta = qi - ki
    key_idx = jnp.arange(nb)[:, None] * blk + jnp.arange(2 * blk)[None, :] - blk
    valid = ((delta >= 0) & (delta <= n_steps))[None] & (key_idx >= 0)[:, None, :]
    bias = -slopes[:, None, None] * (delta * dilation).astype(jnp.float32)[None]
    scores = jnp.where(valid[None, :, None], scores + bias[None, None], -jnp.inf)
    lse = jax.nn.logsumexp(scores, axis=-1)
    p = jnp.exp(scores - lse[..., None])
    out = jnp.einsum('bnhqk,bnkhd->bnqhd', p.astype(v.dtype), vb)

    out = out.reshape(b, dilation, sub_pad, h, dh)[:, :, :sub_len]
    out = out.transpose(0, 2, 1, 3, 4).reshape(b, s, h, dh)
    lse = lse.transpose(0, 1, 3, 2).reshape(b, dilation, sub_pad, h)[:, :, :sub_len]
    lse = lse.transpose(0, 2, 1, 3).reshape(b, s, h)
    return out, lse

def _dilated_attention(h, kv, w_q, w_o, slopes):
    b, s, _ = h.shape
    q = (h @ w_q).reshape(b, s, N_BRANCHES, N_HEADS, HEAD_DIM)
    outs, lses = [], []
    for g, (window, dil) in enumerate(BRANCHES):
        o, l = _dilated_branch(q[:, :, g], kv[:, :, 0, g], kv[:, :, 1, g], window, dil, slopes[g])
        outs.append(o)
        lses.append(l)
    wts = jax.nn.softmax(jnp.stack(lses, axis=0), axis=0)
    o = jnp.sum(wts[..., None] * jnp.stack(outs, axis=0).astype(jnp.float32), axis=0)
    return o.reshape(b, s, D_ATTN).astype(h.dtype) @ w_o

def second_inputs(seed: int = 0) -> dict:
    key = jax.random.key(seed)
    ks = jax.random.split(key, 24)

    def nrm(k, shape, scale):
        return jax.random.normal(k, shape, jnp.float32) * scale

    D, F, G = D_MODEL, D_FF, N_BRANCHES
    return {
        "x": nrm(ks[0], (BATCH, SEQ, D), 1.0),
        "c": nrm(ks[1], (BATCH, D), 1.0),
        "ada_w": nrm(ks[2], (DEPTH_2, D, 6 * D), ADA_SCALE * D ** -0.5),
        "ada_b": nrm(ks[3], (DEPTH_2, 6 * D), 0.02),
        "norm1_g": 1.0 + nrm(ks[4], (DEPTH_2, D), 0.05),
        "norm2_g": 1.0 + nrm(ks[5], (DEPTH_2, D), 0.05),
        "pool_w_in": nrm(ks[6], (N_POOL_LAYERS, D, D), D ** -0.5),
        "pool_w_grp": nrm(ks[7], (N_POOL_LAYERS, N_POOL_GROUPS, POOL_GROUP_DIM, POOL_GROUP_DIM), POOL_GROUP_DIM ** -0.5),
        "pool_scale": 1.0 + nrm(ks[8], (N_POOL_LAYERS, D), 0.1),
        "pool_w_out": nrm(ks[9], (N_POOL_LAYERS, D, D), D ** -0.5),
        "kv_norm_g": 1.0 + nrm(ks[10], (D,), 0.05),
        "kv_ada_w": nrm(ks[11], (D, 2 * D), ADA_SCALE * D ** -0.5),
        "kv_ada_b": nrm(ks[12], (2 * D,), 0.02),
        "w_kv": nrm(ks[13], (D, 2 * G * D_ATTN), D ** -0.5),
        "attn_w_q": nrm(ks[14], (N_ATTN_LAYERS, D, G * D_ATTN), D ** -0.5),
        "attn_w_o": nrm(ks[15], (N_ATTN_LAYERS, D_ATTN, D), D_ATTN ** -0.5),
        "ffn_w_up": nrm(ks[16], (DEPTH_2, D, 2 * F), D ** -0.5),
        "ffn_conv_w": nrm(ks[17], (DEPTH_2, CONV_WIDTH, F), CONV_WIDTH ** -0.5),
        "ffn_conv_b": nrm(ks[18], (DEPTH_2, F), 0.02),
        "ffn_w_down": nrm(ks[19], (DEPTH_2, F, D), F ** -0.5),
        "final_g": 1.0 + nrm(ks[20], (D,), 0.05),
    }

def second_block(x, c, ada_w, ada_b, norm1_g, norm2_g, pool_w_in, pool_w_grp, pool_scale, pool_w_out,
              kv_norm_g, kv_ada_w, kv_ada_b, w_kv, attn_w_q, attn_w_o,
              ffn_w_up, ffn_conv_w, ffn_conv_b, ffn_w_down, final_g):
    b, s, _ = x.shape
    cond = jax.nn.silu(c)
    slopes = jnp.asarray(_alibi_slopes(N_BRANCHES * N_HEADS)).reshape(N_BRANCHES, N_HEADS)
    kv = None
    for layer in range(DEPTH_2):
        mod = cond @ ada_w[layer] + ada_b[layer]
        sh1, sc1, g1, sh2, sc2, g2 = jnp.split(mod, 6, axis=-1)
        h = _modulate(_rmsnorm(x, norm1_g[layer]), sh1, sc1)
        if layer < N_POOL_LAYERS:
            y = _pool_mixer(h, pool_w_in[layer], pool_w_grp[layer], pool_scale[layer], pool_w_out[layer])
        else:
            if layer == N_POOL_LAYERS:
                kv_shift, kv_scale = jnp.split(cond @ kv_ada_w + kv_ada_b, 2, axis=-1)
                hkv = _modulate(_rmsnorm(x, kv_norm_g), kv_shift, kv_scale)
                kv = (hkv @ w_kv).reshape(b, s, 2, N_BRANCHES, N_HEADS, HEAD_DIM)
            j = layer - N_POOL_LAYERS
            y = _dilated_attention(h, kv, attn_w_q[j], attn_w_o[j], slopes)
        x = x + g1[:, None, :] * y
        h = _modulate(_rmsnorm(x, norm2_g[layer]), sh2, sc2)
        x = x + g2[:, None, :] * _conv_ffn(h, ffn_w_up[layer], ffn_conv_w[layer], ffn_conv_b[layer], ffn_w_down[layer])
    return _rmsnorm(x, final_g)


def setup_inputs(seed=0):
    out = dict(first_inputs(seed))
    for name, value in second_inputs(seed + 1).items():
        if name != "x":
            out[name + "_2"] = value
    return out


def reference(
    x, p, pre_mix_norm, post_mix_norm, pre_ffn_norm, post_ffn_norm, w_in, w_out, shift_mu,
    rw_w0, rw_w2, rw_a0, rw_a2, rw_g2, rw_k_k, rw_k_a, rw_r_k, rw_gn_w, rw_gn_b, cmp_pe_k,
    cmp_pe_v, cmp_w1_k, cmp_w2_k, cmp_w1_v, cmp_w2_v, s5_lam_re, s5_lam_im, s5_log_dt, s5_b_re,
    s5_b_im, s5_c_re, s5_c_im, s5_d, s5_w_glu, w_up, conv_w, conv_b, w_down, w_ple, ple_norm,
    w_ple_gate, c_2, ada_w_2, ada_b_2, norm1_g_2, norm2_g_2, pool_w_in_2, pool_w_grp_2,
    pool_scale_2, pool_w_out_2, kv_norm_g_2, kv_ada_w_2, kv_ada_b_2, w_kv_2, attn_w_q_2,
    attn_w_o_2, ffn_w_up_2, ffn_conv_w_2, ffn_conv_b_2, ffn_w_down_2, final_g_2,
):
    x = first_block(
        x, p, pre_mix_norm, post_mix_norm, pre_ffn_norm, post_ffn_norm, w_in, w_out, shift_mu,
        rw_w0, rw_w2, rw_a0, rw_a2, rw_g2, rw_k_k, rw_k_a, rw_r_k, rw_gn_w, rw_gn_b, cmp_pe_k,
        cmp_pe_v, cmp_w1_k, cmp_w2_k, cmp_w1_v, cmp_w2_v, s5_lam_re, s5_lam_im, s5_log_dt,
        s5_b_re, s5_b_im, s5_c_re, s5_c_im, s5_d, s5_w_glu, w_up, conv_w, conv_b, w_down, w_ple,
        ple_norm, w_ple_gate,
    )
    return second_block(
        x, c_2, ada_w_2, ada_b_2, norm1_g_2, norm2_g_2, pool_w_in_2, pool_w_grp_2, pool_scale_2,
        pool_w_out_2, kv_norm_g_2, kv_ada_w_2, kv_ada_b_2, w_kv_2, attn_w_q_2, attn_w_o_2,
        ffn_w_up_2, ffn_conv_w_2, ffn_conv_b_2, ffn_w_down_2, final_g_2,
    )


_drawn_inputs = setup_inputs


def setup_inputs(seed=0):
    import zlib

    import numpy as np

    out = dict(_drawn_inputs(seed))
    spreads = {}
    factors = {'post_mix_norm': 3.738,
     'pre_ffn_norm': 3.498,
     'post_ffn_norm': 4.765,
     'rw_k_k': 7.73,
     'rw_k_a': 4.228,
     'rw_gn_w': 4.828,
     'rw_gn_b': 4.522,
     'cmp_pe_k': 64.0,
     'cmp_pe_v': 8.0,
     's5_lam_re': 64.0,
     's5_lam_im': 25.6,
     's5_log_dt': 26.544,
     's5_b_re': 36.896,
     's5_b_im': 35.752,
     's5_c_re': 36.808,
     's5_c_im': 36.28,
     'conv_b': 3.578,
     'ple_norm': 8.0,
     'ada_b_2': 3.27,
     'norm1_g_2': 7.089,
     'norm2_g_2': 4.892,
     'pool_scale_2': 3.654,
     'kv_norm_g_2': 8.0,
     'kv_ada_b_2': 8.0,
     'ffn_conv_b_2': 8.0}
    for name, (base, spread) in spreads.items():
        noise = np.random.default_rng([zlib.crc32(name.encode()), seed]).standard_normal(out[name].shape)
        drawn = base * np.exp(spread * noise) if base else spread * noise
        out[name] = __import__('jax').numpy.asarray(drawn.astype(out[name].dtype))
    for name, factor in factors.items():
        out[name] = (out[name] * factor).astype(out[name].dtype)
    return out
```

```python
import math
from contextlib import ExitStack

import concourse.bass as bass
from concourse import mybir

F32 = mybir.dt.float32
ALU = mybir.AluOpType
ACT = mybir.ActivationFunctionType
AX = mybir.AxisListType

P = 128
T = 256
D = 1024
KT = D // P
FF = 2816
FT = FF // P
HD = 64
BANKS = 8
SLOTS = 4
SLOT = 4096
FAR = 1.0e32
NCMP = 15
EPS = 1e-6
GN_EPS = 64e-5
MAGIC = 12582912.0
RW_TILES = 11
Q_COL, KC_COL, VC_COL, KS_COL, VS_COL, KW_COL, VW_COL, GATE_COL, U_COL = (
    1408, 1792, 1920, 2048, 2176, 2304, 2432, 2560, 2578)
N_IN = 2834


def nsa_slopes(n):
    def pow2(m):
        return [2.0 ** (-8.0 / m * (i + 1)) for i in range(m)]
    c = 2 ** math.floor(math.log2(n))
    return pow2(c) + pow2(2 * c)[0::2][: n - c]


def dilated_slopes(n):
    def pow2(m):
        start = 2.0 ** (-(2.0 ** -(math.log2(m) - 3)))
        return [start ** (i + 1) for i in range(m)]
    c = 2 ** math.floor(math.log2(n))
    s = pow2(n) if c == n else pow2(c) + pow2(2 * c)[0::2][: n - c]
    return sorted(s, reverse=True)


class Ledger:

    def __init__(self, eng, own):
        self.eng, self.own, self.count, self.open = eng, own, {}, {}

    def emit(self, ins, signal=None, value=None):
        signal = signal or self.own
        ins.then_inc(signal, 1)
        self.count[signal.name] = value or self.count.get(signal.name, 0) + 1
        self.open[signal.name] = (signal, self.count[signal.name])

    def settle(self):
        for signal, value in self.open.values():
            self.eng.wait_ge(signal, value)
        self.open = {}


def two_block_kernel(nc, a, out):
    ctx = ExitStack()
    with ctx:
        sems = {}

        def sem(name):
            if name not in sems:
                sems[name] = ctx.enter_context(nc.semaphore(name))
            return sems[name]

        def sb(name, cols, rows=P):
            return ctx.enter_context(nc.sbuf_tensor(name, [rows, cols], F32))

        def shaped(flat, *dims):
            names = "abcdef"[:len(dims)]
            return flat.rearrange(f"p ({' '.join(names)}) -> p {' '.join(names)}", **dict(zip(names, dims)))

        ident = sb("ident", P)
        ones_mean = sb("ones_mean", P)
        head_ones = sb("head_ones", P)
        head_mean = sb("head_mean", P)
        masks = shaped(sb("masks", 6 * P), 6, P)
        U8, L8M, L16M, L32M, U32S, U32I = (masks[:, i, :] for i in range(6))
        scan_keep = sb("scan_keep", T)
        dist = shaped(sb("dist", 2 * T), 2, T)
        late = sb("late", 10 * T)
        bdist = shaped(late[:, 0:6 * T], 3, 2, T)
        inv_count = shaped(late[:, 6 * T:10 * T], 4, T)
        sums = shaped(late[:, 0:1024], 2, 512)
        cond_wide = shaped(late[:, 1024:1280], KT, 32)
        cdist = shaped(sb("cdist", 30), 2, NCMP)
        cbias = shaped(sb("cbias", 180), 2, 6, NCMP)
        block3 = sb("block3", 3)
        block2 = sb("block2", 2)
        row_ok = sb("row_ok", 2)
        one_each = sb("one_each", 1)
        par = sb("par", 6 * P + 8)
        dt_rows = sb("dt_rows", 2)
        dt_wide = sb("dt_wide", P)
        drv = sb("drv", 32)
        cond = sb("cond", KT)
        mod = sb("mod", 112)
        gsc = sb("gsc", 40)
        pT = shaped(sb("pT", 2 * T), 2, T)
        h = shaped(sb("h", KT * T), KT, T)
        hn = shaped(sb("hn", KT * T), KT, T)
        rs = shaped(sb("rs", 3 * T), 3, T)
        ring = shaped(sb("ring", SLOTS * SLOT), SLOTS, SLOT)
        ARENA = 25480
        arena = sb("arena", ARENA)

        def at(off, *dims):
            n = math.prod(dims)
            assert off + n <= ARENA, (off, dims)
            flat = arena[:, off:off + n]
            return flat if len(dims) == 1 else shaped(flat, *dims)

        banks = ctx.enter_context(nc.psum_tensor("banks", [P, BANKS, 512], F32))

        xtok = at(0, 2, D)
        stage = at(2048, 6, P)
        ptok = at(2816, 2, T)
        zs = at(0, RW_TILES, T)
        kcs = at(2816, 4, T)
        kd = at(3840, 4, T)
        qT = at(4864, 3, T)
        vtok = at(5632, 2, T)
        gate = at(6144, 2, 18)
        uT = at(6208, 2, T)
        lora_w = at(6720, 384)
        g2_w = at(7104, 384)
        cw2 = at(7488, 3, HD)
        M0 = 7680
        tabC, tabS = at(M0, 8, T), at(M0 + 2048, 8, T)
        BT = at(M0 + 4096, 2, 2, P)
        CT = at(M0 + 4608, 2, 2, P)
        wglu = at(M0 + 5120, 2, 512)
        s5w = at(M0 + 6144, 2, 5, 2, T)
        s5v = at(M0 + 11264, 24, 8)
        bfull = at(M0 + 11456, 2, 8, 16)
        bmul = at(M0 + 11712, 2, 8, 16)
        bdup = at(M0 + 11968, 2, 8, 2, 16)
        cdup = at(M0 + 12480, 2, 2, P)
        ygel = at(M0 + 12992, 2, T)
        s5g = at(M0 + 13504, 2, T)
        powr = at(M0 + 14016, 2, 8)
        ptmp = at(M0 + 14032, 2, 8, P)
        assert M0 + 16080 <= ARENA
        nsc = at(M0 + 6144, 2, 2, T)
        npt = at(M0 + 7168, 2, 4, P)
        NB = M0 + 15312
        otok = at(M0 + 11712, 2, 384)
        hid = at(NB + 768, 2, 32)
        kcT = at(NB + 896, 2, NCMP)
        vbd = at(NB + 928, 2, 3, HD)
        csc = at(NB + 1312, 2, 6, 32)
        cst = at(NB + 1696, 2, 4, 6)
        nst = at(NB + 1744, 4, 4, 2)
        cpt = at(M0 + 14032, 2, P)
        hidv = at(M0 + 14288, 2, 3, 32)
        peh = at(NB + 1776, 2)
        W = [at(M0 + 768 * i, 3, T) for i in range(12)]
        tok4 = at(M0 + 9216, 4, 3, P)
        AM = at(M0 + 10752, 3, 2, P)
        AU = at(M0 + 11520, 3, 2, P)
        KEEP = [at(M0 + 12288 + 768 * i, 2, 3, P) for i in range(4)]
        TM = [at(M0 + 768 * i, 2, 3, P) for i in range(6)] + [at(M0 + 15360 + 768 * i, 2, 3, P) for i in range(3)]
        EB, HB = at(M0, 4, 3, P), at(M0 + 1536, 4, 3, P)
        ST = at(2816, 7, 3, P)
        Pend = at(5632, 3, 8)
        assert M0 + 17664 <= ARENA
        act = at(0, FT, T)
        ct = at(5632, 2, 2, T)
        eT = at(8192, KT, T)
        sqb, tn, yb, eb = eT, eT, at(10240, KT, T), at(0, KT, T)
        pu = at(10240, KT, T)
        pw = at(12288, 2, 2, T)
        dk, dv, dq = at(0, 24, T), at(6144, 2, 3072), at(12288, 24, T)
        dsc = at(18432, 2, 3 * T)
        dpt = at(19968, 2, 6, P)
        dotok = at(21504, 2, D)
        dst = at(23552, 4, 4)
        hn2 = at(18432, KT, T)
        outt = at(0, 2, D)
        dint = at(18432, 2, T)

        def rows(x, pat, **k):
            return x.rearrange(pat, **k)
        vecs = [("pre_mix", rows(a["pre_mix_norm"], "l (j p) -> (l j) p", p=P)),
                ("post_mix", rows(a["post_mix_norm"], "l (j p) -> (l j) p", p=P)),
                ("pre_ffn", rows(a["pre_ffn_norm"], "l (j p) -> (l j) p", p=P)),
                ("post_ffn", rows(a["post_ffn_norm"], "l (j p) -> (l j) p", p=P)),
                ("ple_norm", rows(a["ple_norm"], "l (j p) -> (l j) p", p=P)),
                ("norm1", rows(a["norm1_g_2"], "l (j p) -> (l j) p", p=P)),
                ("norm2", rows(a["norm2_g_2"], "l (j p) -> (l j) p", p=P)),
                ("kv_norm", rows(a["kv_norm_g_2"], "(j p) -> j p", p=P)),
                ("final", rows(a["final_g_2"], "(j p) -> j p", p=P)),
                ("c", rows(a["c_2"], "l (j p) -> (l j) p", p=P)),
                ("pool_scale", rows(a["pool_scale_2"], "l (j p) -> (l j) p", p=P)),
                ("mu", rows(a["shift_mu"], "l (j p) -> (l j) p", p=P)),
                ("w0", rows(a["rw_w0"], "l (j p) -> (l j) p", p=P)),
                ("a0", rows(a["rw_a0"], "l (j p) -> (l j) p", p=P)),
                ("k_k", rows(a["rw_k_k"], "l (j p) -> (l j) p", p=P)),
                ("k_a", rows(a["rw_k_a"], "l (j p) -> (l j) p", p=P)),
                ("r_k", rows(a["rw_r_k"], "l (j p) -> (l j) p", p=P)),
                ("gn_w", rows(a["rw_gn_w"], "l (j p) -> (l j) p", p=P)),
                ("gn_b", rows(a["rw_gn_b"], "l (j p) -> (l j) p", p=P)),
                ("pe_k", rows(a["cmp_pe_k"], "l (j q) d -> (l j) (q d)", q=2)),
                ("pe_v", rows(a["cmp_pe_v"], "l (j q) d -> (l j) (q d)", q=2)),
                ("s5_d", rows(a["s5_d"], "l (j p) -> (l j) p", p=P)),
                ("lam_re", rows(a["s5_lam_re"], "l (j g) n -> (l j) (g n)", g=2)),
                ("lam_im", rows(a["s5_lam_im"], "l (j g) n -> (l j) (g n)", g=2)),
                ("ada_b", rows(a["ada_b_2"], "l (j p) -> (l j) p", p=P)),
                ("kv_ada_b", rows(a["kv_ada_b_2"], "(j p) -> j p", p=P)),
                ("conv_w", rows(a["conv_w"], "l w (j p) -> (l w j) p", p=P)),
                ("conv_b", rows(a["conv_b"], "l (j p) -> (l j) p", p=P)),
                ("fconv_w", rows(a["ffn_conv_w_2"], "l w (j p) -> (l w j) p", p=P)),
                ("fconv_b", rows(a["ffn_conv_b_2"], "l (j p) -> (l j) p", p=P))]
        row0, n = {}, 0
        for name, src in vecs:
            row0[name] = n
            n += src.shape[0]
        assert n <= 6 * P
        row0["log_dt"] = 6 * P

        def col(name, i=0):
            return par[:, row0[name] + i:row0[name] + i + 1]

        def cols(name, n, i=0):
            return par[:, row0[name] + i:row0[name] + i + n]

        omm, hw0, ha0, omka = (lambda i: drv[:, i:i + 1]), (lambda i: drv[:, 11 + i:12 + i]), \
            (lambda i: drv[:, 14 + i:15 + i]), (lambda i: drv[:, 17 + i:18 + i])
        eps_col, halfpi = drv[:, 20:21], drv[:, 21:22]

        def mc(layer, which, i):
            j = 48 * layer + 8 * which + i
            return mod[:, j:j + 1]

        def kmaj(w, c0, c1, k0=0, k1=KT):
            return w.rearrange("(k p) n -> p k n", p=P)[:, k0:k1, c0:c1]

        chunk_src = {}
        w_in, w_out = a["w_in"][0], a["w_out"][0]
        for i in range(3):
            chunk_src["in", i] = [kmaj(w_in, 512 * i, 512 * i + 512)]
        chunk_src["in", 3] = [kmaj(w_in, 1536, KC_COL), kmaj(w_in, VS_COL, KW_COL), kmaj(w_in, VW_COL, GATE_COL)]
        chunk_src["in", 4] = [kmaj(w_in, c, c + HD) for g in range(4) for c in [KC_COL + HD * g] * 2]
        chunk_src["in", 5] = [kmaj(w_in, c, c + HD) for k0 in (KS_COL, KW_COL) for g in range(2)
                              for c in [k0 + HD * g] * 2]
        chunk_src["in", 6] = [kmaj(w_in, GATE_COL, N_IN)]
        for i in range(24):
            chunk_src["ada", i] = [kmaj(a["ada_w_2"][i // 12], 512 * (i % 12), 512 * (i % 12) + 512)]
        for i in range(4):
            chunk_src["ada", 24 + i] = [kmaj(a["kv_ada_w_2"], 512 * i, 512 * i + 512)]
        chunk_src["cmp", 0] = [a["cmp_w1_k"][0].rearrange("(k p) n -> p k n", p=P),
                               a["cmp_w1_v"][0].rearrange("(k p) n -> p k n", p=P)]
        for nm, w, n in (("out", w_out, 2), ("pin", a["pool_w_in_2"][0], 2), ("pout", a["pool_w_out_2"][0], 2),
                         ("pleg", a["w_ple_gate"][0], 2), ("kv", a["w_kv_2"], 12), ("dq", a["attn_w_q_2"][0], 6),
                         ("do", a["attn_w_o_2"][0], 2)):
            for i in range(n):
                chunk_src[nm, i] = [kmaj(w, 512 * i, 512 * i + 512)]
        chunk_src["ple", 0] = [a["w_ple"][0].rearrange("(k p) n -> p k n", p=P)]
        chunk_src["pgrp", 0] = [a["pool_w_grp_2"][0].rearrange("g (k p) n -> p (g k) n", p=P)]
        ffn_up = [a["w_up"][0], a["ffn_w_up_2"][0], a["ffn_w_up_2"][1]]
        ffn_down = [a["w_down"][0], a["ffn_w_down_2"][0], a["ffn_w_down_2"][1]]
        for f in range(3):
            for i in range(11):
                chunk_src["up", f, i] = [kmaj(ffn_up[f], 256 * i, 256 * i + 256),
                                         kmaj(ffn_up[f], FF + 256 * i, FF + 256 * i + 256)]
            for m in range(2):
                for i in range(3):
                    chunk_src["down", f, m, i] = [kmaj(ffn_down[f], 512 * m, 512 * m + 512, 8 * i, min(8 * i + 8, FT))]
        chunk_no, chunk_last_job = {}, {}

        def chunk_view(key):
            if key in (("in", 4), ("in", 5)):
                whole = shaped(ring[:, chunk_no[key] % SLOTS, :], KT, 4, 2, HD)
                return [whole[:, :, i // 2, i % 2, :] for i in range(8)]
            slot, off, views = chunk_no[key] % SLOTS, 0, []
            for src in chunk_src[key]:
                k, n = src.shape[1], src.shape[2]
                views.append(shaped(ring[:, slot, off:off + k * n], k, n))
                off += k * n
            return views

        job_no = {}
        psum_ready = sem("psum_ready")
        bank_free = [sem(f"bank_free{b}") for b in range(BANKS)]

        def bank_of(job):
            return banks[:, job_no[job] % BANKS, :]

        def freed(job):
            return bank_free[job_no[job] % BANKS], job_no[job] // BANKS + 1

        pieces = []
        for name, src in vecs:
            r, n, k = row0[name], src.shape[0], 0
            while k < n:
                m = min(n - k, P - (r + k) % P)
                pieces.append((r + k, m, src[k:k + m, :]))
                k += m
        stage_total = [16 * len(pieces) + 16]

        conv_base = [0, 2 * FT, 3 * FT]
        tn_round = [0, 1, 2, 2, 3]

        landed = [sem(f"slot_landed{s}") for s in range(SLOTS)]
        setup_in, stage_in, small_in = sem("setup_in"), sem("stage_in"), sem("small_in")

        block = ctx.enter_context(nc.Block())


        INV = [("L2", 0, 1, None, 4), ("N2", 1, 0, None, 5), ("L4", 5, 4, None, 6), ("Y1", 4, 7, 7, 8),
               ("T8", 6, 8, 8, 0), ("T8t", 0, None, None, 1), ("Ya", 2, 0, None, 4), ("T16", 1, 4, 0, 5),
               ("T16t", 5, None, None, 6), ("Yb", 3, 5, None, 7), ("T32", 6, 7, 5, 9)]

        def tmat(i):
            return KEEP[3] if i == 9 else TM[i]

        @block.tensor
        def _(pe):
            landed_count = [0] * SLOTS
            chunk_wait = {}
            current = [None]

            def opened(job):
                n = job_no[job] = len(job_no)
                if n >= BANKS:
                    pe.wait_ge(bank_free[n % BANKS], n // BANKS)
                current[0] = job
                return banks[:, n % BANKS, :]

            def chunk(key):
                if key not in chunk_no:
                    slot = len(chunk_no) % SLOTS
                    chunk_no[key] = len(chunk_no)
                    landed_count[slot] += 16 * len(chunk_src[key])
                    chunk_wait[key] = landed_count[slot]
                    pe.wait_ge(landed[slot], chunk_wait[key])
                chunk_last_job[key] = job_no[current[0]]
                return chunk_view(key)

            def copied(job):
                pe.wait_ge(*freed(job))

            def mm(o, l, r, start=True, stop=True, **k):
                return nc.tensor.matmul(o, l, r, start=start, stop=stop, **k)

            def close(ins):
                ins.then_inc(psum_ready, 1)

            def turn(job, pieces):
                b, off = opened(job), 0
                for src in pieces:
                    n, m = src.shape[0], src.shape[1]
                    last = nc.tensor.transpose(b[0:m, off:off + n], src, ident[0:n, 0:n])
                    off += n
                close(last)

            def tile(job, key, c0, rhs, part=0, kts=KT, m=P, first=None, n=T):
                b = opened(job)
                w = chunk(key)[part]
                for k in range(kts):
                    if first:
                        first(k)
                    l = w[:, k, c0:c0 + m]
                    last = mm(b[0:m, 0:n], l, rhs[:, k, :], start=(k == 0), stop=(k == kts - 1))
                close(last)

            def mean_square(i, sq):
                b = opened(("ms", i))
                for k in range(KT):
                    if k % 4 == 0:
                        pe.wait_ge(sem("squares"), 2 * i + k // 4 + 1)
                    last = mm(b[:, 0:T], ones_mean[:, :], sq[:, k, :], start=(k == 0), stop=(k == KT - 1))
                close(last)

            ada_left = list(range(28))

            ada_open = []

            def ada_columns():
                if ada_open:
                    i = ada_open.pop()
                    copied(("ada", i))
                    b = opened(("adc", i))
                    for m in range(4):
                        last = mm(b[:, m:m + 1], sums[:, i % 2, m * P:m * P + P], one_each[:, :])
                    close(last)

            def ada(n=1):
                for _ in range(n):
                    if ada_left:
                        i = ada_left.pop(0)
                        if i == 0:
                            pe.wait_ge(sem("cond_ready"), 1)
                        b = opened(("ada", i))
                        w = chunk(("ada", i))[0]
                        for k in range(KT):
                            q = 32 * (k % 4)
                            last = mm(b[q:q + 32, :], cond_wide[:, k, :], w[:, k, :], start=(k < 4), stop=(k >= 4),
                                      tile_position=(0, q))
                        close(last)
                        ada_columns()
                        ada_open.append(i)

            pe.wait_ge(sem("ident_ready"), 2)
            pe.wait_ge(setup_in, 32)
            for j in range(4):
                turn(("xT", j), [xtok[:, s, (2 * j + k) * P:(2 * j + k + 1) * P] for k in range(2) for s in range(2)])
            pe.wait_ge(sem("stage_clear"), 1)
            pe.wait_ge(stage_in, stage_total[0])
            pe.wait_ge(sem("dt_spread"), 1)
            for j in range(2):
                turn(("par", j), [stage[:, 3 * j + i, :] for i in range(3)] + [dt_wide[0:8, :]] * j)
            turn(("pT",), [ptok[:, s, k * P:k * P + P] for k in range(2) for s in range(2)])
            pe.wait_ge(sem("consts"), 1)
            mean_square(0, hn)

            def hn_wait(n):
                return lambda k: pe.wait_ge(sem("hn_ready"), 8 * n + k + 1)

            w0 = hn_wait(0)
            for i in range(8):
                tile(("rw", i), ("in", i // 4), 128 * (i % 4), hn, first=w0 if i == 0 else None)
            for i in range(8, 11):
                tile(("rw", i), ("in", 2), 128 * (i % 4), hn)
            tile(("q", 0), ("in", 2), 384, hn)
            for i in (1, 2):
                tile(("q", i), ("in", 3), 128 * (i - 1), hn)
            for s in range(2):
                b = opened(("vtok", s))
                w = chunk(("in", 3))
                for x in range(2):
                    for k in range(KT):
                        last = mm(b[:, x * P:x * P + P], hn[:, k, s * P:s * P + P], w[1 + x][:, k, :],
                                  start=(k == 0), stop=(k == KT - 1))
                close(last)
            for nm, key in (("kc", ("in", 4)), ("kd", ("in", 5))):
                for i in range(4):
                    b = opened((nm, i))
                    chunk(key)
                    w = shaped(ring[:, chunk_no[key] % SLOTS, :], KT, 4, P)
                    for k in range(KT):
                        last = mm(b[:, 0:T], w[:, k, i, :], hn[:, k, :], start=(k == 0), stop=(k == KT - 1))
                    close(last)
            b = opened(("gtok",))
            w = chunk(("in", 6))[0]
            for s in range(2):
                for k in range(KT):
                    last = mm(b[:, s * 18:s * 18 + 18], hn[:, k, s * P:s * P + P], w[:, k, 0:18],
                              start=(k == 0), stop=(k == KT - 1))
            close(last)
            for i in range(2):
                tile(("u", i), ("in", 6), 18 + 128 * i, hn)

            pe.wait_ge(sem("b_ready"), 1)
            turn(("bT",), [bdup[:, r, 4 * f:4 * f + 4, :, :].rearrange("p a b c -> p (a b c)")
                           for r in range(2) for f in range(2)])
            turn(("cT",), [cdup[:, r, f, :] for r in range(2) for f in range(2)])
            copied(("bT",))
            copied(("cT",))
            for i in range(2):
                copied(("u", i))

            def bu(j):
                b, q = opened(("bu", j)), 32 * (j % 4)
                for r in range(2):
                    last = mm(b[:, r * T:r * T + T], BT[q:q + 32, r, j // 4, :], uT[q:q + 32, j // 4, :])
                close(last)

            def y5(j):
                b, q, r2 = opened(("y5", j)), 32 * (j % 4), j % 2
                pe.wait_ge(sem("s5_states"), j + 1)
                for r in range(2):
                    last = mm(b[q:q + 32, 0:T], CT[:, r, j // 4, q:q + 32], s5w[:, r2, 4, r, :],
                              start=(r == 0), stop=(r == 1))
                close(last)

            bu(0)
            for j in range(8):
                if j < 7:
                    bu(j + 1)
                ada()
                y5(j)
            b = opened(("cmph",))
            w1 = chunk(("cmp", 0))
            for i in range(4):
                copied(("kc", i))
            for v in range(2):
                for lp in range(16):
                    last = mm(b[:, 30 * v:30 * v + 30], w1[v][:, lp, :],
                              kcs[:, 2 * v:2 * v + 2, 2 * lp:2 * lp + 225:16], start=(lp == 0), stop=(lp == 15))
            for v in range(2):
                for lp in range(16):
                    last = mm(b[:, 60 + v:61 + v], w1[v][:, lp, :], col("pe_v" if v else "pe_k", lp),
                              start=(lp == 0), stop=(lp == 15))
            close(last)
            pe.wait_ge(sem("ygel_ready"), 2)
            for m in range(4):
                b = opened(("glu", m))
                for k in range(2):
                    last = mm(b[:, 0:T], wglu[:, k, m * P:m * P + P], ygel[:, k, :], start=(k == 0), stop=(k == 1))
                close(last)
            copied(("cmph",))
            b = opened(("kcT",))
            close(mm(b[:, 0:30], cw2[:, 0:2, :].rearrange("p a b -> p (a b)"), hid[:, 0:2, 0:NCMP]))
            b = opened(("vc",))
            for g in range(2):
                last = mm(b[0:96, g * HD:g * HD + HD], hidv[:, g, :, :].rearrange("p a b -> p (a b)"), cw2[:, 2, :])
            close(last)
            ada()
            copied(("kcT",))
            for i in range(3):
                copied(("q", i))
            for s in range(2):
                for x in range(2):
                    b = opened(("cs", s, x))
                    for i in range(3):
                        hh = x + 2 * i
                        last = mm(b[:, 32 * i:32 * i + NCMP], qT[64 * x:64 * x + 64, hh // 2, s * P:s * P + P],
                                  kcT[64 * x:64 * x + 64, hh // 3, :])
                    close(last)

            def nsa_scores(i):
                s, hh = i // 6, i % 6
                x, g, nk = hh % 2, hh // 3, P * (s + 1)
                b = opened(("ns", i))
                for br in range(2):
                    last = mm(b[:, T * br:T * br + nk], qT[64 * x:64 * x + 64, hh // 2, s * P:s * P + P],
                              kd[64 * x:64 * x + 64, 2 * br + g, 0:nk])
                close(last)

            def nsa_turn(i):
                s = i // 6
                pe.wait_ge(sem("nsa_probs"), i + 1)
                b = opened(("np", i))
                for br in range(2):
                    for kt in range(s + 1):
                        o = (2 * br + kt) * P
                        last = nc.tensor.transpose(b[:, o:o + P], nsc[:, i % 2, br, kt * P:kt * P + P], ident[:, :])
                close(last)

            def nsa_values(i):
                s, g = i // 6, (i % 6) // 3
                copied(("np", i))
                b = opened(("nv", i))
                for br in range(2):
                    for kt in range(s + 1):
                        last = mm(b[:, br * HD:br * HD + HD], npt[:, i % 2, 2 * br + kt, :],
                                  vtok[:, kt, br * P + g * HD:br * P + g * HD + HD], start=(kt == 0), stop=(kt == s))
                close(last)

            for i in range(4):
                copied(("kd", i))
            nsa_scores(0)
            for s in range(2):
                pe.wait_ge(sem("cmp_probs"), s + 1)
                turn(("ct", s), [csc[:, s, 3 * g:3 * g + 3, :].rearrange("p a b -> p (a b)") for g in range(2)])
                copied(("ct", s))
                copied(("vc",))
                b = opened(("cpv", s))
                for g in range(2):
                    last = mm(b[:, 192 * g:192 * g + 192], cpt[0:96, g, :],
                              vbd[0:96, g, :, :].rearrange("p a b -> p (a b)"))
                close(last)
            for i in range(12):
                if i < 11:
                    nsa_scores(i + 1)
                if i > 0:
                    nsa_values(i - 1)
                nsa_turn(i)
                ada()
            nsa_values(11)
            ada()
            pe.wait_ge(sem("otok_ready"), 1)
            for c in range(3):
                turn(("oT", c), [otok[:, s, c * P:c * P + P] for s in range(2)])

            pe.wait_ge(sem("lora_tanh"), 2)
            pe.wait_ge(sem("lora_in"), 1)
            for c in range(3):
                b = opened(("wp", c))
                close(mm(b[:, 0:T], lora_w[0:64, c * P:c * P + P], zs[0:64, 9, :]))
            for c in range(3):
                b = opened(("ap", c))
                close(mm(b[:, 0:T], lora_w[64:128, c * P:c * P + P], zs[64:128, 9, :]))
            for c in range(3):
                b = opened(("gp", c))
                close(mm(b[:, 0:T], g2_w[:, c * P:c * P + P], zs[:, 10, :]))
            pe.wait_ge(sem("kk_sq"), 1)
            for c in range(3):
                b = opened(("kks", c))
                close(mm(b[:, 0:T], head_ones[:, :], W[5][:, c, :]))
            ada()
            pe.wait_ge(sem("bonus_in"), 1)
            for c in range(3):
                b = opened(("bon", c))
                close(mm(b[:, 0:T], head_ones[:, :], W[5][:, c, :]))
            pe.wait_ge(sem("gram_in"), 1)
            for s in range(2):
                cut = slice(s * P, s * P + P)
                for x, src in enumerate((W[6], W[7], W[8], zs[:, 6:9, :])):
                    turn(("tk", s, x), [src[:, c, cut] for c in range(3)])
                for name, lw, rw in (("N", 7, 6), ("L", 6, 7), ("MT", 8, 6), ("Rb", 7, 9), ("Rk", 8, 9)):
                    for p in range(2):
                        b, q = opened((name, s, p)), slice(64 * p, 64 * p + 64)
                        for c in range(3):
                            last = mm(b[:, c * P:c * P + P], W[lw][q, c, cut], W[rw][q, c, cut])
                        close(last)
                for p in range(2):
                    copied(("N", s, p))
                    copied(("L", s, p))
                pe.wait_ge(sem("tri_ready"), s + 1)
                for k, (name, lw, rw, add, dst) in enumerate(INV):
                    for p in range(2):
                        if k:
                            copied((INV[k - 1][0], s, p))
                        b = opened((name, s, p))
                        for c in range(3):
                            o = b[:, c * P:c * P + P]
                            if rw is None:
                                last = nc.tensor.transpose(o, tmat(lw)[:, p, c, :], ident[:, :])
                            else:
                                last = mm(o, tmat(lw)[:, p, c, :], tmat(rw)[:, p, c, :], stop=add is None)
                                if add is not None:
                                    last = mm(o, ident[:, :], tmat(add)[:, p, c, :], start=False)
                        close(last)
                    if k % 4 == 3:
                        ada()
                for p in range(2):
                    copied(("MT", s, p))
                for x in range(4):
                    copied(("tk", s, x))
                b = opened(("mv", s))
                for c in range(3):
                    for p in range(2):
                        o = c * P + p * HD
                        last = mm(b[:, o:o + HD], KEEP[0][:, p, c, :], tok4[:, 3, c, p * HD:p * HD + HD])
                close(last)
                copied(("mv", s))
                for p in range(2):
                    copied(("T32", s, p))
                    b = opened(("au", s, p))
                    for c in range(3):
                        last = mm(b[:, c * P:c * P + P], KEEP[3][:, p, c, :], AM[:, c, :, p * HD:p * HD + HD])
                    close(last)
                for p in range(2):
                    copied(("au", s, p))
                for r in range(4):
                    q = slice(32 * r, 32 * r + 32)
                    if 4 * s + r < 7:
                        b = opened(("H", s, r))
                        for c in range(3):
                            o = b[:, c * P:c * P + P]
                            mm(o, tok4[q, 1, c, :], AU[q, c, 1, :], stop=False)
                            last = mm(o, tok4[q, 2, c, :], tok4[q, 3, c, :], start=False)
                        close(last)
                    if 0 < 4 * s + r < 7:
                        b = opened(("E", s, r))
                        for c in range(3):
                            last = mm(b[:, c * P:c * P + P], AU[q, c, 0, :], tok4[q, 1, c, :])
                        close(last)
                for p in range(2):
                    copied(("Rb", s, p))
                    copied(("Rk", s, p))
                b = opened(("rt", s))
                for p in range(2):
                    for c in range(3):
                        last = mm(b[64 * p:64 * p + 64, c * P:c * P + P], AU[:, c, 0, p * HD:p * HD + HD],
                                  KEEP[1][:, p, c, :])
                close(last)
                for r in range(4):
                    q = 4 * s + r
                    if 0 < q < 7:
                        copied(("E", s, r))
                        copied(("H", 0, 0) if q == 1 else ("st", q - 1))
                        b = opened(("st", q))
                        for c in range(3):
                            o = b[:, c * P:c * P + P]
                            mm(o, EB[:, r, c, :], ST[:, q - 1, c, :], stop=False)
                            last = mm(o, ident[:, :], ST[:, q - 1, c, :], start=False)
                        close(last)
                b = opened(("ol", s))
                for c in range(3):
                    for p in range(2):
                        last = mm(b[64 * p:64 * p + 64, c * P:c * P + P], AU[:, c, 1, p * HD:p * HD + HD],
                                  KEEP[1][:, p, c, :], start=(c == 0), stop=False, skip_group_check=True)
                for c in range(3):
                    for p in range(2):
                        last = mm(b[64 * p:64 * p + 64, c * P:c * P + P], tok4[:, 3, c, p * HD:p * HD + HD],
                                  KEEP[2][:, p, c, :], start=False, stop=False, skip_group_check=True)
                copied(("st", 3 if s == 0 else 6))
                copied(("rt", s))
                for q in range(max(1, 4 * s), 4 * s + 4):
                    for c in range(3):
                        o = c * P + 32 * (q % 4)
                        last = mm(b[:, o:o + 32], ST[:, q - 1, c, :], W[9][:, c, 32 * q:32 * q + 32],
                                  start=False, stop=(q == 4 * s + 3), skip_group_check=True)
                close(last)
            for s in range(2):
                copied(("ol", s))
            for c in range(3):
                b = opened(("gm", c))
                close(mm(b[:, 0:T], head_mean[:, :], zs[:, c, :]))
            for c in range(3):
                pe.wait_ge(sem("gn_sq"), c + 1)
                b = opened(("gv", c))
                close(mm(b[:, 0:T], head_mean[:, :], zs[:, 3 + c, :]))
            ada(28)
            ada_columns()

            for i in range(2):
                copied(("glu", i))
            for c in range(3):
                copied(("oT", c))
            pe.wait_ge(sem("mix_rw"), 3)
            for m in range(8):
                tile(("out", m), ("out", m // 4), 128 * (m % 4), hn)

            def ffn(f, hwait):
                for j in range(FT):
                    for part, nm in enumerate(("ug", "uu")):
                        tile((nm, f, j), ("up", f, j // 2), 128 * (j % 2), hn, part=part,
                             first=hwait if j == 0 and part == 0 else None)
                for m in range(2):
                    outs = [opened(("down", f, 4 * m + i)) for i in range(4)]
                    for c in range(3):
                        w = chunk(("down", f, m, c))[0]
                        n = w.shape[1]
                        for i in range(4):
                            for k in range(n):
                                if m == 0 and i == 0:
                                    t = 8 * c + k
                                    pe.wait_ge(*((sem("act_ready"), t + 1) if f == 0 else freed(("uu", f, t))))
                                last = mm(outs[i][:, 0:T], w[:, k, i * P:i * P + P], act[:, 8 * c + k, :],
                                          start=(c == 0 and k == 0), stop=(c == 2 and k == n - 1))
                            if c == 2:
                                close(last)

            mean_square(1, sqb)
            mean_square(2, hn)
            ffn(0, hn_wait(1))
            mean_square(3, sqb)
            for m in range(8):
                tile(("pl", m), ("ple", 0), 128 * m, pT, kts=2)
            mean_square(4, sqb)
            for m in range(8):
                tile(("pg", m), ("pleg", m // 4), 128 * (m % 4), h,
                     first=(lambda k: pe.wait_ge(sem("h_ready"), 8 + k + 1)) if m == 0 else None)

            def hm_wait(n):
                return lambda k: pe.wait_ge(sem("hm_ready"), 8 * n + k + 1)

            mean_square(5, hn)
            for m in range(8):
                tile(("pi", m), ("pin", m // 4), 128 * (m % 4), hn, first=hm_wait(0) if m == 0 else None)
            for m in range(8):
                b = opened(("pp", m))
                w = chunk(("pgrp", 0))[0]
                for k in range(2):
                    t = 2 * (m // 2) + k
                    pe.wait_ge(sem("pooled"), t + 1)
                    last = mm(b[:, 0:T], w[:, t, (m % 2) * P:(m % 2) * P + P], pu[:, t, :], start=(k == 0), stop=(k == 1))
                close(last)
            for m in range(8):
                tile(("po", m), ("pout", m // 4), 128 * (m % 4), eT,
                     first=(lambda k: copied(("pp", k))) if m == 0 else None)
            mean_square(6, hn)
            ffn(1, hm_wait(1))

            mean_square(7, hn)
            for m in range(24):
                tile(("dk", m), ("kv", m // 4), 128 * (m % 4), hn, first=hm_wait(2) if m == 0 else None)
            for i in range(6):
                for s in range(2):
                    b = opened(("dv", i, s))
                    w = chunk(("kv", 6 + i))[0]
                    for k in range(KT):
                        last = mm(b[:, :], hn[:, k, s * P:s * P + P], w[:, k, :], start=(k == 0), stop=(k == KT - 1))
                    close(last)
            for m in range(24):
                tile(("dq", m), ("dq", m // 4), 128 * (m % 4), hn2, first=hm_wait(3) if m == 0 else None)

            def dil_scores(i):
                hh, s = i // 2, i % 2
                nk, q = P * (s + 1), slice(64 * (hh % 2), 64 * (hh % 2) + 64)
                for job, brs in (("da", (0, 1)), ("db", (2,))):
                    b = opened((job, i))
                    for br in brs:
                        t = 8 * br + hh // 2
                        last = mm(b[:, T * (br % 2):T * (br % 2) + nk], dq[q, t, s * P:s * P + P], dk[q, t, 0:nk])
                    close(last)

            def dil_turn(i):
                s = i % 2
                pe.wait_ge(sem("dil_probs"), i + 1)
                n = 3 * (s + 1)
                src = dsc[:, i % 2, 0:n * P]
                turn(("dp", i, 0), [src[:, k * P:k * P + P] for k in range(3)])
                if s:
                    turn(("dp", i, 1), [src[:, k * P:k * P + P] for k in range(3, 6)])

            def dil_values(i):
                hh, s = i // 2, i % 2
                for x in range(s + 1):
                    copied(("dp", i, x))
                b = opened(("dy", i))
                n = 3 * (s + 1)
                for k in range(n):
                    br, kt = k // (s + 1), k % (s + 1)
                    c = 1024 * br + HD * hh
                    last = mm(b[:, 0:HD], dpt[:, i % 2, k, :], dv[:, kt, c:c + HD], start=(k == 0), stop=(k == n - 1))
                close(last)

            for m in range(24):
                copied(("dq", m))
            dil_scores(0)
            for i in range(32):
                if i < 31:
                    dil_scores(i + 1)
                if i > 0:
                    dil_values(i - 1)
                dil_turn(i)
            dil_values(31)
            copied(("dy", 30))
            copied(("dy", 31))
            for j in range(4):
                turn(("dt", j), [dotok[:, s, (2 * j + k) * P:(2 * j + k + 1) * P] for k in range(2) for s in range(2)])
            for m in range(8):
                tile(("dw", m), ("do", m // 4), 128 * (m % 4), hn,
                     first=(lambda k: copied(("dt", k // 2))) if m == 0 else None)
            mean_square(8, hn2)
            ffn(2, hm_wait(4))
            mean_square(9, hn2)
            for s in range(2):
                for f in range(2):
                    for k in range(4):
                        if s == 0:
                            pe.wait_ge(sem("hn_ready"), 16 + 4 * f + k + 1)
                    turn(("fin", 2 * s + f), [hn[:, 4 * f + k, s * P:s * P + P] for k in range(4)])

        def taker(eng):
            def take(job):
                eng.wait_ge(psum_ready, job_no[job] + 1)
                return bank_of(job)
            return take

        SMALL = 16 * 13

        @block.sync
        def _(sp):
            sp.dma_start(xtok, a["x"][0].rearrange("(s p) d -> p s d", p=P)).then_inc(setup_in, 16)
            sp.dma_start(ptok, a["p"][0, 0].rearrange("(s p) d -> p s d", p=P)).then_inc(setup_in, 16)
            order = sorted(chunk_no, key=chunk_no.get)
            for n, key in enumerate(order):
                if n >= SLOTS:
                    sp.wait_ge(psum_ready, chunk_last_job[order[n - SLOTS]] + 1)
                for dst, src in zip(chunk_view(key), chunk_src[key]):
                    sp.dma_start(dst, src).then_inc(landed[n % SLOTS], 16)
            for s in range(2):
                for f in range(2):
                    sp.wait_ge(*freed(("fin", 2 * s + f)))
                    sp.dma_start(out[0, s * P:s * P + P, 512 * f:512 * f + 512],
                                 outt[:, s, 512 * f:512 * f + 512]).then_inc(sem("out_done"), 16)
            sp.wait_ge(sem("out_done"), 64)

        @block.gpsimd
        def _(pool):
            led = Ledger(pool, sem("pool_own"))
            g = nc.gpsimd

            def keep_if(o, op, base, cm, pattern, fill=0.0, signal=None):
                led.settle()
                led.emit(g.affine_select(out=o, in_=o, compare_op=op, fill=fill, base=base, pattern=pattern,
                                         channel_multiplier=cm), signal)

            def on_blocks(o, size, nb, width):
                v = o if width == 1 else o.rearrange("p (b c) -> p b c", b=nb)
                pat = [[-size, nb]] + ([[0, width]] if width > 1 else [])
                neg = [[size, nb]] + ([[0, width]] if width > 1 else [])
                keep_if(v, ALU.is_ge, 0, 1, pat)
                keep_if(v, ALU.is_ge, size - 1, -1, neg)

            led.emit(g.memset(ident[:, :], 0.0), sem("ident_ready"))
            keep_if(ident[:, :], ALU.not_equal, 0, 1, [[-1, P]], 1.0, sem("ident_ready"))
            led.emit(g.memset(ones_mean[:, :], 1.0 / D))
            led.emit(g.memset(head_ones[:, :], 1.0))
            led.emit(g.memset(head_mean[:, :], 1.0 / HD))
            led.emit(g.memset(masks[:, :, :], 1.0))
            led.emit(g.memset(scan_keep[:, :], 1.0))
            led.emit(g.memset(block3[:, :], 1.0))
            led.emit(g.memset(block2[:, :], 1.0))
            led.emit(g.memset(row_ok[:, :], 1.0))
            on_blocks(head_ones[:, :], HD, 2, HD)
            on_blocks(head_mean[:, :], HD, 2, HD)
            on_blocks(block3[:, :], 32, 3, 1)
            on_blocks(block2[:, :], HD, 2, 1)
            for m, size in ((U8, 8), (L8M, 8), (L16M, 16), (L32M, 32), (U32S, 32), (U32I, 32)):
                on_blocks(m, size, P // size, size)
            for m, up, strict in ((U8, 1, 1), (L8M, 0, 1), (L16M, 0, 1), (L32M, 0, 1), (U32S, 1, 1), (U32I, 1, 0)):
                keep_if(m, ALU.is_ge, -strict, -1 if up else 1, [[1 if up else -1, P]])
            led.settle()
            led.emit(g.tensor_tensor(L32M, L32M, L16M, ALU.subtract))
            led.settle()
            led.emit(g.tensor_tensor(L16M, L16M, L8M, ALU.subtract))
            keep_if(row_ok[:, :], ALU.is_ge, -31, 1, [[P, 2]])
            led.emit(g.memset(shaped(scan_keep[:, :], 8, 32)[:, :, 0], 0.0))
            led.emit(g.iota(dist[:, :, :], pattern=[[P, 2], [-1, T]], base=0, channel_multiplier=1,
                            allow_small_or_imprecise_dtypes=True))
            led.emit(g.iota(cdist[:, :, :], pattern=[[P, 2], [-16, NCMP]], base=-31, channel_multiplier=1,
                            allow_small_or_imprecise_dtypes=True))
            keep_if(dist[:, :, :], ALU.is_ge, 0, 1, [[P, 2], [-1, T]], FAR)
            keep_if(cdist[:, :, :], ALU.is_ge, -31, 1, [[P, 2], [-16, NCMP]], FAR)
            led.emit(g.memset(one_each[:, :], 0.0))
            for q in (0, 32, 64, 96):
                keep_if(one_each[:, :], ALU.not_equal, -q, 1, [[0, 1]], 1.0)
            led.settle()
            for hh, sl in enumerate(nsa_slopes(6)):
                led.emit(g.tensor_scalar(cbias[:, :, hh, :], cdist[:, :, :], -sl, None, ALU.mult))
            led.settle()
            led.emit(g.memset(hid[:, :, :], 0.0))
            led.emit(g.memset(csc[:, :, :, :], 0.0), sem("consts"))
            led.emit(g.memset(tabC[:, :, 0:1], 1.0))
            led.emit(g.memset(tabS[:, :, 0:1], 0.0))

            pool.wait_ge(sem("theta_ready"), 2)
            led.emit(g.tensor_copy(powr[:, 0, :], s5v[:, 8, :]))
            led.emit(g.tensor_copy(powr[:, 1, :], s5v[:, 7, :]))
            n = 1
            while n < T:
                led.settle()
                pc, ps = (powr[:, x, :].unsqueeze(2).broadcast_to([P, 8, n]) for x in range(2))
                lo, hi = slice(0, n), slice(n, 2 * n)
                for tab, (x, y), op in ((tabC, (tabC, tabS), ALU.subtract), (tabS, (tabS, tabC), ALU.add)):
                    led.settle()
                    led.emit(g.tensor_tensor(ptmp[:, 0, :, lo], x[:, :, lo], pc, ALU.mult))
                    led.emit(g.tensor_tensor(ptmp[:, 1, :, lo], y[:, :, lo], ps, ALU.mult))
                    led.settle()
                    led.emit(g.tensor_tensor(tab[:, :, hi], ptmp[:, 0, :, lo], ptmp[:, 1, :, lo], op))
                n *= 2
                if n < T:
                    led.settle()
                    led.emit(g.tensor_tensor(s5v[:, 18, :], powr[:, 0, :], powr[:, 0, :], ALU.mult))
                    led.emit(g.tensor_tensor(s5v[:, 19, :], powr[:, 1, :], powr[:, 1, :], ALU.mult))
                    led.emit(g.tensor_tensor(s5v[:, 20, :], powr[:, 0, :], powr[:, 1, :], ALU.mult))
                    led.settle()
                    led.emit(g.tensor_tensor(powr[:, 0, :], s5v[:, 18, :], s5v[:, 19, :], ALU.subtract))
                    led.emit(g.tensor_scalar(powr[:, 1, :], s5v[:, 20, :], 2.0, None, ALU.mult))
            led.settle()
            led.emit(g.memset(hidv[:, :, :, :], 0.0), sem("tables"))

            def turned_in(j):
                w = s5w[:, j % 2]
                pool.wait_ge(*freed(("bu", j)))
                led.emit(g.tensor_tensor(w[:, 2, 0, :], w[:, 0, 0, :], w[:, 1, 1, :], ALU.add))
                led.emit(g.tensor_tensor(w[:, 2, 1, :], w[:, 0, 1, :], w[:, 1, 0, :], ALU.subtract), sem("s5_in"))

            turned_in(0)
            for j in range(8):
                if j < 7:
                    turned_in(j + 1)
                w = s5w[:, j % 2]
                pool.wait_ge(sem("s5_out"), j + 1)
                if j >= 2:
                    pool.wait_ge(psum_ready, job_no["y5", j - 2] + 1)
                led.emit(g.tensor_tensor(w[:, 4, 0, :], w[:, 0, 0, :], w[:, 1, 1, :], ALU.subtract))
                led.emit(g.tensor_tensor(w[:, 4, 1, :], w[:, 0, 1, :], w[:, 1, 0, :], ALU.add), sem("s5_states"))

            pool.wait_ge(sem("gains"), 5)
            led.emit(g.iota(dint.bitcast(mybir.dt.int32), pattern=[[P, 2], [-1, T]], base=0, channel_multiplier=1))
            led.emit(g.iota(inv_count[:, :, :], pattern=[[0, 4], [1, T]], base=1, channel_multiplier=0,
                            allow_small_or_imprecise_dtypes=True))
            led.emit(g.tensor_copy(bdist[:, 0, :, :], dist[:, :, :]))
            keep_if(bdist[:, 0, :, :], ALU.is_ge, P, -1, [[-P, 2], [1, T]], FAR)
            for w in range(4):
                led.emit(g.tensor_scalar(inv_count[:, w, :], inv_count[:, w, :], float(2 ** (w + 1)), None, ALU.min),
                         sem("late_consts") if w == 3 else None)

        @block.vector
        def _(dve):
            led = Ledger(dve, sem("dve_own"))
            v = nc.vector
            take0 = taker(dve)
            ada_jobs = sorted((n, job) for job, n in job_no.items() if job[0] == "adc")

            def modulation_before(job):
                while ada_jobs and ada_jobs[0][0] < job_no[job]:
                    aj = ada_jobs.pop(0)[1]
                    b, i = take0(aj), aj[1]
                    led.emit(v.tensor_tensor(mod[:, 4 * i:4 * i + 4], b[:, 0:4], cols("ada_b", 4, 4 * i), ALU.add),
                             *freed(aj))

            def take(job):
                modulation_before(job)
                return take0(job)

            def placed(job):
                modulation_before(job)
                dve.wait_ge(*freed(job))

            def tt(o, x, y, op, signal=None, value=None):
                led.emit(v.tensor_tensor(o, x, y, op), signal, value)

            def ts(o, x, s1, op0, s2=None, op1=ALU.bypass, signal=None, value=None):
                led.emit(v.tensor_scalar(o, x, s1, s2, op0, op1) if s2 is not None else
                         v.tensor_scalar(o, x, s1, None, op0), signal, value)

            def stt(o, x, s, y, op0, op1, signal=None, value=None):
                led.emit(v.scalar_tensor_tensor(out=o, in0=x, scalar=s, in1=y, op0=op0, op1=op1), signal, value)

            def copy(o, x, signal=None, value=None):
                led.emit(v.tensor_copy(o, x), signal, value)

            def rec(o, x, signal=None):
                led.emit(v.reciprocal(o, x), signal)

            settle = led.settle
            MUL, ADD, SUB = ALU.mult, ALU.add, ALU.subtract

            led.emit(v.memset(stage[:, :, :], 0.0), sem("stage_clear"))
            for j in range(4):
                b = take(("xT", j))
                copy(h[:, 2 * j:2 * j + 2, :], shaped(b, 2, T), *freed(("xT", j)))
            dve.wait_ge(stage_in, stage_total[0])
            copy(shaped(dt_wide[0:8, :], 2, HD), dt_rows[0:8, :].unsqueeze(2).broadcast_to([8, 2, HD]), sem("dt_spread"))
            for j in range(2):
                b, n = take(("par", j)), 384 + 8 * j
                copy(par[:, 384 * j:384 * j + n], b[:, 0:n], *freed(("par", j)))
            b = take(("pT",))
            copy(pT[:, :, :], shaped(b, 2, T), *freed(("pT",)))
            settle()
            ts(drv[:, 0:11], cols("mu", 11), -1.0, MUL, 1.0, ADD)
            ts(drv[:, 11:14], cols("w0", 3), 0.5, MUL)
            ts(drv[:, 14:17], cols("a0", 3), 0.5, MUL)
            ts(drv[:, 17:20], cols("k_a", 3), -1.0, MUL, 1.0, ADD, signal=sem("derived"))
            dve.wait_ge(sem("cond_tanh"), 1)
            stt(cond[:, :], cond[:, :], 1.0, cols("c", 8), ADD, MUL)
            settle()
            ts(cond_wide[:, :, :], cond[:, :].unsqueeze(2).broadcast_to([P, KT, 32]), 0.5, MUL, signal=sem("cond_ready"))

            def norm_scale(i, eps=EPS):
                b = take(("ms", i))
                ts(rs[:, 0, :], b[:, 0:T], eps, ADD, signal=freed(("ms", i))[0], value=freed(("ms", i))[1])
                settle()
                rec(rs[:, 1, :], rs[:, 0, :], sem("rs_rec"))
                dve.wait_ge(sem("rs_root"), i + 1)

            dve.wait_ge(sem("consts"), 1)

            norm_scale(0)
            for k in range(KT):
                stt(hn[:, k, :], h[:, k, :], col("pre_mix", k), rs[:, 2, :], MUL, MUL, sem("hn_ready"))

            def z(i):
                return s5v[:, i, :]
            lre, lim = cols("lam_re", 8), cols("lam_im", 8)
            dve.wait_ge(sem("s5_dt"), 1)
            tt(z(1), lre, z(0), MUL)
            tt(z(3), lim, z(0), MUL, sem("s5_lr"))
            settle()
            ts(z(4), z(3), 1.0 / (2 * math.pi), MUL, MAGIC, ADD)
            settle()
            ts(z(4), z(4), MAGIC, SUB)
            settle()
            stt(z(5), z(4), -6.28125, z(3), MUL, ADD)
            settle()
            stt(z(5), z(4), -(2 * math.pi - 6.28125), z(5), MUL, ADD)
            settle()
            ts(z(5), z(5), 3.1415925, ALU.min, -3.1415925, ALU.max)
            settle()
            ts(z(6), z(5), math.pi / 2, ALU.is_gt, -2 * math.pi, MUL)
            settle()
            stt(z(6), z(5), math.pi / 2, z(6), ADD, ADD)
            settle()
            ts(z(6), z(6), 3.1415925, ALU.min, -3.1415925, ALU.max, signal=sem("s5_angle"))
            tt(z(11), lre, lre, MUL)
            tt(z(12), lim, lim, MUL)
            settle()
            tt(z(11), z(11), z(12), ADD)
            settle()
            rec(z(12), z(11))
            dve.wait_ge(sem("theta_ready"), 2)
            tt(z(9), z(2), z(8), MUL)
            tt(z(10), z(2), z(7), MUL)
            settle()
            ts(z(15), z(9), 1.0, SUB)
            settle()
            tt(z(13), z(15), lre, MUL)
            tt(z(16), z(10), lim, MUL)
            tt(z(14), z(10), lre, MUL)
            tt(z(17), z(15), lim, MUL)
            settle()
            tt(z(13), z(13), z(16), ADD)
            tt(z(14), z(14), z(17), SUB)
            settle()
            tt(z(13), z(13), z(12), MUL)
            tt(z(14), z(14), z(12), MUL)
            settle()
            dve.wait_ge(small_in, SMALL)
            fre, fim = (z(i).unsqueeze(2).broadcast_to([P, 8, 16]) for i in (13, 14))
            for ri, (x, y, op) in enumerate(((0, 1, SUB), (1, 0, ADD))):
                tt(bmul[:, ri], bfull[:, x], fre, MUL)
                tt(bdup[:, ri, :, 0, :], bfull[:, y], fim, MUL)
                settle()
                tt(bmul[:, ri], bmul[:, ri], bdup[:, ri, :, 0, :], op)
                settle()
                for bb in range(2):
                    ts(bdup[:, ri, :, bb, :], bmul[:, ri], block2[:, bb:bb + 1], MUL,
                       signal=sem("b_ready") if ri and bb else None)

            for i in range(RW_TILES):
                b = take(("rw", i))
                dve.wait_ge(sem("shift_own"), i + 1)
                stt(zs[:, i, 1:T], b[:, 0:T - 1], col("mu", i), zs[:, i, 1:T], MUL, ADD, *freed(("rw", i)))
            placed(("gtok",))
            ts(gate[:, :, :], gate[:, :, :], 0.5, MUL, 0.5, ADD)

            b = take(("bT",))
            copy(BT[:, :, :, :].rearrange("p a b c -> p (a b c)"), b, *freed(("bT",)))
            b = take(("cT",))
            pb = shaped(b, 2, 2, 4, 2, 16)
            for ri in range(2):
                for bb in range(2):
                    last = ri == 1 and bb == 1
                    o = CT[:, ri].rearrange("p f (a b c) -> p f a b c", a=4, b=2)[:, :, :, bb, :]
                    ts(o, pb[:, ri, :, :, bb, :], block2[:, bb:bb + 1], MUL, -1.0 if ri else 1.0, MUL,
                       signal=freed(("cT",))[0] if last else None, value=freed(("cT",))[1] if last else None)
            dve.wait_ge(sem("tables"), 1)

            def s5_in(j):
                b = shaped(take(("bu", j)), 2, T)
                w = s5w[:, j % 2]
                if j >= 2:
                    dve.wait_ge(sem("s5_states"), j - 1)
                tt(w[:, 0], b, tabC[:, j, :].unsqueeze(1).broadcast_to([P, 2, T]), MUL)
                tt(w[:, 1], b, tabS[:, j, :].unsqueeze(1).broadcast_to([P, 2, T]), MUL, *freed(("bu", j)))

            def s5_scan(j):
                w = s5w[:, j % 2]
                dve.wait_ge(sem("s5_in"), j + 1)
                for x in range(2):
                    led.emit(v.tensor_tensor_scan(w[:, 3, x, :], z(2)[:, j:j + 1].broadcast_to([P, T]), w[:, 2, x, :],
                                                  0.0, MUL, ADD))
                settle()
                tt(w[:, 0], w[:, 3], tabC[:, j, :].unsqueeze(1).broadcast_to([P, 2, T]), MUL)
                tt(w[:, 1], w[:, 3], tabS[:, j, :].unsqueeze(1).broadcast_to([P, 2, T]), MUL, sem("s5_out"))

            def s5_y(j):
                b, q = take(("y5", j)), slice(32 * (j % 4), 32 * (j % 4) + 32)
                f = j // 4
                stt(ygel[q, f, :], uT[q, f, :], par[q, row0["s5_d"] + f:row0["s5_d"] + f + 1], b[q, 0:T], MUL, ADD,
                    *freed(("y5", j)))

            s5_in(0)
            for j in range(8):
                if j < 7:
                    s5_in(j + 1)
                s5_scan(j)
                if j:
                    s5_y(j - 1)
            s5_y(7)
            for m in range(2):
                placed(("glu", 2 + m))
                ts(s5g[:, m, :], s5g[:, m, :], 0.5, MUL, 0.5, ADD)
            settle()
            for m in range(2):
                b = take(("glu", m))
                tt(hn[:, 6 + m, :], b[:, 0:T], s5g[:, m, :], MUL, *freed(("glu", m)))

            b = take(("vc",))
            for x in range(3):
                ts(vbd[0:96, :, x, :], shaped(b[0:96, 0:P], 2, HD), block3[0:96, x:x + 1], MUL,
                   signal=freed(("vc",))[0] if x == 2 else None, value=freed(("vc",))[1] if x == 2 else None)
            for s in range(2):
                for x in range(2):
                    b = take(("cs", s, x))
                    tt(csc[:, s, x::2, 0:NCMP], shaped(b[:, 0:96], 3, 32)[:, :, 0:NCMP], cbias[:, s, x::2, :], ADD,
                       *freed(("cs", s, x)))
            settle()
            for s in range(2):
                led.emit(v.tensor_reduce(cst[:, s, 0, :], csc[:, s, :, 0:NCMP], AX.X, ALU.max))
            settle()
            for s in range(2):
                tt(csc[:, s, :, 0:NCMP], csc[:, s, :, 0:NCMP], cst[:, s, 0, :].unsqueeze(2).broadcast_to([P, 6, NCMP]),
                   SUB, sem("cmp_shifted"))
            for s in range(2):
                dve.wait_ge(sem("cmp_exp"), s + 1)
                led.emit(v.tensor_reduce(cst[:, s, 1, :], csc[:, s, :, 0:NCMP], AX.X, ADD))
            settle()
            for s in range(2):
                rec(cst[:, s, 2, :], cst[:, s, 1, :])
            settle()
            for s in range(2):
                stt(cst[:, s, 3, :], cst[:, s, 2, :], row_ok[:, s:s + 1], gate[:, s, 0::3], MUL, MUL)
            settle()
            for s in range(2):
                tt(csc[:, s, :, 0:NCMP], csc[:, s, :, 0:NCMP], cst[:, s, 3, :].unsqueeze(2).broadcast_to([P, 6, NCMP]),
                   MUL, sem("cmp_probs"))

            slopes6 = nsa_slopes(6)

            def nsa_bias(i):
                s, hh, u = i // 6, i % 6, i % 2
                nk = P * (s + 1)
                b = shaped(take(("ns", i)), 2, T)
                if i >= 2:
                    dve.wait_ge(psum_ready, job_no["np", i - 2] + 1)
                stt(nsc[:, u, :, 0:nk], dist[:, s, 0:nk].unsqueeze(1).broadcast_to([P, 2, nk]), -slopes6[hh],
                    b[:, :, 0:nk], MUL, ADD, *freed(("ns", i)))
                settle()
                led.emit(v.tensor_reduce(nst[:, i % 4, 0, :], nsc[:, u, :, 0:nk], AX.X, ALU.max, negate=True),
                         sem("nsa_max"))

            def nsa_out(i):
                s, hh, u = i // 6, i % 6, i % 2
                dve.wait_ge(sem("nsa_probs"), i + 1)
                rec(nst[:, i % 4, 2, :], nst[:, i % 4, 1, :])
                settle()
                tt(nst[:, i % 4, 3, :], nst[:, i % 4, 2, :], gate[:, s, 3 * hh + 1:3 * hh + 3], MUL)
                b = take(("nv", i))
                o = otok[:, s, HD * hh:HD * hh + HD]
                settle()
                stt(o, b[:, 0:HD], nst[:, i % 4, 3, 0:1], o, MUL, ADD)
                settle()
                stt(o, b[:, HD:2 * HD], nst[:, i % 4, 3, 1:2], o, MUL, ADD, *freed(("nv", i)))

            nsa_bias(0)
            for s in range(2):
                b = take(("ct", s))
                if s:
                    dve.wait_ge(psum_ready, job_no["cpv", 0] + 1)
                copy(cpt[0:96, :, :], shaped(b[0:96, 0:T], 2, P), *freed(("ct", s)))
                b = take(("cpv", s))
                copy(otok[:, s, :], b[:, 0:384], *freed(("cpv", s)))
            for i in range(12):
                if i < 11:
                    nsa_bias(i + 1)
                if i > 0:
                    nsa_out(i - 1)
            nsa_out(11)
            settle()
            led.emit(v.memset(nst[:, 0, 0, :], 0.0), sem("otok_ready"))

            rr, kk_, vv = zs[:, 0:3, :], zs[:, 3:6, :], zs[:, 6:9, :]
            dve.wait_ge(sem("lora_tanh"), 2)
            ts(zs[:, 10, :], zs[:, 10, :], 0.5, MUL, 0.5, ADD, signal=sem("lora_in"))
            for c in range(3):
                placed(("wp", c))
            ts(W[0], W[0], -0.5 * math.exp(-0.5), MUL, -0.5 * math.exp(-0.5), ADD)
            settle()
            for c in range(3):
                led.emit(v.tensor_tensor_scan(W[1][:, c, :], scan_keep[:, :], W[0][:, c, :], 0.0, MUL, ADD))
            settle()
            tt(W[0], W[1], W[0], SUB, sem("logs"))
            for c in range(3):
                ts(W[4][:, c, :], kk_[:, c, :], col("k_k", c), MUL)
            settle()
            tt(W[5], W[4], W[4], MUL, sem("kk_sq"))
            for c in range(3):
                placed(("ap", c))
            ts(W[3], W[3], 0.5, MUL, 0.5, ADD)
            settle()
            for c in range(3):
                ts(W[11][:, c, :], W[3][:, c, :], col("k_a", c), MUL, omka(c), ADD)
            settle()
            tt(kk_, kk_, W[11], MUL)
            for c in range(3):
                b = take(("kks", c))
                ts(W[5][:, c, :], b[:, 0:T], 1e-24, ALU.max, signal=freed(("kks", c))[0], value=freed(("kks", c))[1])
            settle()
            rec(W[5], W[5], sem("kk_rec"))
            dve.wait_ge(sem("exps"), 3)
            tt(W[8], kk_, W[2], MUL)
            tt(W[9], rr, W[1], MUL)
            copy(Pend[:, :, :], W[1][:, :, 31::32])
            dve.wait_ge(sem("kk_root"), 1)
            tt(W[4], W[4], W[5], MUL)
            settle()
            for c in range(3):
                stt(W[5][:, c, :], rr[:, c, :], col("r_k", c), kk_[:, c, :], MUL, MUL,
                    sem("bonus_in") if c == 2 else None)
            tt(W[7], W[4], W[3], MUL)
            stt(W[6].rearrange("p a b -> p (a b)"), W[4].rearrange("p a b -> p (a b)"), -1.0,
                W[0].rearrange("p a b -> p (a b)"), MUL, MUL)
            settle()
            tt(W[7], W[7], W[2], MUL, sem("gram_in"))
            for c in range(3):
                b = take(("bon", c))
                tt(W[11][:, c, :], b[:, 0:T], vv[:, c, :], MUL, *freed(("bon", c)))

            def over3(m):
                return m.unsqueeze(1).broadcast_to([P, 3, P])

            def three(b):
                return shaped(b[:, 0:384], 3, P)

            for s in range(2):
                cut = slice(s * P, s * P + P)
                for p in range(2):
                    b = take(("N", s, p))
                    tt(TM[0][:, p], three(b), over3(U8), MUL, *freed(("N", s, p)))
                for p in range(2):
                    b = take(("L", s, p))
                    tt(TM[1][:, p], three(b), over3(L8M), MUL)
                    tt(TM[2][:, p], three(b), over3(L16M), MUL)
                    tt(TM[3][:, p], three(b), over3(L32M), MUL, *freed(("L", s, p)))
                settle()
                for p in range(2):
                    tt(TM[7][:, p], TM[0][:, p], over3(ident[:, :]), ADD, sem("tri_ready") if p else None)
                for name, k, m in (("MT", 0, U32S), ("Rb", 1, U32I), ("Rk", 2, U32I)):
                    for p in range(2):
                        b = take((name, s, p))
                        tt(KEEP[k][:, p], three(b), over3(m), MUL, *freed((name, s, p)))
                for name, _l, _r, _a, to in INV:
                    b = take((name, s, 0))
                    copy(tmat(to)[:, 0], three(b), *freed((name, s, 0)))
                b = take(("mv", s))
                copy(AM[:, :, 1, :], three(b), *freed(("mv", s)))
                b = take(("au", s, 0))
                copy(AU[:, :, :, 0:HD], shaped(b[:, 0:384], 3, 2, HD), *freed(("au", s, 0)))
                for r in range(4):
                    q = 4 * s + r
                    if q < 7:
                        b = three(take(("H", s, r)))
                        for c in range(3):
                            o = ST[:, 0, c, :] if q == 0 else HB[:, r, c, :]
                            stt(o, b[:, c, :], Pend[:, c, q:q + 1], head_ones[:, :], MUL, MUL,
                                *(freed(("H", s, r)) if c == 2 else (None, None)))
                    if 0 < q < 7:
                        b = three(take(("E", s, r)))
                        tt(EB[:, r], b, over3(head_ones[:, :]), MUL, *freed(("E", s, r)))
                b = take(("rt", s))
                tt(W[9][:, :, cut], three(b), W[9][:, :, cut], ADD, *freed(("rt", s)))
                settle()
                for r in range(4):
                    q = 4 * s + r
                    if 0 < q < 7:
                        b = three(take(("st", q)))
                        for c in range(3):
                            stt(ST[:, q, c, :], b[:, c, :], Pend[:, c, q:q + 1], HB[:, r, c, :], MUL, ADD,
                                *(freed(("st", q)) if c == 2 else (None, None)))
            for s in range(2):
                placed(("ol", s))
            for c in range(3):
                b = take(("gm", c))
                tt(zs[:, c, :], zs[:, c, :], b[:, 0:T], SUB, *freed(("gm", c)))
            for c in range(3):
                b = take(("gv", c))
                ts(zs[:, 6 + c, :], b[:, 0:T], GN_EPS, ADD, signal=freed(("gv", c))[0], value=freed(("gv", c))[1])
            settle()
            rec(vv, vv, sem("gn_rec"))
            dve.wait_ge(sem("gn_root"), 1)
            tt(rr, rr, vv, MUL)
            settle()
            for c in range(3):
                ts(zs[:, c, :], zs[:, c, :], col("gn_w", c), MUL, col("gn_b", c), ADD)
            settle()
            tt(rr, rr, W[11], ADD)
            settle()
            for c in range(3):
                tt(hn[:, c, :], zs[:, c, :], W[10][:, c, :], MUL, sem("mix_rw"))

            def add_normed(i, gain, y):
                norm_scale(i)
                for k in range(KT):
                    stt(y[:, k, :], y[:, k, :], col(gain, k), rs[:, 2, :], MUL, MUL)
                settle()
                for k in range(KT):
                    tt(h[:, k, :], h[:, k, :], y[:, k, :], ADD, sem("h_ready"))

            def ffn(f):
                W0, B0, n = (row0["conv_w"], row0["conv_b"], 44) if f == 0 else \
                    (row0["fconv_w"] + 66 * (f - 1), row0["fconv_b"] + 22 * (f - 1), 22)

                def product(j):
                    u = j % 2
                    dve.wait_ge(sem("gate_act"), FT * f + j + 1)
                    if f == 0:
                        tt(act[:, j, :], ct[:, u, 0, :], ct[:, u, 1, :], MUL, sem("act_ready"))
                    else:
                        b = take(("uu", f, j))
                        tt(act[:, j, :], b[:, 0:T], ct[:, u, 0, :], MUL, *freed(("uu", f, j)))

                parts = ("ug", "uu") if f == 0 else ("ug",)
                for j in range(FT):
                    bs = []
                    for x, nm in enumerate(parts):
                        bs.append(take((nm, f, j)))
                        dve.wait_ge(sem("conv_own"), conv_base[f] + len(parts) * j + x + 1)
                        t = ct[:, j % 2, x, :]
                        w = W0 + n + 22 * x + j
                        stt(t[:, 1:T], bs[x][:, 0:T - 1], par[:, w:w + 1], t[:, 1:T], MUL, ADD)
                    settle()
                    for x, nm in enumerate(parts):
                        t = ct[:, j % 2, x, :]
                        w = W0 + 22 * x + j
                        stt(t[:, 2:T], bs[x][:, 0:T - 2], par[:, w:w + 1], t[:, 2:T], MUL, ADD, *freed((nm, f, j)))
                    if j:
                        product(j - 1)
                settle()
                product(FT - 1)
                if f:
                    for m in range(8):
                        b = take(("down", f, m))
                        stt(h[:, m, :], b[:, 0:T], mc(f - 1, 5, m), h[:, m, :], MUL, ADD, *freed(("down", f, m)))

            def scaled(i):
                norm_scale(i)
                for k in range(KT):
                    tt(tn[:, k, :], h[:, k, :], rs[:, 2, :], MUL, sem("tn_ready"))

            add_normed(1, "post_mix", yb)
            norm_scale(2)
            for k in range(KT):
                stt(hn[:, k, :], h[:, k, :], col("pre_ffn", k), rs[:, 2, :], MUL, MUL, sem("hn_ready"))
            for n, (l, sc, gn) in enumerate(((0, 1, cols("norm1", 8)), (0, 4, cols("norm2", 8)), (2, 1, cols("kv_norm", 8)),
                                             (1, 1, cols("norm1", 8, 8)), (1, 4, cols("norm2", 8, 8)))):
                c0 = 48 * l + 8 * sc
                stt(gsc[:, 8 * n:8 * n + 8], mod[:, c0:c0 + 8], 1.0, gn, ADD, MUL, sem("gains"))
            ffn(0)
            dve.wait_ge(sem("late_consts"), 1)
            rec(inv_count[:, :, :], inv_count[:, :, :])
            for br, low in ((1, 3), (2, 15)):
                m = bdist[:, br, :, :]
                led.emit(v.tensor_scalar(m.bitcast(mybir.dt.int32), dint.bitcast(mybir.dt.int32), low, None,
                                         ALU.bitwise_and))
            settle()
            for br in (1, 2):
                m = bdist[:, br, :, :]
                ts(m, m.bitcast(mybir.dt.int32), 1.0, ALU.min, FAR, MUL)
            settle()
            for br in (1, 2):
                tt(bdist[:, br, :, :], bdist[:, br, :, :], dist[:, :, :], ALU.max)
            add_normed(3, "post_ffn", yb)
            norm_scale(4)
            for k in range(KT):
                stt(eb[:, k, :], eb[:, k, :], col("ple_norm", k), rs[:, 2, :], MUL, MUL)
            settle()
            for m in range(8):
                placed(("pg", m))
                stt(yb[:, m, :], yb[:, m, :], 1.0, eb[:, m, :], ADD, MUL)
            settle()
            for m in range(8):
                stt(h[:, m, :], yb[:, m, :], 0.5, h[:, m, :], MUL, ADD, sem("h_ready"))

            scaled(5)
            for gq in range(4):
                for i in range(2):
                    placed(("pi", 2 * gq + i))
                src = pu[:, 2 * gq:2 * gq + 2, :]
                for l in range(gq + 1):
                    sh, o = 2 ** l, pw[:, l % 2]
                    copy(o[:, :, 0:sh], src[:, :, 0:sh])
                    tt(o[:, :, sh:T], src[:, :, sh:T], src[:, :, 0:T - sh], ADD)
                    settle()
                    src = o
                tt(src, src, inv_count[:, gq, :].unsqueeze(1).broadcast_to([P, 2, T]), MUL)
                settle()
                for i in range(2):
                    tt(pu[:, 2 * gq + i, :], src[:, i, :], pu[:, 2 * gq + i, :], SUB, sem("pooled"))
                settle()
            for m in range(8):
                b = take(("po", m))
                stt(h[:, m, :], b[:, 0:T], mc(0, 2, m), h[:, m, :], MUL, ADD, *freed(("po", m)))
            settle()
            scaled(6)
            ffn(1)
            settle()
            scaled(7)

            slopes48 = dilated_slopes(48)

            def dil_bias(i):
                hh, s, u = i // 2, i % 2, i % 2
                nk = P * (s + 1)
                if i >= 2:
                    dve.wait_ge(psum_ready, job_no["dp", i - 2, s] + 1)
                for job, brs in (("da", (0, 1)), ("db", (2,))):
                    b = take((job, i))
                    for br in brs:
                        last = br != 0
                        o = T * (br % 2)
                        stt(dsc[:, u, br * nk:br * nk + nk], bdist[:, br, s, 0:nk], -float(slopes48[16 * br + hh]),
                            b[:, o:o + nk], MUL, ADD, *(freed((job, i)) if last else (None, None)))
                settle()
                led.emit(v.tensor_reduce(dst[:, i % 4, 0:1], dsc[:, u, 0:3 * nk], AX.X, ALU.max, negate=True),
                         sem("dil_max"))

            def dil_out(i):
                hh, s, u = i // 2, i % 2, i % 2
                if s:
                    b = take(("dp", i, 1))
                    if i >= 2:
                        dve.wait_ge(psum_ready, job_no["dy", i - 2] + 1)
                    copy(dpt[:, u, 3:6, :], three(b), *freed(("dp", i, 1)))
                dve.wait_ge(sem("dil_probs"), i + 1)
                rec(dst[:, i % 4, 2:3], dst[:, i % 4, 1:2])
                settle()
                b = take(("dy", i))
                ts(dotok[:, s, HD * hh:HD * hh + HD], b[:, 0:HD], dst[:, i % 4, 2:3], MUL,
                   signal=freed(("dy", i))[0], value=freed(("dy", i))[1])

            dil_bias(0)
            for i in range(32):
                if i < 31:
                    dil_bias(i + 1)
                dil_out(i)
            for m in range(8):
                b = take(("dw", m))
                stt(h[:, m, :], b[:, 0:T], mc(1, 2, m), h[:, m, :], MUL, ADD, *freed(("dw", m)))
            settle()
            scaled(8)
            ffn(2)
            settle()
            norm_scale(9)
            for k in range(KT):
                stt(hn[:, k, :], h[:, k, :], col("final", k), rs[:, 2, :], MUL, MUL, sem("hn_ready"))
            for s in range(2):
                b = take(("fin", 2 * s))
                copy(outt[:, s, 0:512], b, *freed(("fin", 2 * s)))

        @block.scalar
        def _(act_):
            led = Ledger(act_, sem("act_own"))
            take0 = taker(act_)
            sum_jobs = sorted((n, job) for job, n in job_no.items() if job[0] == "ada")
            settle = led.settle

            def af(o, x, func=ACT.Identity, signal=None, value=None, **k):
                led.emit(nc.scalar.activation(o, x, func, **k), signal, value)

            def sums_before(job):
                while sum_jobs and sum_jobs[0][0] < job_no[job]:
                    aj = sum_jobs.pop(0)[1]
                    b = take0(aj)
                    if aj[1] >= 2:
                        act_.wait_ge(psum_ready, job_no["adc", aj[1] - 2] + 1)
                    af(sums[:, aj[1] % 2, :], b, ACT.Identity, *freed(aj))

            def take(job):
                sums_before(job)
                return take0(job)

            act_.wait_ge(sem("stage_clear"), 1)
            for r, m, src in pieces:
                act_.dma_start(stage[r % P:r % P + m, r // P, :], src).then_inc(stage_in, 16)
            act_.dma_start(dt_rows[0:8, :], a["s5_log_dt"].rearrange("l (j g) -> (l j) g", g=2)).then_inc(stage_in, 16)
            act_.dma_start(lora_w[0:64, :], a["rw_w2"][0]).then_inc(small_in, 16)
            act_.dma_start(lora_w[64:128, :], a["rw_a2"][0]).then_inc(small_in, 16)
            act_.dma_start(g2_w, a["rw_g2"][0]).then_inc(small_in, 16)
            act_.dma_start(cw2[:, 0, :], a["cmp_w2_k"][0]).then_inc(small_in, 16)
            act_.dma_start(cw2[:, 1, :], a["cmp_w2_k"][0]).then_inc(small_in, 16)
            act_.dma_start(cw2[:, 2, :], a["cmp_w2_v"][0]).then_inc(small_in, 16)
            act_.dma_start(wglu, a["s5_w_glu"][0].rearrange("(k p) n -> p k n", p=P)).then_inc(small_in, 16)
            for ri, nm in enumerate(("s5_b_re", "s5_b_im")):
                act_.dma_start(bfull[:, ri], a[nm][0].rearrange("(j g) n c -> (g n) j c", g=2)).then_inc(small_in, 16)
            for ri, nm in enumerate(("s5_c_re", "s5_c_im")):
                for x in range(2):
                    act_.dma_start(cdup[:, ri, :, HD * x:HD * x + HD],
                                   a[nm][0].rearrange("(f g) c n -> (g c) f n", f=2)).then_inc(small_in, 16)

            def squares(dst_, after=None):
                for f in range(2):
                    if after:
                        for k in range(4 * f, 4 * f + 4):
                            act_.wait_ge(*after(k))
                    af(dst_[:, 4 * f:4 * f + 4, :], h[:, 4 * f:4 * f + 4, :], ACT.Square, sem("squares"))

            def root(i):
                act_.wait_ge(sem("rs_rec"), i + 1)
                af(rs[:, 2, :], rs[:, 1, :], ACT.Sqrt, sem("rs_root"))

            for j in range(4):
                act_.wait_ge(*freed(("xT", j)))
            squares(hn)
            for j in range(2):
                act_.wait_ge(*freed(("par", j)))
            af(cond[:, :], cols("c", 8), ACT.Tanh, sem("cond_tanh"), scale=0.5)
            af(s5v[:, 0, :], cols("log_dt", 8), ACT.Exp, sem("s5_dt"))
            root(0)
            act_.wait_ge(sem("s5_lr"), 1)
            af(s5v[:, 2, :], s5v[:, 1, :], ACT.Exp)
            act_.wait_ge(sem("s5_angle"), 1)
            af(s5v[:, 7, :], s5v[:, 5, :], ACT.Sin, sem("theta_ready"))
            af(s5v[:, 8, :], s5v[:, 6, :], ACT.Sin, sem("theta_ready"))
            act_.wait_ge(sem("derived"), 1)

            def rw(i):
                b = take(("rw", i))
                af(zs[:, i, :], b[:, 0:T], ACT.Identity, sem("shift_own"), scale=omm(i))

            for i in range(11):
                rw(i)
            for i in range(3):
                b = take(("q", i))
                af(qT[:, i, :], b[:, 0:T], ACT.Identity, *freed(("q", i)), scale=0.125)
            for s in range(2):
                b = take(("vtok", s))
                af(vtok[:, s, :], b[:, 0:T], ACT.Identity, *freed(("vtok", s)))
            for i in range(4):
                b = take(("kc", i))
                af(kcs[0:64, i, :], b[0:64, 0:T])
                af(kcs[64:128, i, 0:T - 1], b[64:128, 1:T], ACT.Identity, *freed(("kc", i)))
            for i in range(4):
                b = take(("kd", i))
                af(kd[:, i, :], b[:, 0:T], ACT.Identity, *freed(("kd", i)))
            b = take(("gtok",))
            af(gate[:, :, :].rearrange("p a b -> p (a b)"), b[:, 0:36], ACT.Tanh, *freed(("gtok",)), scale=0.5)
            for i in range(2):
                b = take(("u", i))
                af(uT[:, i, :], b[:, 0:T], ACT.Identity, *freed(("u", i)))
            act_.wait_ge(*freed(("rw", 9)))
            af(zs[0:64, 9, :], zs[0:64, 9, :], ACT.Tanh, sem("lora_tanh"))
            act_.wait_ge(*freed(("rw", 10)))
            af(zs[:, 10, :], zs[:, 10, :], ACT.Tanh, sem("lora_tanh"), scale=0.5)
            b = take(("cmph",))
            act_.wait_ge(sem("tables"), 1)
            af(peh[:, :], b[:, 60:62])
            settle()
            af(hid[:, 0:2, 0:NCMP], shaped(b[:, 0:30], 2, NCMP), ACT.Gelu_apprx_tanh, bias=peh[:, 0:1])
            af(hidv[:, :, :, 0:NCMP], shaped(b[:, 30:60], 2, NCMP).unsqueeze(2).broadcast_to([P, 2, 3, NCMP]), ACT.Gelu_apprx_tanh, *freed(("cmph",)),
               bias=peh[:, 1:2])
            for f in range(2):
                for j in range(4 * f, 4 * f + 4):
                    sums_before(("y5", j))
                    act_.wait_ge(*freed(("y5", j)))
                af(ygel[:, f, :], ygel[:, f, :], ACT.Gelu_apprx_tanh, sem("ygel_ready"))
            for m in range(2):
                b = take(("glu", 2 + m))
                af(s5g[:, m, :], b[:, 0:T], ACT.Tanh, *freed(("glu", 2 + m)), scale=0.5)
            b = take(("kcT",))
            af(kcT[:, :, :], shaped(b[:, 0:30], 2, NCMP), ACT.Identity, *freed(("kcT",)))
            for s in range(2):
                sums_before(("cs", 1, 1))
                act_.wait_ge(sem("cmp_shifted"), s + 1)
                af(csc[:, s, :, 0:NCMP], csc[:, s, :, 0:NCMP], ACT.Exp, sem("cmp_exp"))

            def nsa_exp(i):
                s, u = i // 6, i % 2
                nk = P * (s + 1)
                sums_before(("ns", i))
                act_.wait_ge(sem("nsa_max"), i + 1)
                for br in range(2):
                    af(nsc[:, u, br, 0:nk], nsc[:, u, br, 0:nk], ACT.Exp, sem("nsa_probs") if br else None,
                       bias=nst[:, i % 4, 0, br:br + 1], accum_out=nst[:, i % 4, 1, br:br + 1])

            def nsa_copy(i):
                s, u = i // 6, i % 2
                b = take(("np", i))
                if i >= 2:
                    act_.wait_ge(psum_ready, job_no["nv", i - 2] + 1)
                af(npt[:, u].rearrange("p (a b) c -> p a b c", a=2)[:, :, 0:s + 1, :],
                   shaped(b, 2, 2, P)[:, :, 0:s + 1, :], ACT.Identity, *freed(("np", i)))

            nsa_exp(0)
            for i in range(12):
                nsa_copy(i)
                if i < 11:
                    nsa_exp(i + 1)
            for c in range(3):
                b = take(("oT", c))
                af(hn[:, 3 + c, :], b[:, 0:T], ACT.Identity, *freed(("oT", c)))

            for c in range(3):
                b = take(("wp", c))
                af(W[0][:, c, :], b[:, 0:T], ACT.Tanh, *freed(("wp", c)), scale=0.5, bias=hw0(c))
            for c in range(3):
                b = take(("ap", c))
                af(W[3][:, c, :], b[:, 0:T], ACT.Tanh, *freed(("ap", c)), scale=0.5, bias=ha0(c))
            for c in range(3):
                b = take(("gp", c))
                af(W[10][:, c, :], b[:, 0:T], ACT.Identity, *freed(("gp", c)))
            sums_before(("gp", 2))
            act_.wait_ge(sem("logs"), 1)
            af(W[2], W[1], ACT.Exp, sem("exps"), scale=-1.0)
            af(W[0], W[0], ACT.Exp, sem("exps"))
            af(W[1], W[1], ACT.Exp, sem("exps"))
            sums_before(("kks", 2))
            act_.wait_ge(sem("kk_rec"), 1)
            af(W[5], W[5], ACT.Sqrt, sem("kk_root"))
            for s in range(2):
                for x in range(4):
                    b = take(("tk", s, x))
                    o = AM[:, :, 0, :] if x == 0 else tok4[:, x]
                    af(o, shaped(b[:, 0:384], 3, P), ACT.Identity, *freed(("tk", s, x)))
                for name, _l, _r, _a, dst_ in INV:
                    b = take((name, s, 1))
                    af(tmat(dst_)[:, 1], shaped(b[:, 0:384], 3, P), ACT.Identity, *freed((name, s, 1)))
                b = take(("au", s, 1))
                af(AU[:, :, :, HD:P], shaped(b[:, 0:384], 3, 2, HD), ACT.Identity, *freed(("au", s, 1)))
                b = take(("ol", s))
                af(zs[:, 0:3, s * P:s * P + P], shaped(b[:, 0:384], 3, P), ACT.Identity, *freed(("ol", s)))
            for c in range(3):
                sums_before(("gm", c))
                act_.wait_ge(*freed(("gm", c)))
                af(zs[:, 3 + c, :], zs[:, c, :], ACT.Square, sem("gn_sq"))
            sums_before(("gv", 2))
            act_.wait_ge(sem("gn_rec"), 1)
            af(zs[:, 6:9, :], zs[:, 6:9, :], ACT.Sqrt, sem("gn_root"))

            def out_squares(jobs, y):
                for k, job in enumerate(jobs):
                    b = take(job)
                    af(sqb[:, k, :], b[:, 0:T], ACT.Square, sem("squares") if k % 4 == 3 else None)
                    af(y[:, k, :], b[:, 0:T], ACT.Identity, *freed(job))

            def h_at(n):
                return lambda k: (sem("h_ready"), 8 * n + k + 1)

            def modulate(n, dst_, sh):
                act_.wait_ge(sem("gains"), 5)
                for k in range(KT):
                    act_.wait_ge(sem("tn_ready"), 8 * tn_round[n] + k + 1)
                    af(dst_[:, k, :], tn[:, k, :], ACT.Identity, sem("hm_ready"), scale=gsc[:, 8 * n + k:8 * n + k + 1],
                       bias=mod[:, sh + k:sh + k + 1])

            def ffn(f):
                W0, B0, n = (row0["conv_w"], row0["conv_b"], 44) if f == 0 else \
                    (row0["fconv_w"] + 66 * (f - 1), row0["fconv_b"] + 22 * (f - 1), 22)
                parts = ("ug", "uu") if f == 0 else ("ug",)

                def own(j):
                    for x, nm in enumerate(parts):
                        b = take((nm, f, j))
                        if j >= 2:
                            act_.wait_ge(*((sem("act_ready"), j - 1) if f == 0 else freed(("uu", f, j - 2))))
                        w, bc = W0 + 2 * n + 22 * x + j, B0 + 22 * x + j
                        af(ct[:, j % 2, x, :], b[:, 0:T], ACT.Identity, sem("conv_own"), scale=par[:, w:w + 1],
                           bias=par[:, bc:bc + 1])

                def gated(j):
                    act_.wait_ge(*freed(("ug", f, j)))
                    t = ct[:, j % 2, 0, :]
                    af(t, t, ACT.Gelu_apprx_tanh if f == 0 else ACT.Silu, sem("gate_act"))

                for j in range(FT):
                    own(j)
                    if j:
                        gated(j - 1)
                gated(FT - 1)

            out_squares([("out", m) for m in range(8)], yb)
            root(1)
            squares(hn, h_at(0))
            root(2)
            ffn(0)
            out_squares([("down", 0, m) for m in range(8)], yb)
            root(3)
            out_squares([("pl", m) for m in range(8)], eb)
            root(4)
            for m in range(8):
                b = take(("pg", m))
                af(yb[:, m, :], b[:, 0:T], ACT.Tanh, *freed(("pg", m)), scale=0.5)
            squares(hn, h_at(2))
            root(5)
            modulate(0, hn, 0)
            for m in range(8):
                b = take(("pi", m))
                af(pu[:, m, :], b[:, 0:T], ACT.Identity, *freed(("pi", m)))
            for m in range(8):
                b = take(("pp", m))
                af(eT[:, m, :], b[:, 0:T], ACT.Identity, *freed(("pp", m)), scale=col("pool_scale", m))
            squares(hn, lambda k: freed(("po", k)))
            root(6)
            modulate(1, hn, 24)
            ffn(1)
            squares(hn, lambda k: freed(("down", 1, k)))
            root(7)
            modulate(2, hn, 96)
            modulate(3, hn2, 48)
            for m in range(24):
                b = take(("dk", m))
                af(dk[:, m, :], b[:, 0:T], ACT.Identity, *freed(("dk", m)))
            for i in range(6):
                for s in range(2):
                    b = take(("dv", i, s))
                    af(dv[:, s, 512 * i:512 * i + 512], b, ACT.Identity, *freed(("dv", i, s)))
            for m in range(24):
                b = take(("dq", m))
                af(dq[:, m, :], b[:, 0:T], ACT.Identity, *freed(("dq", m)), scale=0.125)

            def dil_exp(i):
                s, u = i % 2, i % 2
                n = 3 * P * (s + 1)
                act_.wait_ge(sem("dil_max"), i + 1)
                af(dsc[:, u, 0:n], dsc[:, u, 0:n], ACT.Exp, sem("dil_probs"), bias=dst[:, i % 4, 0:1],
                   accum_out=dst[:, i % 4, 1:2])

            dil_exp(0)
            for i in range(32):
                b = take(("dp", i, 0))
                if i >= 2:
                    act_.wait_ge(psum_ready, job_no["dy", i - 2] + 1)
                af(dpt[:, i % 2, 0:3, :], shaped(b[:, 0:384], 3, P), ACT.Identity, *freed(("dp", i, 0)))
                if i < 31:
                    dil_exp(i + 1)
            for j in range(4):
                b = take(("dt", j))
                af(hn[:, 2 * j:2 * j + 2, :], shaped(b, 2, T), ACT.Identity, *freed(("dt", j)))
            squares(hn2, lambda k: freed(("dw", k)))
            root(8)
            modulate(4, hn, 72)
            ffn(2)
            squares(hn2, lambda k: freed(("down", 2, k)))
            root(9)
            for s in range(2):
                b = take(("fin", 2 * s + 1))
                af(outt[:, s, 512:1024], b, ACT.Identity, *freed(("fin", 2 * s + 1)))


_INS = ['x', 'p', 'pre_mix_norm', 'post_mix_norm', 'pre_ffn_norm', 'post_ffn_norm', 'w_in', 'w_out', 'shift_mu',
        'rw_w0', 'rw_w2', 'rw_a0', 'rw_a2', 'rw_g2', 'rw_k_k', 'rw_k_a', 'rw_r_k', 'rw_gn_w', 'rw_gn_b', 'cmp_pe_k',
        'cmp_pe_v', 'cmp_w1_k', 'cmp_w2_k', 'cmp_w1_v', 'cmp_w2_v', 's5_lam_re', 's5_lam_im', 's5_log_dt', 's5_b_re',
        's5_b_im', 's5_c_re', 's5_c_im', 's5_d', 's5_w_glu', 'w_up', 'conv_w', 'conv_b', 'w_down', 'w_ple', 'ple_norm',
        'w_ple_gate', 'c_2', 'ada_w_2', 'ada_b_2', 'norm1_g_2', 'norm2_g_2', 'pool_w_in_2', 'pool_w_grp_2',
        'pool_scale_2', 'pool_w_out_2', 'kv_norm_g_2', 'kv_ada_w_2', 'kv_ada_b_2', 'w_kv_2', 'attn_w_q_2',
        'attn_w_o_2', 'ffn_w_up_2', 'ffn_conv_w_2', 'ffn_conv_b_2', 'ffn_w_down_2', 'final_g_2']


def kernel(**inputs):
    import numpy as _np
    import concourse.bacc as _bacc
    from concourse import mybir as _mybir
    from concourse.bass_utils import run_bass_kernel_spmd as _run

    nc = _bacc.Bacc("TRN2", target_bir_lowering=False, num_devices=1)
    arrays, args = {}, {}
    for name in _INS:
        a = _np.ascontiguousarray(inputs[name])
        arrays[f"in_{name}_dram"] = a
        args[name] = nc.dram_tensor(f"in_{name}_dram", a.shape, _mybir.dt.from_np(a.dtype), kind="ExternalInput").ap()
    out = nc.dram_tensor("out_0_dram", (1, T, D), _mybir.dt.float32, kind="ExternalOutput").ap()
    two_block_kernel(nc, args, out)
    r = _run(nc, [arrays], core_ids=[0])
    return r.results[0]["out_0_dram"]
```

```python
import math
from contextlib import ExitStack

import concourse.bass as bass
from concourse import mybir

F32 = mybir.dt.float32
F32R = mybir.dt.float32r
ALU = mybir.AluOpType
ACT = mybir.ActivationFunctionType
AX = mybir.AxisListType

P = 128
T = 256
D = 1024
KT = D // P
FF = 2816
FT = FF // P
HD = 64
BANKS = 8
SLOTS = 6
SLOT = 2048
HI_SLOTS = 4
FAR = 1.0e32
NCMP = 15
EPS = 1e-6
GN_EPS = 64e-5
MAGIC = 12582912.0
RW_TILES = 11
Q_COL, KC_COL, VC_COL, KS_COL, VS_COL, KW_COL, VW_COL, GATE_COL, U_COL = (
    1408, 1792, 1920, 2048, 2176, 2304, 2432, 2560, 2578)
N_IN = 2834


def nsa_slopes(n):
    def pow2(m):
        return [2.0 ** (-8.0 / m * (i + 1)) for i in range(m)]
    c = 2 ** math.floor(math.log2(n))
    return pow2(c) + pow2(2 * c)[0::2][: n - c]


def dilated_slopes(n):
    def pow2(m):
        start = 2.0 ** (-(2.0 ** -(math.log2(m) - 3)))
        return [start ** (i + 1) for i in range(m)]
    c = 2 ** math.floor(math.log2(n))
    s = pow2(n) if c == n else pow2(c) + pow2(2 * c)[0::2][: n - c]
    return sorted(s, reverse=True)


class Ledger:

    def __init__(self, eng, own):
        self.eng, self.own, self.count, self.open = eng, own, {}, {}

    def emit(self, ins, signal=None, value=None):
        signal = signal or self.own
        ins.then_inc(signal, 1)
        self.count[signal.name] = value or self.count.get(signal.name, 0) + 1
        self.open[signal.name] = (signal, self.count[signal.name])

    def settle(self):
        for signal, value in self.open.values():
            self.eng.wait_ge(signal, value)
        self.open = {}


def two_block_kernel(nc, a, out):
    ctx = ExitStack()
    with ctx:
        sems = {}

        def sem(name):
            if name not in sems:
                sems[name] = ctx.enter_context(nc.semaphore(name))
            return sems[name]

        def sb(name, cols, rows=P):
            return ctx.enter_context(nc.sbuf_tensor(name, [rows, cols], F32))

        def shaped(flat, *dims):
            names = "abcdef"[:len(dims)]
            return flat.rearrange(f"p ({' '.join(names)}) -> p {' '.join(names)}", **dict(zip(names, dims)))

        ident = sb("ident", P)
        ones_mean = sb("ones_mean", P)
        head_ones = sb("head_ones", P)
        head_mean = sb("head_mean", P)
        masks = shaped(sb("masks", 6 * P), 6, P)
        U8, L8M, L16M, L32M, U32S, U32I = (masks[:, i, :] for i in range(6))
        scan_keep = sb("scan_keep", T)
        dist = shaped(sb("dist", 2 * T), 2, T)
        late = sb("late", 10 * T)
        bdist = shaped(late[:, 0:6 * T], 3, 2, T)
        inv_count = shaped(late[:, 6 * T:10 * T], 4, T)
        sums = shaped(late[:, 0:1024], 2, 512)
        cond_wide = shaped(late[:, 1024:1280], KT, 32)
        cdist = shaped(sb("cdist", 30), 2, NCMP)
        cbias = shaped(sb("cbias", 180), 2, 6, NCMP)
        block3 = sb("block3", 3)
        block2 = sb("block2", 2)
        row_ok = sb("row_ok", 2)
        one_each = sb("one_each", 1)
        par = sb("par", 6 * P + 8)
        dt_rows = sb("dt_rows", 2)
        dt_wide = sb("dt_wide", P)
        drv = sb("drv", 32)
        cond = sb("cond", KT)
        mod = sb("mod", 112)
        gsc = sb("gsc", 40)
        pT = shaped(sb("pT", 2 * T), 2, T)
        h = shaped(sb("h", KT * T), KT, T)
        rs = shaped(sb("rs", 3 * T), 3, T)
        HN, ARENA0, ARENA = SLOTS * SLOT, SLOTS * SLOT + 2 * KT * T, 27520

        def place(name, off, dtype, *dims):
            with ExitStack() as brief:
                if off:
                    brief.enter_context(nc.sbuf_tensor(name + "_offset", [P, off], F32))
                flat = brief.enter_context(nc.sbuf_tensor(name, [P, math.prod(dims)], dtype))
            return shaped(flat, *dims)

        ring = place("ring", 0, F32, SLOTS, SLOT)
        ring_lo = place("ring_lo", 0, F32R, SLOTS, SLOT)
        hn = place("hn", HN, F32, KT, T)
        hn_lo = place("hn_lo", HN, F32R, KT, T)
        hn_hi = place("hn_hi", HN + KT * T, F32R, KT, T)
        arena = place("arena", ARENA0, F32, 1, ARENA)[:, 0, :]

        def at(off, *dims):
            n = math.prod(dims)
            assert off + n <= ARENA, (off, dims)
            flat = arena[:, off:off + n]
            return flat if len(dims) == 1 else shaped(flat, *dims)

        def parts(name, off, *dims):
            assert off + math.prod(dims) <= ARENA
            return place(name, ARENA0 + off, F32R, *dims)

        banks = ctx.enter_context(nc.psum_tensor("banks", [P, BANKS, 512], F32))

        xtok = at(0, 2, D)
        stage = at(2048, 6, P)
        ptok = at(2816, 2, T)
        zs = at(0, RW_TILES, T)
        kcs = at(2816, 4, T)
        kd = at(3840, 4, T)
        qT = at(4864, 3, T)
        vtok = at(5632, 2, T)
        gate = at(6144, 2, 18)
        uT = at(6208, 2, T)
        lora_w = at(6720, 384)
        g2_w = at(7104, 384)
        cw2 = at(7488, 3, HD)
        M0 = 7680
        tabC, tabS = at(M0, 8, T), at(M0 + 2048, 8, T)
        BT = at(M0 + 4096, 2, 2, P)
        CT = at(M0 + 4608, 2, 2, P)
        wglu = at(M0 + 5120, 2, 512)
        s5w = at(M0 + 6144, 2, 5, 2, T)
        s5v = at(M0 + 11264, 24, 8)
        bfull = at(M0 + 11456, 2, 8, 16)
        bmul = at(M0 + 11712, 2, 8, 16)
        bdup = at(M0 + 11968, 2, 8, 2, 16)
        cdup = at(M0 + 12480, 2, 2, P)
        ygel = at(M0 + 12992, 2, T)
        s5g = at(M0 + 13504, 2, T)
        powr = at(M0 + 14016, 2, 8)
        ptmp = at(M0 + 14032, 2, 8, P)
        assert M0 + 16080 <= ARENA
        nsc = at(M0 + 6144, 2, 2, T)
        npt = at(M0 + 7168, 2, 4, P)
        NB = M0 + 15312
        otok = at(M0 + 11712, 2, 384)
        hid = at(NB + 768, 2, 32)
        kcT = at(NB + 896, 2, NCMP)
        vbd = at(NB + 928, 2, 3, HD)
        csc = at(NB + 1312, 2, 6, 32)
        cst = at(NB + 1696, 2, 4, 6)
        nst = at(NB + 1744, 4, 4, 2)
        cpt = at(M0 + 14032, 2, P)
        hidv = at(M0 + 14288, 2, 3, 32)
        peh = at(NB + 1776, 2)
        W = [at(M0 + 768 * i, 3, T) for i in range(12)]
        tok4 = at(M0 + 9216, 4, 3, P)
        AM = at(M0 + 10752, 3, 2, P)
        AU = at(M0 + 11520, 3, 2, P)
        KEEP = [at(M0 + 12288 + 768 * i, 2, 3, P) for i in range(4)]
        TM = [at(M0 + 768 * i, 2, 3, P) for i in range(6)] + [at(M0 + 15360 + 768 * i, 2, 3, P) for i in range(3)]
        EB, HB = at(M0, 4, 3, P), at(M0 + 1536, 4, 3, P)
        ST = at(2816, 7, 3, P)
        Pend = at(5632, 3, 8)
        assert M0 + 17664 <= ARENA
        HI0 = ARENA - HI_SLOTS * SLOT
        ring_hi = parts("ring_hi", HI0, HI_SLOTS, SLOT)
        act = at(0, FT, T)
        act_lo, act_hi = parts("act_lo", 0, FT, T), parts("act_hi", 13312, FT, T)
        eT_lo = parts("eT_lo", 8192, KT, T)
        assert 13312 + FT * T <= HI0
        ct = at(5632, 2, 2, T)
        eT = at(8192, KT, T)
        sqb, tn, yb, eb = eT, eT, at(10240, KT, T), at(0, KT, T)
        pu = at(10240, KT, T)
        pw = at(12288, 2, 2, T)
        dk, dv, dq = at(0, 2, 6, T), at(3072, 2, 2, 3, T), at(6144, 2, 6, T)
        dsc = at(9216, 2, 3 * T)
        dpt = at(10752, 2, 6, P)
        dotok = at(12288, 2, D)
        dst = at(14336, 4, 4)
        hn2 = at(14400, KT, T)
        hn2_lo, hn2_hi = parts("hn2_lo", 14400, KT, T), parts("hn2_hi", 16448, KT, T)
        assert 18496 <= HI0
        outt = at(0, 2, D)
        dint = at(12288, 2, T)

        def rows(x, pat, **k):
            return x.rearrange(pat, **k)
        vecs = [("pre_mix", rows(a["pre_mix_norm"], "l (j p) -> (l j) p", p=P)),
                ("post_mix", rows(a["post_mix_norm"], "l (j p) -> (l j) p", p=P)),
                ("pre_ffn", rows(a["pre_ffn_norm"], "l (j p) -> (l j) p", p=P)),
                ("post_ffn", rows(a["post_ffn_norm"], "l (j p) -> (l j) p", p=P)),
                ("ple_norm", rows(a["ple_norm"], "l (j p) -> (l j) p", p=P)),
                ("norm1", rows(a["norm1_g_2"], "l (j p) -> (l j) p", p=P)),
                ("norm2", rows(a["norm2_g_2"], "l (j p) -> (l j) p", p=P)),
                ("kv_norm", rows(a["kv_norm_g_2"], "(j p) -> j p", p=P)),
                ("final", rows(a["final_g_2"], "(j p) -> j p", p=P)),
                ("c", rows(a["c_2"], "l (j p) -> (l j) p", p=P)),
                ("pool_scale", rows(a["pool_scale_2"], "l (j p) -> (l j) p", p=P)),
                ("mu", rows(a["shift_mu"], "l (j p) -> (l j) p", p=P)),
                ("w0", rows(a["rw_w0"], "l (j p) -> (l j) p", p=P)),
                ("a0", rows(a["rw_a0"], "l (j p) -> (l j) p", p=P)),
                ("k_k", rows(a["rw_k_k"], "l (j p) -> (l j) p", p=P)),
                ("k_a", rows(a["rw_k_a"], "l (j p) -> (l j) p", p=P)),
                ("r_k", rows(a["rw_r_k"], "l (j p) -> (l j) p", p=P)),
                ("gn_w", rows(a["rw_gn_w"], "l (j p) -> (l j) p", p=P)),
                ("gn_b", rows(a["rw_gn_b"], "l (j p) -> (l j) p", p=P)),
                ("pe_k", rows(a["cmp_pe_k"], "l (j q) d -> (l j) (q d)", q=2)),
                ("pe_v", rows(a["cmp_pe_v"], "l (j q) d -> (l j) (q d)", q=2)),
                ("s5_d", rows(a["s5_d"], "l (j p) -> (l j) p", p=P)),
                ("lam_re", rows(a["s5_lam_re"], "l (j g) n -> (l j) (g n)", g=2)),
                ("lam_im", rows(a["s5_lam_im"], "l (j g) n -> (l j) (g n)", g=2)),
                ("ada_b", rows(a["ada_b_2"], "l (j p) -> (l j) p", p=P)),
                ("kv_ada_b", rows(a["kv_ada_b_2"], "(j p) -> j p", p=P)),
                ("conv_w", rows(a["conv_w"], "l w (j p) -> (l w j) p", p=P)),
                ("conv_b", rows(a["conv_b"], "l (j p) -> (l j) p", p=P)),
                ("fconv_w", rows(a["ffn_conv_w_2"], "l w (j p) -> (l w j) p", p=P)),
                ("fconv_b", rows(a["ffn_conv_b_2"], "l (j p) -> (l j) p", p=P))]
        row0, n = {}, 0
        for name, src in vecs:
            row0[name] = n
            n += src.shape[0]
        assert n <= 6 * P
        row0["log_dt"] = 6 * P

        def col(name, i=0):
            return par[:, row0[name] + i:row0[name] + i + 1]

        def cols(name, n, i=0):
            return par[:, row0[name] + i:row0[name] + i + n]

        omm, hw0, ha0, omka = (lambda i: drv[:, i:i + 1]), (lambda i: drv[:, 11 + i:12 + i]), \
            (lambda i: drv[:, 14 + i:15 + i]), (lambda i: drv[:, 17 + i:18 + i])
        eps_col, halfpi = drv[:, 20:21], drv[:, 21:22]

        def mc(layer, which, i):
            j = 48 * layer + 8 * which + i
            return mod[:, j:j + 1]

        def kmaj(w, c0, c1, k0=0, k1=KT):
            return w.rearrange("(k p) n -> p k n", p=P)[:, k0:k1, c0:c1]

        def k256(w, i, k0=0, k1=KT):
            return [kmaj(w, 256 * i, 256 * i + 256, k0, k1)]

        chunk_src = {}
        w_in, w_out = a["w_in"][0], a["w_out"][0]
        for i in range(7):
            chunk_src["in", i] = k256(w_in, i)
        chunk_src["in", 7] = [kmaj(w_in, VS_COL, KW_COL), kmaj(w_in, VW_COL, GATE_COL)]
        for i, (c0, c1) in enumerate(((KC_COL, KC_COL + HD), (VC_COL, VC_COL + HD), (KS_COL, KS_COL + HD),
                                      (KW_COL, KW_COL + HD))):
            chunk_src["keys", i] = [kmaj(w_in, c, c + HD) for c in (c0, c0, c1, c1)]
        chunk_src["gate", 0] = [kmaj(w_in, GATE_COL, U_COL)]
        chunk_src["u", 0] = [kmaj(w_in, U_COL, N_IN)]
        for i in range(28):
            w = a["ada_w_2"][i // 12] if i < 24 else a["kv_ada_w_2"]
            c = 512 * (i % 12 if i < 24 else i - 24)
            for f in range(2):
                chunk_src["ada", i, f] = [kmaj(w, c, c + 512, 4 * f, 4 * f + 4)]
        for f, nm in enumerate(("cmp_w1_k", "cmp_w1_v")):
            chunk_src["cmp", f] = [a[nm][0].rearrange("(k p) n -> p k n", p=P)]
        chunk_src["ple", 0] = [a["w_ple"][0].rearrange("(k p) n -> p k n", p=P)]
        chunk_src["pgrp", 0] = [a["pool_w_grp_2"][0].rearrange("g (k p) n -> p (g k) n", p=P)]
        split = set()
        for nm, w, n in (("out", w_out, 4), ("pin", a["pool_w_in_2"][0], 4), ("pout", a["pool_w_out_2"][0], 4),
                         ("pleg", a["w_ple_gate"][0], 4), ("kv", a["w_kv_2"], 24), ("dq", a["attn_w_q_2"][0], 12),
                         ("do", a["attn_w_o_2"][0], 4)):
            for i in range(n):
                chunk_src[nm, i] = k256(w, i)
                split.add((nm, i))
        ffn_up = [a["w_up"][0], a["ffn_w_up_2"][0], a["ffn_w_up_2"][1]]
        ffn_down = [a["w_down"][0], a["ffn_w_down_2"][0], a["ffn_w_down_2"][1]]
        for f in range(3):
            for i in range(11):
                for x, nm in enumerate(("ug", "uu")):
                    chunk_src[nm, f, i] = k256(ffn_up[f], 11 * x + i)
                    split.add((nm, f, i))
            for m in range(4):
                for i in range(3):
                    chunk_src["down", f, m, i] = k256(ffn_down[f], m, 8 * i, min(8 * i + 8, FT))
                    split.add(("down", f, m, i))
        chunk_no, split_no = {}, {}
        chunk_landed, chunk_used = {}, {}
        used_at = {}

        def chunk_flat(key):
            n = sum(src.shape[1] * src.shape[2] for src in chunk_src[key])
            s = chunk_no[key] % SLOTS
            return (ring[:, s, 0:n], ring_lo[:, s, 0:n],
                    ring_hi[:, split_no[key] % HI_SLOTS, 0:n] if key in split_no else None)

        def chunk_view(key):
            flat = chunk_flat(key)[0]
            if key[0] == "keys":
                whole = shaped(flat, KT, 4, HD)
                return [whole[:, :, i, :] for i in range(4)]
            off, views = 0, []
            for src in chunk_src[key]:
                k, n = src.shape[1], src.shape[2]
                views.append(shaped(flat[:, off:off + k * n], k, n))
                off += k * n
            return views

        job_no = {}
        psum_ready = sem("psum_ready")
        bank_free = [sem(f"bank_free{b}") for b in range(BANKS)]

        def bank_of(job):
            return banks[:, job_no[job] % BANKS, :]

        def freed(job):
            return bank_free[job_no[job] % BANKS], job_no[job] // BANKS + 1

        pieces = []
        for name, src in vecs:
            r, n, k = row0[name], src.shape[0], 0
            while k < n:
                m = min(n - k, P - (r + k) % P)
                pieces.append((r + k, m, src[k:k + m, :]))
                k += m
        stage_total = [16 * len(pieces) + 16]

        def proj_share(i):
            return (3, 3, 3, 3, 2, 2, 2, 0)[i % 8]

        conv_base = [0, 2 * FT, 3 * FT]
        tn_round = [0, 1, 2, 2, 3]

        landed = [sem(f"slot_landed{s}") for s in range(SLOTS)]
        setup_in, stage_in, small_in = sem("setup_in"), sem("stage_in"), sem("small_in")

        block = ctx.enter_context(nc.Block())


        INV = [("L2", 0, 1, None, 4), ("N2", 1, 0, None, 5), ("L4", 5, 4, None, 6), ("Y1", 4, 7, 7, 8),
               ("T8", 6, 8, 8, 0), ("T8t", 0, None, None, 1), ("Ya", 2, 0, None, 4), ("T16", 1, 4, 0, 5),
               ("T16t", 5, None, None, 6), ("Yb", 3, 5, None, 7), ("T32", 6, 7, 5, 9)]

        def tmat(i):
            return KEEP[3] if i == 9 else TM[i]

        @block.tensor
        def _(pe):
            landed_count = [0] * SLOTS
            current = [None]

            def opened(job):
                n = job_no[job] = len(job_no)
                if n >= BANKS:
                    pe.wait_ge(bank_free[n % BANKS], n // BANKS)
                current[0] = job
                return banks[:, n % BANKS, :]

            def chunk(key):
                if key not in chunk_no:
                    slot = len(chunk_no) % SLOTS
                    chunk_no[key] = len(chunk_no)
                    landed_count[slot] += 16 * len(chunk_src[key])
                    chunk_landed[key] = (landed[slot], landed_count[slot])
                    if key in split:
                        split_no[key] = len(split_no)
                        pe.wait_ge(sem("lo_ready"), split_no[key] + 1)
                    else:
                        pe.wait_ge(*chunk_landed[key])
                used_at[key] = job_no[current[0]]
                chunk_used[key] = (psum_ready, used_at[key] + 1)
                if key in split:
                    k, n = chunk_src[key][0].shape[1:]
                    return [shaped(part, k, n) for part in chunk_flat(key)[1:]]
                return chunk_view(key)

            def copied(job):
                pe.wait_ge(*freed(job))

            def mm(o, l, r, start=True, stop=True, **k):
                return nc.tensor.matmul(o, l, r, start=start, stop=stop, **k)

            def close(ins):
                ins.then_inc(psum_ready, 1)

            def turn(job, pieces):
                b, off = opened(job), 0
                for src in pieces:
                    n, m = src.shape[0], src.shape[1]
                    last = nc.tensor.transpose(b[0:m, off:off + n], src, ident[0:n, 0:n])
                    off += n
                close(last)

            def tile(job, key, c0, rhs, part=0, kts=KT, m=P, first=None, n=T):
                b = opened(job)
                w = chunk(key)[part]
                for k in range(kts):
                    if first:
                        first(k)
                    l = w[:, k, c0:c0 + m]
                    last = mm(b[0:m, 0:n], l, rhs[:, k, :], start=(k == 0), stop=(k == kts - 1))
                close(last)

            def three_passes(o, w, x, start, stop):
                (w_lo, w_hi), (x_lo, x_hi) = w, x
                mm(o, w_hi, x_hi, start=start, stop=False)
                mm(o, w_hi, x_lo, start=False, stop=False)
                return mm(o, w_lo, x_hi, start=False, stop=stop)

            def split_tile(job, key, c0, x, first=None, ks=tuple(range(KT))):
                b = opened(job)
                w = chunk(key)
                for n, k in enumerate(ks):
                    if first is not None:
                        pe.wait_ge(sem("x_split"), KT * first + n + 1)
                    last = three_passes(b[:, 0:T], [v[:, k, c0:c0 + P] for v in w], [v[:, k, :] for v in x],
                                        n == 0, n == KT - 1)
                close(last)

            def mean_square(i, sq):
                b = opened(("ms", i))
                for k in range(KT):
                    if k % 4 == 0:
                        pe.wait_ge(sem("squares"), 2 * i + k // 4 + 1)
                    last = mm(b[:, 0:T], ones_mean[:, :], sq[:, k, :], start=(k == 0), stop=(k == KT - 1))
                close(last)

            ada_left = list(range(28))

            ada_open = []

            def ada_columns():
                if ada_open:
                    i = ada_open.pop()
                    copied(("ada", i))
                    b = opened(("adc", i))
                    for m in range(4):
                        last = mm(b[:, m:m + 1], sums[:, i % 2, m * P:m * P + P], one_each[:, :])
                    close(last)

            def ada(n=1):
                for _ in range(n):
                    if ada_left:
                        i = ada_left.pop(0)
                        if i == 0:
                            pe.wait_ge(sem("cond_ready"), 1)
                        b = opened(("ada", i))
                        for k in range(KT):
                            w = chunk(("ada", i, k // 4))[0]
                            q = 32 * (k % 4)
                            last = mm(b[q:q + 32, :], cond_wide[:, k, :], w[:, k % 4, :], start=(k < 4), stop=(k >= 4),
                                      tile_position=(0, q))
                        close(last)
                        ada_columns()
                        ada_open.append(i)

            pe.wait_ge(sem("ident_ready"), 2)
            pe.wait_ge(setup_in, 32)
            for j in range(4):
                turn(("xT", j), [xtok[:, s, (2 * j + k) * P:(2 * j + k + 1) * P] for k in range(2) for s in range(2)])
            pe.wait_ge(sem("stage_clear"), 1)
            pe.wait_ge(stage_in, stage_total[0])
            pe.wait_ge(sem("dt_spread"), 1)
            for j in range(2):
                turn(("par", j), [stage[:, 3 * j + i, :] for i in range(3)] + [dt_wide[0:8, :]] * j)
            turn(("pT",), [ptok[:, s, k * P:k * P + P] for k in range(2) for s in range(2)])
            pe.wait_ge(sem("consts"), 1)
            mean_square(0, hn)

            def hn_wait(n):
                return lambda k: pe.wait_ge(sem("hn_ready"), 8 * n + k + 1)

            w0 = hn_wait(0)
            for i in range(14):
                tile(("rw", i) if i < 11 else ("q", i - 11), ("in", i // 2), 128 * (i % 2), hn,
                     first=w0 if i == 0 else None)
            for s in range(2):
                b = opened(("vtok", s))
                w = chunk(("in", 7))
                for x in range(2):
                    for k in range(KT):
                        last = mm(b[:, x * P:x * P + P], hn[:, k, s * P:s * P + P], w[x][:, k, :],
                                  start=(k == 0), stop=(k == KT - 1))
                close(last)
            for x, nm in enumerate(("kc", "kd")):
                for i in range(4):
                    b = opened((nm, i))
                    key = ("keys", 2 * x + i // 2)
                    chunk(key)
                    w = shaped(chunk_flat(key)[0], KT, 2, P)
                    for k in range(KT):
                        last = mm(b[:, 0:T], w[:, k, i % 2, :], hn[:, k, :], start=(k == 0), stop=(k == KT - 1))
                    close(last)
            b = opened(("gtok",))
            w = chunk(("gate", 0))[0]
            for s in range(2):
                for k in range(KT):
                    last = mm(b[:, s * 18:s * 18 + 18], hn[:, k, s * P:s * P + P], w[:, k, 0:18],
                              start=(k == 0), stop=(k == KT - 1))
            close(last)
            for i in range(2):
                tile(("u", i), ("u", 0), 128 * i, hn)

            pe.wait_ge(sem("b_ready"), 1)
            turn(("bT",), [bdup[:, r, 4 * f:4 * f + 4, :, :].rearrange("p a b c -> p (a b c)")
                           for r in range(2) for f in range(2)])
            turn(("cT",), [cdup[:, r, f, :] for r in range(2) for f in range(2)])
            copied(("bT",))
            copied(("cT",))
            for i in range(2):
                copied(("u", i))

            def bu(j):
                b, q = opened(("bu", j)), 32 * (j % 4)
                for r in range(2):
                    last = mm(b[:, r * T:r * T + T], BT[q:q + 32, r, j // 4, :], uT[q:q + 32, j // 4, :])
                close(last)

            def y5(j):
                b, q, r2 = opened(("y5", j)), 32 * (j % 4), j % 2
                pe.wait_ge(sem("s5_states"), j + 1)
                for r in range(2):
                    last = mm(b[q:q + 32, 0:T], CT[:, r, j // 4, q:q + 32], s5w[:, r2, 4, r, :],
                              start=(r == 0), stop=(r == 1))
                close(last)

            bu(0)
            for j in range(8):
                if j < 7:
                    bu(j + 1)
                ada()
                y5(j)
            b = opened(("cmph",))
            w1 = [chunk(("cmp", v))[0] for v in range(2)]
            for i in range(4):
                copied(("kc", i))
            for v in range(2):
                for lp in range(16):
                    last = mm(b[:, 30 * v:30 * v + 30], w1[v][:, lp, :],
                              kcs[:, 2 * v:2 * v + 2, 2 * lp:2 * lp + 225:16], start=(lp == 0), stop=(lp == 15))
            for v in range(2):
                for lp in range(16):
                    last = mm(b[:, 60 + v:61 + v], w1[v][:, lp, :], col("pe_v" if v else "pe_k", lp),
                              start=(lp == 0), stop=(lp == 15))
            close(last)
            pe.wait_ge(sem("ygel_ready"), 2)
            for m in range(4):
                b = opened(("glu", m))
                for k in range(2):
                    last = mm(b[:, 0:T], wglu[:, k, m * P:m * P + P], ygel[:, k, :], start=(k == 0), stop=(k == 1))
                close(last)
            copied(("cmph",))
            b = opened(("kcT",))
            close(mm(b[:, 0:30], cw2[:, 0:2, :].rearrange("p a b -> p (a b)"), hid[:, 0:2, 0:NCMP]))
            b = opened(("vc",))
            for g in range(2):
                last = mm(b[0:96, g * HD:g * HD + HD], hidv[:, g, :, :].rearrange("p a b -> p (a b)"), cw2[:, 2, :])
            close(last)
            ada()
            copied(("kcT",))
            for i in range(3):
                copied(("q", i))
            for s in range(2):
                for x in range(2):
                    b = opened(("cs", s, x))
                    for i in range(3):
                        hh = x + 2 * i
                        last = mm(b[:, 32 * i:32 * i + NCMP], qT[64 * x:64 * x + 64, hh // 2, s * P:s * P + P],
                                  kcT[64 * x:64 * x + 64, hh // 3, :])
                    close(last)

            def nsa_scores(i):
                s, hh = i // 6, i % 6
                x, g, nk = hh % 2, hh // 3, P * (s + 1)
                b = opened(("ns", i))
                for br in range(2):
                    last = mm(b[:, T * br:T * br + nk], qT[64 * x:64 * x + 64, hh // 2, s * P:s * P + P],
                              kd[64 * x:64 * x + 64, 2 * br + g, 0:nk])
                close(last)

            def nsa_turn(i):
                s = i // 6
                pe.wait_ge(sem("nsa_probs"), i + 1)
                b = opened(("np", i))
                for br in range(2):
                    for kt in range(s + 1):
                        o = (2 * br + kt) * P
                        last = nc.tensor.transpose(b[:, o:o + P], nsc[:, i % 2, br, kt * P:kt * P + P], ident[:, :])
                close(last)

            def nsa_values(i):
                s, g = i // 6, (i % 6) // 3
                copied(("np", i))
                b = opened(("nv", i))
                for br in range(2):
                    for kt in range(s + 1):
                        last = mm(b[:, br * HD:br * HD + HD], npt[:, i % 2, 2 * br + kt, :],
                                  vtok[:, kt, br * P + g * HD:br * P + g * HD + HD], start=(kt == 0), stop=(kt == s))
                close(last)

            for i in range(4):
                copied(("kd", i))
            nsa_scores(0)
            for s in range(2):
                pe.wait_ge(sem("cmp_probs"), s + 1)
                turn(("ct", s), [csc[:, s, 3 * g:3 * g + 3, :].rearrange("p a b -> p (a b)") for g in range(2)])
                copied(("ct", s))
                copied(("vc",))
                b = opened(("cpv", s))
                for g in range(2):
                    last = mm(b[:, 192 * g:192 * g + 192], cpt[0:96, g, :],
                              vbd[0:96, g, :, :].rearrange("p a b -> p (a b)"))
                close(last)
            for i in range(12):
                if i < 11:
                    nsa_scores(i + 1)
                if i > 0:
                    nsa_values(i - 1)
                nsa_turn(i)
                ada()
            nsa_values(11)
            ada()
            pe.wait_ge(sem("otok_ready"), 1)
            for c in range(3):
                turn(("oT", c), [otok[:, s, c * P:c * P + P] for s in range(2)])

            pe.wait_ge(sem("lora_tanh"), 2)
            pe.wait_ge(sem("lora_in"), 1)
            for c in range(3):
                b = opened(("wp", c))
                close(mm(b[:, 0:T], lora_w[0:64, c * P:c * P + P], zs[0:64, 9, :]))
            for c in range(3):
                b = opened(("ap", c))
                close(mm(b[:, 0:T], lora_w[64:128, c * P:c * P + P], zs[64:128, 9, :]))
            for c in range(3):
                b = opened(("gp", c))
                close(mm(b[:, 0:T], g2_w[:, c * P:c * P + P], zs[:, 10, :]))
            pe.wait_ge(sem("kk_sq"), 1)
            for c in range(3):
                b = opened(("kks", c))
                close(mm(b[:, 0:T], head_ones[:, :], W[5][:, c, :]))
            ada()
            pe.wait_ge(sem("bonus_in"), 1)
            for c in range(3):
                b = opened(("bon", c))
                close(mm(b[:, 0:T], head_ones[:, :], W[5][:, c, :]))
            pe.wait_ge(sem("gram_in"), 1)
            for s in range(2):
                cut = slice(s * P, s * P + P)
                for x, src in enumerate((W[6], W[7], W[8], zs[:, 6:9, :])):
                    turn(("tk", s, x), [src[:, c, cut] for c in range(3)])
                for name, lw, rw in (("N", 7, 6), ("L", 6, 7), ("MT", 8, 6), ("Rb", 7, 9), ("Rk", 8, 9)):
                    for p in range(2):
                        b, q = opened((name, s, p)), slice(64 * p, 64 * p + 64)
                        for c in range(3):
                            last = mm(b[:, c * P:c * P + P], W[lw][q, c, cut], W[rw][q, c, cut])
                        close(last)
                for p in range(2):
                    copied(("N", s, p))
                    copied(("L", s, p))
                pe.wait_ge(sem("tri_ready"), s + 1)
                for k, (name, lw, rw, add, dst) in enumerate(INV):
                    for p in range(2):
                        if k:
                            copied((INV[k - 1][0], s, p))
                        b = opened((name, s, p))
                        for c in range(3):
                            o = b[:, c * P:c * P + P]
                            if rw is None:
                                last = nc.tensor.transpose(o, tmat(lw)[:, p, c, :], ident[:, :])
                            else:
                                last = mm(o, tmat(lw)[:, p, c, :], tmat(rw)[:, p, c, :], stop=add is None)
                                if add is not None:
                                    last = mm(o, ident[:, :], tmat(add)[:, p, c, :], start=False)
                        close(last)
                    if k % 4 == 3:
                        ada()
                for p in range(2):
                    copied(("MT", s, p))
                for x in range(4):
                    copied(("tk", s, x))
                b = opened(("mv", s))
                for c in range(3):
                    for p in range(2):
                        o = c * P + p * HD
                        last = mm(b[:, o:o + HD], KEEP[0][:, p, c, :], tok4[:, 3, c, p * HD:p * HD + HD])
                close(last)
                copied(("mv", s))
                for p in range(2):
                    copied(("T32", s, p))
                    b = opened(("au", s, p))
                    for c in range(3):
                        last = mm(b[:, c * P:c * P + P], KEEP[3][:, p, c, :], AM[:, c, :, p * HD:p * HD + HD])
                    close(last)
                for p in range(2):
                    copied(("au", s, p))
                for r in range(4):
                    q = slice(32 * r, 32 * r + 32)
                    if 4 * s + r < 7:
                        b = opened(("H", s, r))
                        for c in range(3):
                            o = b[:, c * P:c * P + P]
                            mm(o, tok4[q, 1, c, :], AU[q, c, 1, :], stop=False)
                            last = mm(o, tok4[q, 2, c, :], tok4[q, 3, c, :], start=False)
                        close(last)
                    if 0 < 4 * s + r < 7:
                        b = opened(("E", s, r))
                        for c in range(3):
                            last = mm(b[:, c * P:c * P + P], AU[q, c, 0, :], tok4[q, 1, c, :])
                        close(last)
                for p in range(2):
                    copied(("Rb", s, p))
                    copied(("Rk", s, p))
                b = opened(("rt", s))
                for p in range(2):
                    for c in range(3):
                        last = mm(b[64 * p:64 * p + 64, c * P:c * P + P], AU[:, c, 0, p * HD:p * HD + HD],
                                  KEEP[1][:, p, c, :])
                close(last)
                for r in range(4):
                    q = 4 * s + r
                    if 0 < q < 7:
                        copied(("E", s, r))
                        copied(("H", 0, 0) if q == 1 else ("st", q - 1))
                        b = opened(("st", q))
                        for c in range(3):
                            o = b[:, c * P:c * P + P]
                            mm(o, EB[:, r, c, :], ST[:, q - 1, c, :], stop=False)
                            last = mm(o, ident[:, :], ST[:, q - 1, c, :], start=False)
                        close(last)
                b = opened(("ol", s))
                for c in range(3):
                    for p in range(2):
                        last = mm(b[64 * p:64 * p + 64, c * P:c * P + P], AU[:, c, 1, p * HD:p * HD + HD],
                                  KEEP[1][:, p, c, :], start=(c == 0), stop=False, skip_group_check=True)
                for c in range(3):
                    for p in range(2):
                        last = mm(b[64 * p:64 * p + 64, c * P:c * P + P], tok4[:, 3, c, p * HD:p * HD + HD],
                                  KEEP[2][:, p, c, :], start=False, stop=False, skip_group_check=True)
                copied(("st", 3 if s == 0 else 6))
                copied(("rt", s))
                for q in range(max(1, 4 * s), 4 * s + 4):
                    for c in range(3):
                        o = c * P + 32 * (q % 4)
                        last = mm(b[:, o:o + 32], ST[:, q - 1, c, :], W[9][:, c, 32 * q:32 * q + 32],
                                  start=False, stop=(q == 4 * s + 3), skip_group_check=True)
                close(last)
            for s in range(2):
                copied(("ol", s))
            for c in range(3):
                b = opened(("gm", c))
                close(mm(b[:, 0:T], head_mean[:, :], zs[:, c, :]))
            for c in range(3):
                pe.wait_ge(sem("gn_sq"), c + 1)
                b = opened(("gv", c))
                close(mm(b[:, 0:T], head_mean[:, :], zs[:, 3 + c, :]))
            ada(28)
            ada_columns()

            for i in range(2):
                copied(("glu", i))
            for c in range(3):
                copied(("oT", c))
            for m in range(8):
                split_tile(("out", m), ("out", m // 2), 128 * (m % 2), (hn_lo, hn_hi), first=0 if m == 0 else None,
                           ks=(3, 4, 5, 6, 7, 0, 1, 2))

            down_used = [0]

            def ffn(f, first):
                for j in range(FT):
                    for nm in ("ug", "uu"):
                        split_tile((nm, f, j), (nm, f, j // 2), 128 * (j % 2), (hn_lo, hn_hi),
                                   first=first if j == 0 and nm == "ug" else None)
                for m in range(4):
                    outs = [opened(("down", f, 2 * m + i)) for i in range(2)]
                    for c in range(3):
                        key = ("down", f, m, c)
                        w = chunk(key)
                        n = chunk_src[key][0].shape[1]
                        for i in range(2):
                            for k in range(n):
                                t = 8 * c + k
                                if m == 0 and i == 0:
                                    pe.wait_ge(sem("act_split"), FT * f + t + 1)
                                last = three_passes(outs[i][:, 0:T], [v[:, k, i * P:i * P + P] for v in w],
                                                    (act_lo[:, t, :], act_hi[:, t, :]), t == 0, t == FT - 1)
                            if c == 2:
                                close(last)
                        if c < 2:
                            last.then_inc(sem("down_used"), 1)
                            down_used[0] += 1
                            chunk_used[key] = (sem("down_used"), down_used[0])
                            used_at[key] = job_no["down", f, 2 * m] - 0.5

            mean_square(1, sqb)
            mean_square(2, hn)
            ffn(0, 1)
            mean_square(3, sqb)
            for m in range(8):
                tile(("pl", m), ("ple", 0), 128 * m, pT, kts=2)
            mean_square(4, sqb)
            for m in range(8):
                split_tile(("pg", m), ("pleg", m // 2), 128 * (m % 2), (hn_lo, hn_hi), first=2 if m == 0 else None)

            mean_square(5, hn)
            for m in range(8):
                split_tile(("pi", m), ("pin", m // 2), 128 * (m % 2), (hn_lo, hn_hi), first=3 if m == 0 else None)
            for m in range(8):
                b = opened(("pp", m))
                w = chunk(("pgrp", 0))[0]
                for k in range(2):
                    t = 2 * (m // 2) + k
                    pe.wait_ge(sem("pooled"), t + 1)
                    last = mm(b[:, 0:T], w[:, t, (m % 2) * P:(m % 2) * P + P], pu[:, t, :], start=(k == 0), stop=(k == 1))
                close(last)
            for m in range(8):
                split_tile(("po", m), ("pout", m // 2), 128 * (m % 2), (eT_lo, hn_hi), first=4 if m == 0 else None)
            mean_square(6, hn)
            ffn(1, 5)

            mean_square(7, hn)

            def projections(c):
                for br in range(3):
                    for i in range(2):
                        yield split_tile(("dk", c, br, i), ("kv", 4 * br + c), 128 * i, (hn_lo, hn_hi),
                                         first=6 if c == br == i == 0 else None)
                for br in range(3):
                    for s in range(2):
                        b = opened(("dv", c, br, s))
                        w = chunk(("kv", 12 + 4 * br + c))
                        for k in range(KT):
                            last = three_passes(b[:, 0:T], [v[:, k, s * P:s * P + P] for v in (hn_lo, hn_hi)],
                                                [v[:, k, :] for v in w], k == 0, k == KT - 1)
                        yield close(last)
                for br in range(3):
                    for i in range(2):
                        yield split_tile(("dq", c, br, i), ("dq", 4 * br + c), 128 * i, (hn2_lo, hn2_hi),
                                         first=7 if c == br == i == 0 else None)

            def dil_scores(i):
                hh, s = i // 2, i % 2
                c = i // 8
                nk, q = P * (s + 1), slice(64 * (hh % 2), 64 * (hh % 2) + 64)
                if i % 8 == 0:
                    for br in range(3):
                        for x in range(2):
                            copied(("dk", c, br, x))
                            copied(("dq", c, br, x))
                for job, brs in (("da", (0, 1)), ("db", (2,))):
                    b = opened((job, i))
                    for br in brs:
                        t = 2 * br + hh // 2 % 2
                        last = mm(b[:, T * (br % 2):T * (br % 2) + nk], dq[q, c % 2, t, s * P:s * P + P],
                                  dk[q, c % 2, t, 0:nk])
                    close(last)

            def dil_turn(i):
                s = i % 2
                pe.wait_ge(sem("dil_probs"), i + 1)
                n = 3 * (s + 1)
                src = dsc[:, i % 2, 0:n * P]
                turn(("dp", i, 0), [src[:, k * P:k * P + P] for k in range(3)])
                if s:
                    turn(("dp", i, 1), [src[:, k * P:k * P + P] for k in range(3, 6)])

            def dil_values(i):
                hh, s = i // 2, i % 2
                for x in range(s + 1):
                    copied(("dp", i, x))
                if i % 8 == 0:
                    for br in range(3):
                        for x in range(2):
                            copied(("dv", i // 8, br, x))
                b = opened(("dy", i))
                n = 3 * (s + 1)
                for k in range(n):
                    br, kt = k // (s + 1), k % (s + 1)
                    c = HD * (hh % 4)
                    last = mm(b[:, 0:HD], dpt[:, i % 2, k, :], dv[:, i // 8 % 2, kt, br, c:c + HD], start=(k == 0), stop=(k == n - 1))
                close(last)

            for _ in projections(0):
                pass
            dil_scores(0)
            for i in range(32):
                if i < 31:
                    dil_scores(i + 1)
                if i > 0:
                    dil_values(i - 1)
                dil_turn(i)
                if i % 8 == 0:
                    coming = projections(i // 8 + 1) if i < 24 else iter(())
                for _ in range(proj_share(i)):
                    next(coming, None)
            dil_values(31)
            copied(("dy", 30))
            copied(("dy", 31))
            for j in range(4):
                turn(("dt", j), [dotok[:, s, (2 * j + k) * P:(2 * j + k + 1) * P] for k in range(2) for s in range(2)])
            for m in range(8):
                split_tile(("dw", m), ("do", m // 2), 128 * (m % 2), (hn_lo, hn_hi), first=8 if m == 0 else None)
            mean_square(8, hn2)
            ffn(2, 9)
            mean_square(9, hn)
            for s in range(2):
                for f in range(2):
                    for k in range(4):
                        if s == 0:
                            pe.wait_ge(sem("hn_ready"), 16 + 4 * f + k + 1)
                    turn(("fin", 2 * s + f), [hn[:, 4 * f + k, s * P:s * P + P] for k in range(4)])

        def taker(eng):
            def take(job):
                eng.wait_ge(psum_ready, job_no[job] + 1)
                return bank_of(job)
            return take

        SMALL = 16 * 13

        @block.sync
        def _(sp):
            sp.dma_start(xtok, a["x"][0].rearrange("(s p) d -> p s d", p=P)).then_inc(setup_in, 16)
            sp.dma_start(ptok, a["p"][0, 0].rearrange("(s p) d -> p s d", p=P)).then_inc(setup_in, 16)
            order = sorted(chunk_no, key=chunk_no.get)
            for n, key in enumerate(order):
                if n >= SLOTS:
                    sp.wait_ge(*chunk_used[order[n - SLOTS]])
                for dst, src in zip(chunk_view(key), chunk_src[key]):
                    sp.dma_start(dst, src).then_inc(landed[n % SLOTS], 16)
            for s in range(2):
                for f in range(2):
                    sp.wait_ge(*freed(("fin", 2 * s + f)))
                    sp.dma_start(out[0, s * P:s * P + P, 512 * f:512 * f + 512],
                                 outt[:, s, 512 * f:512 * f + 512]).then_inc(sem("out_done"), 16)
            sp.wait_ge(sem("out_done"), 64)

        @block.gpsimd
        def _(pool):
            led = Ledger(pool, sem("pool_own"))
            g = nc.gpsimd

            def keep_if(o, op, base, cm, pattern, fill=0.0, signal=None):
                led.settle()
                led.emit(g.affine_select(out=o, in_=o, compare_op=op, fill=fill, base=base, pattern=pattern,
                                         channel_multiplier=cm), signal)

            def on_blocks(o, size, nb, width):
                v = o if width == 1 else o.rearrange("p (b c) -> p b c", b=nb)
                pat = [[-size, nb]] + ([[0, width]] if width > 1 else [])
                neg = [[size, nb]] + ([[0, width]] if width > 1 else [])
                keep_if(v, ALU.is_ge, 0, 1, pat)
                keep_if(v, ALU.is_ge, size - 1, -1, neg)

            led.emit(g.memset(ident[:, :], 0.0), sem("ident_ready"))
            keep_if(ident[:, :], ALU.not_equal, 0, 1, [[-1, P]], 1.0, sem("ident_ready"))
            led.emit(g.memset(ones_mean[:, :], 1.0 / D))
            led.emit(g.memset(head_ones[:, :], 1.0))
            led.emit(g.memset(head_mean[:, :], 1.0 / HD))
            led.emit(g.memset(masks[:, :, :], 1.0))
            led.emit(g.memset(scan_keep[:, :], 1.0))
            led.emit(g.memset(block3[:, :], 1.0))
            led.emit(g.memset(block2[:, :], 1.0))
            led.emit(g.memset(row_ok[:, :], 1.0))
            on_blocks(head_ones[:, :], HD, 2, HD)
            on_blocks(head_mean[:, :], HD, 2, HD)
            on_blocks(block3[:, :], 32, 3, 1)
            on_blocks(block2[:, :], HD, 2, 1)
            for m, size in ((U8, 8), (L8M, 8), (L16M, 16), (L32M, 32), (U32S, 32), (U32I, 32)):
                on_blocks(m, size, P // size, size)
            for m, up, strict in ((U8, 1, 1), (L8M, 0, 1), (L16M, 0, 1), (L32M, 0, 1), (U32S, 1, 1), (U32I, 1, 0)):
                keep_if(m, ALU.is_ge, -strict, -1 if up else 1, [[1 if up else -1, P]])
            led.settle()
            led.emit(g.tensor_tensor(L32M, L32M, L16M, ALU.subtract))
            led.settle()
            led.emit(g.tensor_tensor(L16M, L16M, L8M, ALU.subtract))
            keep_if(row_ok[:, :], ALU.is_ge, -31, 1, [[P, 2]])
            led.emit(g.memset(shaped(scan_keep[:, :], 8, 32)[:, :, 0], 0.0))
            led.emit(g.iota(dist[:, :, :], pattern=[[P, 2], [-1, T]], base=0, channel_multiplier=1,
                            allow_small_or_imprecise_dtypes=True))
            led.emit(g.iota(cdist[:, :, :], pattern=[[P, 2], [-16, NCMP]], base=-31, channel_multiplier=1,
                            allow_small_or_imprecise_dtypes=True))
            keep_if(dist[:, :, :], ALU.is_ge, 0, 1, [[P, 2], [-1, T]], FAR)
            keep_if(cdist[:, :, :], ALU.is_ge, -31, 1, [[P, 2], [-16, NCMP]], FAR)
            led.emit(g.memset(one_each[:, :], 0.0))
            for q in (0, 32, 64, 96):
                keep_if(one_each[:, :], ALU.not_equal, -q, 1, [[0, 1]], 1.0)
            led.settle()
            for hh, sl in enumerate(nsa_slopes(6)):
                led.emit(g.tensor_scalar(cbias[:, :, hh, :], cdist[:, :, :], -sl, None, ALU.mult))
            led.settle()
            led.emit(g.memset(hid[:, :, :], 0.0))
            led.emit(g.memset(csc[:, :, :, :], 0.0), sem("consts"))
            led.emit(g.memset(tabC[:, :, 0:1], 1.0))
            led.emit(g.memset(tabS[:, :, 0:1], 0.0))

            pool.wait_ge(sem("theta_ready"), 2)
            led.emit(g.tensor_copy(powr[:, 0, :], s5v[:, 8, :]))
            led.emit(g.tensor_copy(powr[:, 1, :], s5v[:, 7, :]))
            n = 1
            while n < T:
                led.settle()
                pc, ps = (powr[:, x, :].unsqueeze(2).broadcast_to([P, 8, n]) for x in range(2))
                lo, hi = slice(0, n), slice(n, 2 * n)
                for tab, (x, y), op in ((tabC, (tabC, tabS), ALU.subtract), (tabS, (tabS, tabC), ALU.add)):
                    led.settle()
                    led.emit(g.tensor_tensor(ptmp[:, 0, :, lo], x[:, :, lo], pc, ALU.mult))
                    led.emit(g.tensor_tensor(ptmp[:, 1, :, lo], y[:, :, lo], ps, ALU.mult))
                    led.settle()
                    led.emit(g.tensor_tensor(tab[:, :, hi], ptmp[:, 0, :, lo], ptmp[:, 1, :, lo], op))
                n *= 2
                if n < T:
                    led.settle()
                    led.emit(g.tensor_tensor(s5v[:, 18, :], powr[:, 0, :], powr[:, 0, :], ALU.mult))
                    led.emit(g.tensor_tensor(s5v[:, 19, :], powr[:, 1, :], powr[:, 1, :], ALU.mult))
                    led.emit(g.tensor_tensor(s5v[:, 20, :], powr[:, 0, :], powr[:, 1, :], ALU.mult))
                    led.settle()
                    led.emit(g.tensor_tensor(powr[:, 0, :], s5v[:, 18, :], s5v[:, 19, :], ALU.subtract))
                    led.emit(g.tensor_scalar(powr[:, 1, :], s5v[:, 20, :], 2.0, None, ALU.mult))
            led.settle()
            led.emit(g.memset(hidv[:, :, :, :], 0.0), sem("tables"))

            def turned_in(j):
                w = s5w[:, j % 2]
                pool.wait_ge(*freed(("bu", j)))
                led.emit(g.tensor_tensor(w[:, 2, 0, :], w[:, 0, 0, :], w[:, 1, 1, :], ALU.add))
                led.emit(g.tensor_tensor(w[:, 2, 1, :], w[:, 0, 1, :], w[:, 1, 0, :], ALU.subtract), sem("s5_in"))

            turned_in(0)
            for j in range(8):
                if j < 7:
                    turned_in(j + 1)
                w = s5w[:, j % 2]
                pool.wait_ge(sem("s5_out"), j + 1)
                if j >= 2:
                    pool.wait_ge(psum_ready, job_no["y5", j - 2] + 1)
                led.emit(g.tensor_tensor(w[:, 4, 0, :], w[:, 0, 0, :], w[:, 1, 1, :], ALU.subtract))
                led.emit(g.tensor_tensor(w[:, 4, 1, :], w[:, 0, 1, :], w[:, 1, 0, :], ALU.add), sem("s5_states"))

            def low_parts(keys):
                for key in keys:
                    raw, low, high = chunk_flat(key)
                    pool.wait_ge(sem("hi_ready"), split_no[key] + 1)
                    led.emit(g.tensor_tensor(low, raw, high.bitcast(F32), ALU.subtract), sem("lo_ready"))

            order = sorted(split_no, key=split_no.get)
            low_parts(order[:10])
            pool.wait_ge(sem("gains"), 5)
            led.emit(g.iota(dint.bitcast(mybir.dt.int32), pattern=[[P, 2], [-1, T]], base=0, channel_multiplier=1))
            led.emit(g.iota(inv_count[:, :, :], pattern=[[0, 4], [1, T]], base=1, channel_multiplier=0,
                            allow_small_or_imprecise_dtypes=True))
            led.emit(g.tensor_copy(bdist[:, 0, :, :], dist[:, :, :]))
            keep_if(bdist[:, 0, :, :], ALU.is_ge, P, -1, [[-P, 2], [1, T]], FAR)
            for w in range(4):
                led.emit(g.tensor_scalar(inv_count[:, w, :], inv_count[:, w, :], float(2 ** (w + 1)), None, ALU.min),
                         sem("late_consts") if w == 3 else None)
            low_parts(order[10:])

        @block.vector
        def _(dve):
            led = Ledger(dve, sem("dve_own"))
            v = nc.vector
            take0 = taker(dve)
            ada_jobs = sorted((n, job) for job, n in job_no.items() if job[0] == "adc")

            def modulation_before(job):
                while ada_jobs and ada_jobs[0][0] < job_no[job]:
                    aj = ada_jobs.pop(0)[1]
                    b, i = take0(aj), aj[1]
                    led.emit(v.tensor_tensor(mod[:, 4 * i:4 * i + 4], b[:, 0:4], cols("ada_b", 4, 4 * i), ALU.add),
                             *freed(aj))

            def take(job):
                modulation_before(job)
                return take0(job)

            def placed(job):
                modulation_before(job)
                dve.wait_ge(*freed(job))

            def tt(o, x, y, op, signal=None, value=None):
                led.emit(v.tensor_tensor(o, x, y, op), signal, value)

            def ts(o, x, s1, op0, s2=None, op1=ALU.bypass, signal=None, value=None):
                led.emit(v.tensor_scalar(o, x, s1, s2, op0, op1) if s2 is not None else
                         v.tensor_scalar(o, x, s1, None, op0), signal, value)

            def stt(o, x, s, y, op0, op1, signal=None, value=None):
                led.emit(v.scalar_tensor_tensor(out=o, in0=x, scalar=s, in1=y, op0=op0, op1=op1), signal, value)

            def copy(o, x, signal=None, value=None):
                led.emit(v.tensor_copy(o, x), signal, value)

            def rec(o, x, signal=None):
                led.emit(v.reciprocal(o, x), signal)

            settle = led.settle
            MUL, ADD, SUB = ALU.mult, ALU.add, ALU.subtract

            def low_part(n, low, x, high):
                dve.wait_ge(sem("x_high"), n + 1)
                tt(low, x, high.bitcast(F32), SUB, sem("x_split"))

            led.emit(v.memset(stage[:, :, :], 0.0), sem("stage_clear"))
            for j in range(4):
                b = take(("xT", j))
                copy(h[:, 2 * j:2 * j + 2, :], shaped(b, 2, T), *freed(("xT", j)))
            dve.wait_ge(stage_in, stage_total[0])
            copy(shaped(dt_wide[0:8, :], 2, HD), dt_rows[0:8, :].unsqueeze(2).broadcast_to([8, 2, HD]), sem("dt_spread"))
            for j in range(2):
                b, n = take(("par", j)), 384 + 8 * j
                copy(par[:, 384 * j:384 * j + n], b[:, 0:n], *freed(("par", j)))
            b = take(("pT",))
            copy(pT[:, :, :], shaped(b, 2, T), *freed(("pT",)))
            settle()
            ts(drv[:, 0:11], cols("mu", 11), -1.0, MUL, 1.0, ADD)
            ts(drv[:, 11:14], cols("w0", 3), 0.5, MUL)
            ts(drv[:, 14:17], cols("a0", 3), 0.5, MUL)
            ts(drv[:, 17:20], cols("k_a", 3), -1.0, MUL, 1.0, ADD, signal=sem("derived"))
            dve.wait_ge(sem("cond_tanh"), 1)
            stt(cond[:, :], cond[:, :], 1.0, cols("c", 8), ADD, MUL)
            settle()
            ts(cond_wide[:, :, :], cond[:, :].unsqueeze(2).broadcast_to([P, KT, 32]), 0.5, MUL, signal=sem("cond_ready"))

            def norm_scale(i, eps=EPS):
                b = take(("ms", i))
                ts(rs[:, 0, :], b[:, 0:T], eps, ADD, signal=freed(("ms", i))[0], value=freed(("ms", i))[1])
                settle()
                rec(rs[:, 1, :], rs[:, 0, :], sem("rs_rec"))
                dve.wait_ge(sem("rs_root"), i + 1)

            dve.wait_ge(sem("consts"), 1)

            norm_scale(0)
            for k in range(KT):
                stt(hn[:, k, :], h[:, k, :], col("pre_mix", k), rs[:, 2, :], MUL, MUL, sem("hn_ready"))

            def z(i):
                return s5v[:, i, :]
            lre, lim = cols("lam_re", 8), cols("lam_im", 8)
            dve.wait_ge(sem("s5_dt"), 1)
            tt(z(1), lre, z(0), MUL)
            tt(z(3), lim, z(0), MUL, sem("s5_lr"))
            settle()
            ts(z(4), z(3), 1.0 / (2 * math.pi), MUL, MAGIC, ADD)
            settle()
            ts(z(4), z(4), MAGIC, SUB)
            settle()
            stt(z(5), z(4), -6.28125, z(3), MUL, ADD)
            settle()
            stt(z(5), z(4), -(2 * math.pi - 6.28125), z(5), MUL, ADD)
            settle()
            ts(z(5), z(5), 3.1415925, ALU.min, -3.1415925, ALU.max)
            settle()
            ts(z(6), z(5), math.pi / 2, ALU.is_gt, -2 * math.pi, MUL)
            settle()
            stt(z(6), z(5), math.pi / 2, z(6), ADD, ADD)
            settle()
            ts(z(6), z(6), 3.1415925, ALU.min, -3.1415925, ALU.max, signal=sem("s5_angle"))
            tt(z(11), lre, lre, MUL)
            tt(z(12), lim, lim, MUL)
            settle()
            tt(z(11), z(11), z(12), ADD)
            settle()
            rec(z(12), z(11))
            dve.wait_ge(sem("theta_ready"), 2)
            tt(z(9), z(2), z(8), MUL)
            tt(z(10), z(2), z(7), MUL)
            settle()
            ts(z(15), z(9), 1.0, SUB)
            settle()
            tt(z(13), z(15), lre, MUL)
            tt(z(16), z(10), lim, MUL)
            tt(z(14), z(10), lre, MUL)
            tt(z(17), z(15), lim, MUL)
            settle()
            tt(z(13), z(13), z(16), ADD)
            tt(z(14), z(14), z(17), SUB)
            settle()
            tt(z(13), z(13), z(12), MUL)
            tt(z(14), z(14), z(12), MUL)
            settle()
            dve.wait_ge(small_in, SMALL)
            fre, fim = (z(i).unsqueeze(2).broadcast_to([P, 8, 16]) for i in (13, 14))
            for ri, (x, y, op) in enumerate(((0, 1, SUB), (1, 0, ADD))):
                tt(bmul[:, ri], bfull[:, x], fre, MUL)
                tt(bdup[:, ri, :, 0, :], bfull[:, y], fim, MUL)
                settle()
                tt(bmul[:, ri], bmul[:, ri], bdup[:, ri, :, 0, :], op)
                settle()
                for bb in range(2):
                    ts(bdup[:, ri, :, bb, :], bmul[:, ri], block2[:, bb:bb + 1], MUL,
                       signal=sem("b_ready") if ri and bb else None)

            for i in range(RW_TILES):
                b = take(("rw", i))
                dve.wait_ge(sem("shift_own"), i + 1)
                stt(zs[:, i, 1:T], b[:, 0:T - 1], col("mu", i), zs[:, i, 1:T], MUL, ADD, *freed(("rw", i)))
            placed(("gtok",))
            ts(gate[:, :, :], gate[:, :, :], 0.5, MUL, 0.5, ADD)

            b = take(("bT",))
            copy(BT[:, :, :, :].rearrange("p a b c -> p (a b c)"), b, *freed(("bT",)))
            b = take(("cT",))
            pb = shaped(b, 2, 2, 4, 2, 16)
            for ri in range(2):
                for bb in range(2):
                    last = ri == 1 and bb == 1
                    o = CT[:, ri].rearrange("p f (a b c) -> p f a b c", a=4, b=2)[:, :, :, bb, :]
                    ts(o, pb[:, ri, :, :, bb, :], block2[:, bb:bb + 1], MUL, -1.0 if ri else 1.0, MUL,
                       signal=freed(("cT",))[0] if last else None, value=freed(("cT",))[1] if last else None)
            dve.wait_ge(sem("tables"), 1)

            def s5_in(j):
                b = shaped(take(("bu", j)), 2, T)
                w = s5w[:, j % 2]
                if j >= 2:
                    dve.wait_ge(sem("s5_states"), j - 1)
                tt(w[:, 0], b, tabC[:, j, :].unsqueeze(1).broadcast_to([P, 2, T]), MUL)
                tt(w[:, 1], b, tabS[:, j, :].unsqueeze(1).broadcast_to([P, 2, T]), MUL, *freed(("bu", j)))

            def s5_scan(j):
                w = s5w[:, j % 2]
                dve.wait_ge(sem("s5_in"), j + 1)
                for x in range(2):
                    led.emit(v.tensor_tensor_scan(w[:, 3, x, :], z(2)[:, j:j + 1].broadcast_to([P, T]), w[:, 2, x, :],
                                                  0.0, MUL, ADD))
                settle()
                tt(w[:, 0], w[:, 3], tabC[:, j, :].unsqueeze(1).broadcast_to([P, 2, T]), MUL)
                tt(w[:, 1], w[:, 3], tabS[:, j, :].unsqueeze(1).broadcast_to([P, 2, T]), MUL, sem("s5_out"))

            def s5_y(j):
                b, q = take(("y5", j)), slice(32 * (j % 4), 32 * (j % 4) + 32)
                f = j // 4
                stt(ygel[q, f, :], uT[q, f, :], par[q, row0["s5_d"] + f:row0["s5_d"] + f + 1], b[q, 0:T], MUL, ADD,
                    *freed(("y5", j)))

            s5_in(0)
            for j in range(8):
                if j < 7:
                    s5_in(j + 1)
                s5_scan(j)
                if j:
                    s5_y(j - 1)
            s5_y(7)
            for m in range(2):
                placed(("glu", 2 + m))
                ts(s5g[:, m, :], s5g[:, m, :], 0.5, MUL, 0.5, ADD)
            settle()
            for m in range(2):
                b = take(("glu", m))
                tt(hn[:, 6 + m, :], b[:, 0:T], s5g[:, m, :], MUL, *freed(("glu", m)))

            b = take(("vc",))
            for x in range(3):
                ts(vbd[0:96, :, x, :], shaped(b[0:96, 0:P], 2, HD), block3[0:96, x:x + 1], MUL,
                   signal=freed(("vc",))[0] if x == 2 else None, value=freed(("vc",))[1] if x == 2 else None)
            for s in range(2):
                for x in range(2):
                    b = take(("cs", s, x))
                    tt(csc[:, s, x::2, 0:NCMP], shaped(b[:, 0:96], 3, 32)[:, :, 0:NCMP], cbias[:, s, x::2, :], ADD,
                       *freed(("cs", s, x)))
            settle()
            for s in range(2):
                led.emit(v.tensor_reduce(cst[:, s, 0, :], csc[:, s, :, 0:NCMP], AX.X, ALU.max))
            settle()
            for s in range(2):
                tt(csc[:, s, :, 0:NCMP], csc[:, s, :, 0:NCMP], cst[:, s, 0, :].unsqueeze(2).broadcast_to([P, 6, NCMP]),
                   SUB, sem("cmp_shifted"))
            for s in range(2):
                dve.wait_ge(sem("cmp_exp"), s + 1)
                led.emit(v.tensor_reduce(cst[:, s, 1, :], csc[:, s, :, 0:NCMP], AX.X, ADD))
            settle()
            for s in range(2):
                rec(cst[:, s, 2, :], cst[:, s, 1, :])
            settle()
            for s in range(2):
                stt(cst[:, s, 3, :], cst[:, s, 2, :], row_ok[:, s:s + 1], gate[:, s, 0::3], MUL, MUL)
            settle()
            for s in range(2):
                tt(csc[:, s, :, 0:NCMP], csc[:, s, :, 0:NCMP], cst[:, s, 3, :].unsqueeze(2).broadcast_to([P, 6, NCMP]),
                   MUL, sem("cmp_probs"))

            slopes6 = nsa_slopes(6)

            def nsa_bias(i):
                s, hh, u = i // 6, i % 6, i % 2
                nk = P * (s + 1)
                b = shaped(take(("ns", i)), 2, T)
                if i >= 2:
                    dve.wait_ge(psum_ready, job_no["np", i - 2] + 1)
                stt(nsc[:, u, :, 0:nk], dist[:, s, 0:nk].unsqueeze(1).broadcast_to([P, 2, nk]), -slopes6[hh],
                    b[:, :, 0:nk], MUL, ADD, *freed(("ns", i)))
                settle()
                led.emit(v.tensor_reduce(nst[:, i % 4, 0, :], nsc[:, u, :, 0:nk], AX.X, ALU.max, negate=True),
                         sem("nsa_max"))

            def nsa_out(i):
                s, hh, u = i // 6, i % 6, i % 2
                dve.wait_ge(sem("nsa_probs"), i + 1)
                rec(nst[:, i % 4, 2, :], nst[:, i % 4, 1, :])
                settle()
                tt(nst[:, i % 4, 3, :], nst[:, i % 4, 2, :], gate[:, s, 3 * hh + 1:3 * hh + 3], MUL)
                b = take(("nv", i))
                o = otok[:, s, HD * hh:HD * hh + HD]
                settle()
                stt(o, b[:, 0:HD], nst[:, i % 4, 3, 0:1], o, MUL, ADD)
                settle()
                stt(o, b[:, HD:2 * HD], nst[:, i % 4, 3, 1:2], o, MUL, ADD, *freed(("nv", i)))

            nsa_bias(0)
            for s in range(2):
                b = take(("ct", s))
                if s:
                    dve.wait_ge(psum_ready, job_no["cpv", 0] + 1)
                copy(cpt[0:96, :, :], shaped(b[0:96, 0:T], 2, P), *freed(("ct", s)))
                b = take(("cpv", s))
                copy(otok[:, s, :], b[:, 0:384], *freed(("cpv", s)))
            for i in range(12):
                if i < 11:
                    nsa_bias(i + 1)
                if i > 0:
                    nsa_out(i - 1)
            nsa_out(11)
            settle()
            led.emit(v.memset(nst[:, 0, 0, :], 0.0), sem("otok_ready"))

            rr, kk_, vv = zs[:, 0:3, :], zs[:, 3:6, :], zs[:, 6:9, :]
            dve.wait_ge(sem("lora_tanh"), 2)
            ts(zs[:, 10, :], zs[:, 10, :], 0.5, MUL, 0.5, ADD, signal=sem("lora_in"))
            for c in range(3):
                placed(("wp", c))
            ts(W[0], W[0], -0.5 * math.exp(-0.5), MUL, -0.5 * math.exp(-0.5), ADD)
            settle()
            for c in range(3):
                led.emit(v.tensor_tensor_scan(W[1][:, c, :], scan_keep[:, :], W[0][:, c, :], 0.0, MUL, ADD))
            settle()
            tt(W[0], W[1], W[0], SUB, sem("logs"))
            for c in range(3):
                ts(W[4][:, c, :], kk_[:, c, :], col("k_k", c), MUL)
            settle()
            tt(W[5], W[4], W[4], MUL, sem("kk_sq"))
            for c in range(3):
                placed(("ap", c))
            ts(W[3], W[3], 0.5, MUL, 0.5, ADD)
            settle()
            for c in range(3):
                ts(W[11][:, c, :], W[3][:, c, :], col("k_a", c), MUL, omka(c), ADD)
            settle()
            tt(kk_, kk_, W[11], MUL)
            for c in range(3):
                b = take(("kks", c))
                ts(W[5][:, c, :], b[:, 0:T], 1e-24, ALU.max, signal=freed(("kks", c))[0], value=freed(("kks", c))[1])
            settle()
            rec(W[5], W[5], sem("kk_rec"))
            dve.wait_ge(sem("exps"), 3)
            tt(W[8], kk_, W[2], MUL)
            tt(W[9], rr, W[1], MUL)
            copy(Pend[:, :, :], W[1][:, :, 31::32])
            dve.wait_ge(sem("kk_root"), 1)
            tt(W[4], W[4], W[5], MUL)
            settle()
            for c in range(3):
                stt(W[5][:, c, :], rr[:, c, :], col("r_k", c), kk_[:, c, :], MUL, MUL,
                    sem("bonus_in") if c == 2 else None)
            tt(W[7], W[4], W[3], MUL)
            stt(W[6].rearrange("p a b -> p (a b)"), W[4].rearrange("p a b -> p (a b)"), -1.0,
                W[0].rearrange("p a b -> p (a b)"), MUL, MUL)
            settle()
            tt(W[7], W[7], W[2], MUL, sem("gram_in"))
            for k in range(3, 8):
                low_part(k - 3, hn_lo[:, k, :], hn[:, k, :], hn_hi[:, k, :])
            for c in range(3):
                b = take(("bon", c))
                tt(W[11][:, c, :], b[:, 0:T], vv[:, c, :], MUL, *freed(("bon", c)))

            def over3(m):
                return m.unsqueeze(1).broadcast_to([P, 3, P])

            def three(b):
                return shaped(b[:, 0:384], 3, P)

            for s in range(2):
                cut = slice(s * P, s * P + P)
                for p in range(2):
                    b = take(("N", s, p))
                    tt(TM[0][:, p], three(b), over3(U8), MUL, *freed(("N", s, p)))
                for p in range(2):
                    b = take(("L", s, p))
                    tt(TM[1][:, p], three(b), over3(L8M), MUL)
                    tt(TM[2][:, p], three(b), over3(L16M), MUL)
                    tt(TM[3][:, p], three(b), over3(L32M), MUL, *freed(("L", s, p)))
                settle()
                for p in range(2):
                    tt(TM[7][:, p], TM[0][:, p], over3(ident[:, :]), ADD, sem("tri_ready") if p else None)
                for name, k, m in (("MT", 0, U32S), ("Rb", 1, U32I), ("Rk", 2, U32I)):
                    for p in range(2):
                        b = take((name, s, p))
                        tt(KEEP[k][:, p], three(b), over3(m), MUL, *freed((name, s, p)))
                for name, _l, _r, _a, to in INV:
                    b = take((name, s, 0))
                    copy(tmat(to)[:, 0], three(b), *freed((name, s, 0)))
                b = take(("mv", s))
                copy(AM[:, :, 1, :], three(b), *freed(("mv", s)))
                b = take(("au", s, 0))
                copy(AU[:, :, :, 0:HD], shaped(b[:, 0:384], 3, 2, HD), *freed(("au", s, 0)))
                for r in range(4):
                    q = 4 * s + r
                    if q < 7:
                        b = three(take(("H", s, r)))
                        for c in range(3):
                            o = ST[:, 0, c, :] if q == 0 else HB[:, r, c, :]
                            stt(o, b[:, c, :], Pend[:, c, q:q + 1], head_ones[:, :], MUL, MUL,
                                *(freed(("H", s, r)) if c == 2 else (None, None)))
                    if 0 < q < 7:
                        b = three(take(("E", s, r)))
                        tt(EB[:, r], b, over3(head_ones[:, :]), MUL, *freed(("E", s, r)))
                b = take(("rt", s))
                tt(W[9][:, :, cut], three(b), W[9][:, :, cut], ADD, *freed(("rt", s)))
                settle()
                for r in range(4):
                    q = 4 * s + r
                    if 0 < q < 7:
                        b = three(take(("st", q)))
                        for c in range(3):
                            stt(ST[:, q, c, :], b[:, c, :], Pend[:, c, q:q + 1], HB[:, r, c, :], MUL, ADD,
                                *(freed(("st", q)) if c == 2 else (None, None)))
            for s in range(2):
                placed(("ol", s))
            for c in range(3):
                b = take(("gm", c))
                tt(zs[:, c, :], zs[:, c, :], b[:, 0:T], SUB, *freed(("gm", c)))
            for c in range(3):
                b = take(("gv", c))
                ts(zs[:, 6 + c, :], b[:, 0:T], GN_EPS, ADD, signal=freed(("gv", c))[0], value=freed(("gv", c))[1])
            settle()
            rec(vv, vv, sem("gn_rec"))
            dve.wait_ge(sem("gn_root"), 1)
            tt(rr, rr, vv, MUL)
            settle()
            for c in range(3):
                ts(zs[:, c, :], zs[:, c, :], col("gn_w", c), MUL, col("gn_b", c), ADD)
            settle()
            tt(rr, rr, W[11], ADD)
            settle()
            for c in range(3):
                tt(hn[:, c, :], zs[:, c, :], W[10][:, c, :], MUL, sem("mix_rw"))
            for c in range(3):
                low_part(5 + c, hn_lo[:, c, :], hn[:, c, :], hn_hi[:, c, :])

            def add_normed(i, gain, y):
                norm_scale(i)
                for k in range(KT):
                    stt(y[:, k, :], y[:, k, :], col(gain, k), rs[:, 2, :], MUL, MUL)
                settle()
                for k in range(KT):
                    tt(h[:, k, :], h[:, k, :], y[:, k, :], ADD, sem("h_ready"))

            def ffn(f):
                W0, B0, n = (row0["conv_w"], row0["conv_b"], 44) if f == 0 else \
                    (row0["fconv_w"] + 66 * (f - 1), row0["fconv_b"] + 22 * (f - 1), 22)

                def product(j):
                    u = j % 2
                    dve.wait_ge(sem("gate_act"), FT * f + j + 1)
                    other = ct[:, u, 1, :] if f == 0 else take(("uu", f, j))[:, 0:T]
                    tt(act[:, j, :], other, ct[:, u, 0, :], MUL)
                    tt(act_hi[:, j, :], other, ct[:, u, 0, :], MUL, *((sem("act_ready"),) if f == 0 else freed(("uu", f, j))))

                def act_low(j):
                    tt(act_lo[:, j, :], act[:, j, :], act_hi[:, j, :].bitcast(F32), SUB, sem("act_split"))

                parts = ("ug", "uu") if f == 0 else ("ug",)
                for j in range(FT):
                    bs = []
                    for x, nm in enumerate(parts):
                        bs.append(take((nm, f, j)))
                        dve.wait_ge(sem("conv_own"), conv_base[f] + len(parts) * j + x + 1)
                        t = ct[:, j % 2, x, :]
                        w = W0 + n + 22 * x + j
                        stt(t[:, 1:T], bs[x][:, 0:T - 1], par[:, w:w + 1], t[:, 1:T], MUL, ADD)
                    settle()
                    for x, nm in enumerate(parts):
                        t = ct[:, j % 2, x, :]
                        w = W0 + 22 * x + j
                        stt(t[:, 2:T], bs[x][:, 0:T - 2], par[:, w:w + 1], t[:, 2:T], MUL, ADD, *freed((nm, f, j)))
                    if j > 1:
                        act_low(j - 2)
                    if j:
                        product(j - 1)
                settle()
                act_low(FT - 2)
                product(FT - 1)
                settle()
                act_low(FT - 1)
                if f:
                    for m in range(8):
                        b = take(("down", f, m))
                        stt(h[:, m, :], b[:, 0:T], mc(f - 1, 5, m), h[:, m, :], MUL, ADD, *freed(("down", f, m)))

            def scaled(i, *rounds):
                norm_scale(i)
                for k in range(KT):
                    tt(tn[:, k, :], h[:, k, :], rs[:, 2, :], MUL, sem("tn_ready"))
                for rnd, n, x, low, high in rounds:
                    for k in range(KT):
                        dve.wait_ge(sem("hm_ready"), 8 * n + k + 1)
                        low_part(8 * rnd + k, low[:, k, :], x[:, k, :], high[:, k, :])

            add_normed(1, "post_mix", yb)
            norm_scale(2)
            for k in range(KT):
                stt(hn[:, k, :], h[:, k, :], col("pre_ffn", k), rs[:, 2, :], MUL, MUL, sem("hn_ready"))
            for k in range(KT):
                low_part(8 + k, hn_lo[:, k, :], hn[:, k, :], hn_hi[:, k, :])
            for n, (l, sc, gn) in enumerate(((0, 1, cols("norm1", 8)), (0, 4, cols("norm2", 8)), (2, 1, cols("kv_norm", 8)),
                                             (1, 1, cols("norm1", 8, 8)), (1, 4, cols("norm2", 8, 8)))):
                c0 = 48 * l + 8 * sc
                stt(gsc[:, 8 * n:8 * n + 8], mod[:, c0:c0 + 8], 1.0, gn, ADD, MUL, sem("gains"))
            ffn(0)
            dve.wait_ge(sem("late_consts"), 1)
            rec(inv_count[:, :, :], inv_count[:, :, :])
            for br, low in ((1, 3), (2, 15)):
                m = bdist[:, br, :, :]
                led.emit(v.tensor_scalar(m.bitcast(mybir.dt.int32), dint.bitcast(mybir.dt.int32), low, None,
                                         ALU.bitwise_and))
            settle()
            for br in (1, 2):
                m = bdist[:, br, :, :]
                ts(m, m.bitcast(mybir.dt.int32), 1.0, ALU.min, FAR, MUL)
            settle()
            for br in (1, 2):
                tt(bdist[:, br, :, :], bdist[:, br, :, :], dist[:, :, :], ALU.max)
            add_normed(3, "post_ffn", yb)
            for k in range(KT):
                low_part(16 + k, hn_lo[:, k, :], h[:, k, :], hn_hi[:, k, :])
            norm_scale(4)
            for k in range(KT):
                stt(eb[:, k, :], eb[:, k, :], col("ple_norm", k), rs[:, 2, :], MUL, MUL)
            settle()
            for m in range(8):
                placed(("pg", m))
                stt(yb[:, m, :], yb[:, m, :], 1.0, eb[:, m, :], ADD, MUL)
            settle()
            for m in range(8):
                stt(h[:, m, :], yb[:, m, :], 0.5, h[:, m, :], MUL, ADD, sem("h_ready"))

            scaled(5, (3, 0, hn, hn_lo, hn_hi))
            for gq in range(4):
                for i in range(2):
                    placed(("pi", 2 * gq + i))
                src = pu[:, 2 * gq:2 * gq + 2, :]
                for l in range(gq + 1):
                    sh, o = 2 ** l, pw[:, l % 2]
                    copy(o[:, :, 0:sh], src[:, :, 0:sh])
                    tt(o[:, :, sh:T], src[:, :, sh:T], src[:, :, 0:T - sh], ADD)
                    settle()
                    src = o
                tt(src, src, inv_count[:, gq, :].unsqueeze(1).broadcast_to([P, 2, T]), MUL)
                settle()
                for i in range(2):
                    tt(pu[:, 2 * gq + i, :], src[:, i, :], pu[:, 2 * gq + i, :], SUB, sem("pooled"))
                settle()
            for m in range(8):
                placed(("pp", m))
                low_part(32 + m, eT_lo[:, m, :], eT[:, m, :], hn_hi[:, m, :])
            for m in range(8):
                b = take(("po", m))
                stt(h[:, m, :], b[:, 0:T], mc(0, 2, m), h[:, m, :], MUL, ADD, *freed(("po", m)))
            settle()
            scaled(6, (5, 1, hn, hn_lo, hn_hi))
            ffn(1)
            settle()
            scaled(7, (6, 2, hn, hn_lo, hn_hi), (7, 3, hn2, hn2_lo, hn2_hi))

            slopes48 = dilated_slopes(48)

            def dil_bias(i):
                hh, s, u = i // 2, i % 2, i % 2
                nk = P * (s + 1)
                if i >= 2:
                    dve.wait_ge(psum_ready, job_no["dp", i - 2, s] + 1)
                for job, brs in (("da", (0, 1)), ("db", (2,))):
                    b = take((job, i))
                    for br in brs:
                        last = br != 0
                        o = T * (br % 2)
                        stt(dsc[:, u, br * nk:br * nk + nk], bdist[:, br, s, 0:nk], -float(slopes48[16 * br + hh]),
                            b[:, o:o + nk], MUL, ADD, *(freed((job, i)) if last else (None, None)))
                settle()
                led.emit(v.tensor_reduce(dst[:, i % 4, 0:1], dsc[:, u, 0:3 * nk], AX.X, ALU.max, negate=True),
                         sem("dil_max"))

            def dil_out(i):
                hh, s, u = i // 2, i % 2, i % 2
                if s:
                    b = take(("dp", i, 1))
                    if i >= 2:
                        dve.wait_ge(psum_ready, job_no["dy", i - 2] + 1)
                    copy(dpt[:, u, 3:6, :], three(b), *freed(("dp", i, 1)))
                dve.wait_ge(sem("dil_probs"), i + 1)
                rec(dst[:, i % 4, 2:3], dst[:, i % 4, 1:2])
                settle()
                b = take(("dy", i))
                ts(dotok[:, s, HD * hh:HD * hh + HD], b[:, 0:HD], dst[:, i % 4, 2:3], MUL,
                   signal=freed(("dy", i))[0], value=freed(("dy", i))[1])

            dil_bias(0)
            for i in range(32):
                if i < 31:
                    dil_bias(i + 1)
                dil_out(i)
            for m in range(8):
                placed(("dt", m // 2))
                low_part(64 + m, hn_lo[:, m, :], hn[:, m, :], hn_hi[:, m, :])
            for m in range(8):
                b = take(("dw", m))
                stt(h[:, m, :], b[:, 0:T], mc(1, 2, m), h[:, m, :], MUL, ADD, *freed(("dw", m)))
            settle()
            scaled(8, (9, 4, hn, hn_lo, hn_hi))
            ffn(2)
            settle()
            norm_scale(9)
            for k in range(KT):
                stt(hn[:, k, :], h[:, k, :], col("final", k), rs[:, 2, :], MUL, MUL, sem("hn_ready"))
            for s in range(2):
                b = take(("fin", 2 * s))
                copy(outt[:, s, 0:512], b, *freed(("fin", 2 * s)))

        @block.scalar
        def _(act_):
            led = Ledger(act_, sem("act_own"))
            take0 = taker(act_)
            sum_jobs = sorted((n, job) for job, n in job_no.items() if job[0] == "ada")
            settle = led.settle

            def af(o, x, func=ACT.Identity, signal=None, value=None, **k):
                led.emit(nc.scalar.activation(o, x, func, **k), signal, value)

            def sums_before(job):
                while sum_jobs and sum_jobs[0][0] < job_no[job]:
                    aj = sum_jobs.pop(0)[1]
                    b = take0(aj)
                    if aj[1] >= 2:
                        act_.wait_ge(psum_ready, job_no["adc", aj[1] - 2] + 1)
                    af(sums[:, aj[1] % 2, :], b, ACT.Identity, *freed(aj))

            split_order = sorted(split_no, key=split_no.get)
            chunk_order = sorted(chunk_no, key=chunk_no.get)
            high_done = [0]

            def reach(job):
                sums_before(job)
                while high_done[0] < len(split_order):
                    n = high_done[0]
                    key = split_order[n]
                    before = [split_order[n - HI_SLOTS]] if n >= HI_SLOTS else []
                    earlier = before + chunk_order[max(0, chunk_no[key] - SLOTS):max(0, chunk_no[key] - SLOTS + 1)]
                    if any(used_at[x] >= job_no[job] for x in earlier) or job_no[job] <= job_no["ol", 1]:
                        break
                    if n == 0:
                        act_.wait_ge(psum_ready, job_no["ol", 1] + 1)
                    for x in before:
                        act_.wait_ge(*chunk_used[x])
                    act_.wait_ge(*chunk_landed[key])
                    raw, _, high = chunk_flat(key)
                    af(high, raw, ACT.Identity, sem("hi_ready"))
                    high_done[0] += 1

            def take(job):
                reach(job)
                return take0(job)

            def gone(job):
                reach(job)
                act_.wait_ge(*freed(job))

            def high_part(x_hi, x, **k):
                af(x_hi, x, ACT.Identity, sem("x_high"), **k)

            act_.wait_ge(sem("stage_clear"), 1)
            for r, m, src in pieces:
                act_.dma_start(stage[r % P:r % P + m, r // P, :], src).then_inc(stage_in, 16)
            act_.dma_start(dt_rows[0:8, :], a["s5_log_dt"].rearrange("l (j g) -> (l j) g", g=2)).then_inc(stage_in, 16)
            act_.dma_start(lora_w[0:64, :], a["rw_w2"][0]).then_inc(small_in, 16)
            act_.dma_start(lora_w[64:128, :], a["rw_a2"][0]).then_inc(small_in, 16)
            act_.dma_start(g2_w, a["rw_g2"][0]).then_inc(small_in, 16)
            act_.dma_start(cw2[:, 0, :], a["cmp_w2_k"][0]).then_inc(small_in, 16)
            act_.dma_start(cw2[:, 1, :], a["cmp_w2_k"][0]).then_inc(small_in, 16)
            act_.dma_start(cw2[:, 2, :], a["cmp_w2_v"][0]).then_inc(small_in, 16)
            act_.dma_start(wglu, a["s5_w_glu"][0].rearrange("(k p) n -> p k n", p=P)).then_inc(small_in, 16)
            for ri, nm in enumerate(("s5_b_re", "s5_b_im")):
                act_.dma_start(bfull[:, ri], a[nm][0].rearrange("(j g) n c -> (g n) j c", g=2)).then_inc(small_in, 16)
            for ri, nm in enumerate(("s5_c_re", "s5_c_im")):
                for x in range(2):
                    act_.dma_start(cdup[:, ri, :, HD * x:HD * x + HD],
                                   a[nm][0].rearrange("(f g) c n -> (g c) f n", f=2)).then_inc(small_in, 16)

            def squares(dst_, after=None):
                for f in range(2):
                    if after:
                        for k in range(4 * f, 4 * f + 4):
                            after(k)
                    af(dst_[:, 4 * f:4 * f + 4, :], h[:, 4 * f:4 * f + 4, :], ACT.Square, sem("squares"))

            def root(i):
                reach(("ms", i))
                act_.wait_ge(sem("rs_rec"), i + 1)
                af(rs[:, 2, :], rs[:, 1, :], ACT.Sqrt, sem("rs_root"))

            for j in range(4):
                act_.wait_ge(*freed(("xT", j)))
            squares(hn)
            for j in range(2):
                act_.wait_ge(*freed(("par", j)))
            af(cond[:, :], cols("c", 8), ACT.Tanh, sem("cond_tanh"), scale=0.5)
            af(s5v[:, 0, :], cols("log_dt", 8), ACT.Exp, sem("s5_dt"))
            root(0)
            act_.wait_ge(sem("s5_lr"), 1)
            af(s5v[:, 2, :], s5v[:, 1, :], ACT.Exp)
            act_.wait_ge(sem("s5_angle"), 1)
            af(s5v[:, 7, :], s5v[:, 5, :], ACT.Sin, sem("theta_ready"))
            af(s5v[:, 8, :], s5v[:, 6, :], ACT.Sin, sem("theta_ready"))
            act_.wait_ge(sem("derived"), 1)

            def rw(i):
                b = take(("rw", i))
                af(zs[:, i, :], b[:, 0:T], ACT.Identity, sem("shift_own"), scale=omm(i))

            for i in range(11):
                rw(i)
            for i in range(3):
                b = take(("q", i))
                af(qT[:, i, :], b[:, 0:T], ACT.Identity, *freed(("q", i)), scale=0.125)
            for s in range(2):
                b = take(("vtok", s))
                af(vtok[:, s, :], b[:, 0:T], ACT.Identity, *freed(("vtok", s)))
            for i in range(4):
                b = take(("kc", i))
                af(kcs[0:64, i, :], b[0:64, 0:T])
                af(kcs[64:128, i, 0:T - 1], b[64:128, 1:T], ACT.Identity, *freed(("kc", i)))
            for i in range(4):
                b = take(("kd", i))
                af(kd[:, i, :], b[:, 0:T], ACT.Identity, *freed(("kd", i)))
            b = take(("gtok",))
            af(gate[:, :, :].rearrange("p a b -> p (a b)"), b[:, 0:36], ACT.Tanh, *freed(("gtok",)), scale=0.5)
            for i in range(2):
                b = take(("u", i))
                af(uT[:, i, :], b[:, 0:T], ACT.Identity, *freed(("u", i)))
            act_.wait_ge(*freed(("rw", 9)))
            af(zs[0:64, 9, :], zs[0:64, 9, :], ACT.Tanh, sem("lora_tanh"))
            act_.wait_ge(*freed(("rw", 10)))
            af(zs[:, 10, :], zs[:, 10, :], ACT.Tanh, sem("lora_tanh"), scale=0.5)
            b = take(("cmph",))
            act_.wait_ge(sem("tables"), 1)
            af(peh[:, :], b[:, 60:62])
            settle()
            af(hid[:, 0:2, 0:NCMP], shaped(b[:, 0:30], 2, NCMP), ACT.Gelu_apprx_tanh, bias=peh[:, 0:1])
            af(hidv[:, :, :, 0:NCMP], shaped(b[:, 30:60], 2, NCMP).unsqueeze(2).broadcast_to([P, 2, 3, NCMP]), ACT.Gelu_apprx_tanh, *freed(("cmph",)),
               bias=peh[:, 1:2])
            for f in range(2):
                for j in range(4 * f, 4 * f + 4):
                    reach(("y5", j))
                    act_.wait_ge(*freed(("y5", j)))
                af(ygel[:, f, :], ygel[:, f, :], ACT.Gelu_apprx_tanh, sem("ygel_ready"))
            for m in range(2):
                b = take(("glu", 2 + m))
                af(s5g[:, m, :], b[:, 0:T], ACT.Tanh, *freed(("glu", 2 + m)), scale=0.5)
            b = take(("kcT",))
            af(kcT[:, :, :], shaped(b[:, 0:30], 2, NCMP), ACT.Identity, *freed(("kcT",)))
            for s in range(2):
                reach(("cs", 1, 1))
                act_.wait_ge(sem("cmp_shifted"), s + 1)
                af(csc[:, s, :, 0:NCMP], csc[:, s, :, 0:NCMP], ACT.Exp, sem("cmp_exp"))

            def nsa_exp(i):
                s, u = i // 6, i % 2
                nk = P * (s + 1)
                reach(("ns", i))
                act_.wait_ge(sem("nsa_max"), i + 1)
                for br in range(2):
                    af(nsc[:, u, br, 0:nk], nsc[:, u, br, 0:nk], ACT.Exp, sem("nsa_probs") if br else None,
                       bias=nst[:, i % 4, 0, br:br + 1], accum_out=nst[:, i % 4, 1, br:br + 1])

            def nsa_copy(i):
                s, u = i // 6, i % 2
                b = take(("np", i))
                if i >= 2:
                    act_.wait_ge(psum_ready, job_no["nv", i - 2] + 1)
                af(npt[:, u].rearrange("p (a b) c -> p a b c", a=2)[:, :, 0:s + 1, :],
                   shaped(b, 2, 2, P)[:, :, 0:s + 1, :], ACT.Identity, *freed(("np", i)))

            nsa_exp(0)
            for i in range(12):
                nsa_copy(i)
                if i < 11:
                    nsa_exp(i + 1)
            for c in range(3):
                b = take(("oT", c))
                high_part(hn_hi[:, 3 + c, :], b[:, 0:T])
                af(hn[:, 3 + c, :], b[:, 0:T], ACT.Identity, *freed(("oT", c)))
            for m in range(2):
                gone(("glu", m))
                high_part(hn_hi[:, 6 + m, :], hn[:, 6 + m, :])

            for c in range(3):
                b = take(("wp", c))
                af(W[0][:, c, :], b[:, 0:T], ACT.Tanh, *freed(("wp", c)), scale=0.5, bias=hw0(c))
            for c in range(3):
                b = take(("ap", c))
                af(W[3][:, c, :], b[:, 0:T], ACT.Tanh, *freed(("ap", c)), scale=0.5, bias=ha0(c))
            for c in range(3):
                b = take(("gp", c))
                af(W[10][:, c, :], b[:, 0:T], ACT.Identity, *freed(("gp", c)))
            reach(("gp", 2))
            act_.wait_ge(sem("logs"), 1)
            af(W[2], W[1], ACT.Exp, sem("exps"), scale=-1.0)
            af(W[0], W[0], ACT.Exp, sem("exps"))
            af(W[1], W[1], ACT.Exp, sem("exps"))
            reach(("kks", 2))
            act_.wait_ge(sem("kk_rec"), 1)
            af(W[5], W[5], ACT.Sqrt, sem("kk_root"))
            for s in range(2):
                for x in range(4):
                    b = take(("tk", s, x))
                    o = AM[:, :, 0, :] if x == 0 else tok4[:, x]
                    af(o, shaped(b[:, 0:384], 3, P), ACT.Identity, *freed(("tk", s, x)))
                for name, _l, _r, _a, dst_ in INV:
                    b = take((name, s, 1))
                    af(tmat(dst_)[:, 1], shaped(b[:, 0:384], 3, P), ACT.Identity, *freed((name, s, 1)))
                b = take(("au", s, 1))
                af(AU[:, :, :, HD:P], shaped(b[:, 0:384], 3, 2, HD), ACT.Identity, *freed(("au", s, 1)))
                b = take(("ol", s))
                af(zs[:, 0:3, s * P:s * P + P], shaped(b[:, 0:384], 3, P), ACT.Identity, *freed(("ol", s)))
            for c in range(3):
                reach(("gm", c))
                act_.wait_ge(*freed(("gm", c)))
                af(zs[:, 3 + c, :], zs[:, c, :], ACT.Square, sem("gn_sq"))
            reach(("gv", 2))
            act_.wait_ge(sem("gn_rec"), 1)
            af(zs[:, 6:9, :], zs[:, 6:9, :], ACT.Sqrt, sem("gn_root"))

            reach(("gv", 2))
            for c in range(3):
                act_.wait_ge(sem("mix_rw"), c + 1)
                high_part(hn_hi[:, c, :], hn[:, c, :])

            def out_squares(jobs, y):
                for k, job in enumerate(jobs):
                    b = take(job)
                    af(sqb[:, k, :], b[:, 0:T], ACT.Square, sem("squares") if k % 4 == 3 else None)
                    af(y[:, k, :], b[:, 0:T], ACT.Identity, *freed(job))

            def h_at(n):
                return lambda k: act_.wait_ge(sem("h_ready"), 8 * n + k + 1)

            def modulate(n, dst_, high, sh):
                act_.wait_ge(sem("gains"), 5)
                for k in range(KT):
                    act_.wait_ge(sem("tn_ready"), 8 * tn_round[n] + k + 1)
                    gain, shift = gsc[:, 8 * n + k:8 * n + k + 1], mod[:, sh + k:sh + k + 1]
                    af(dst_[:, k, :], tn[:, k, :], ACT.Identity, sem("hm_ready"), scale=gain, bias=shift)
                    high_part(high[:, k, :], tn[:, k, :], scale=gain, bias=shift)

            def ffn(f):
                W0, B0, n = (row0["conv_w"], row0["conv_b"], 44) if f == 0 else \
                    (row0["fconv_w"] + 66 * (f - 1), row0["fconv_b"] + 22 * (f - 1), 22)
                parts = ("ug", "uu") if f == 0 else ("ug",)

                def own(j):
                    for x, nm in enumerate(parts):
                        b = take((nm, f, j))
                        if j >= 2:
                            act_.wait_ge(*((sem("act_ready"), j - 1) if f == 0 else freed(("uu", f, j - 2))))
                        w, bc = W0 + 2 * n + 22 * x + j, B0 + 22 * x + j
                        af(ct[:, j % 2, x, :], b[:, 0:T], ACT.Identity, sem("conv_own"), scale=par[:, w:w + 1],
                           bias=par[:, bc:bc + 1])

                def gated(j):
                    act_.wait_ge(*freed(("ug", f, j)))
                    t = ct[:, j % 2, 0, :]
                    af(t, t, ACT.Gelu_apprx_tanh if f == 0 else ACT.Silu, sem("gate_act"))

                for j in range(FT):
                    own(j)
                    if j:
                        gated(j - 1)
                gated(FT - 1)

            out_squares([("out", m) for m in range(8)], yb)
            root(1)
            squares(hn, h_at(0))
            root(2)
            for k in range(KT):
                act_.wait_ge(sem("hn_ready"), 8 + k + 1)
                high_part(hn_hi[:, k, :], hn[:, k, :])
            ffn(0)
            out_squares([("down", 0, m) for m in range(8)], yb)
            root(3)
            for k in range(KT):
                act_.wait_ge(sem("h_ready"), 8 + k + 1)
                high_part(hn_hi[:, k, :], h[:, k, :])
            out_squares([("pl", m) for m in range(8)], eb)
            root(4)
            for m in range(8):
                b = take(("pg", m))
                af(yb[:, m, :], b[:, 0:T], ACT.Tanh, *freed(("pg", m)), scale=0.5)
            squares(hn, h_at(2))
            root(5)
            modulate(0, hn, hn_hi, 0)
            for m in range(8):
                b = take(("pi", m))
                af(pu[:, m, :], b[:, 0:T], ACT.Identity, *freed(("pi", m)))
            for m in range(8):
                b = take(("pp", m))
                high_part(hn_hi[:, m, :], b[:, 0:T], scale=col("pool_scale", m))
                af(eT[:, m, :], b[:, 0:T], ACT.Identity, *freed(("pp", m)), scale=col("pool_scale", m))
            squares(hn, lambda k: gone(("po", k)))
            root(6)
            modulate(1, hn, hn_hi, 24)
            ffn(1)
            squares(hn, lambda k: gone(("down", 1, k)))
            root(7)
            modulate(2, hn, hn_hi, 96)
            modulate(3, hn2, hn2_hi, 48)

            def projected(c):
                u = c % 2
                for br in range(3):
                    for i in range(2):
                        b = take(("dk", c, br, i))
                        yield af(dk[:, u, 2 * br + i, :], b[:, 0:T], ACT.Identity, *freed(("dk", c, br, i)))
                for br in range(3):
                    for s in range(2):
                        b = take(("dv", c, br, s))
                        yield af(dv[:, u, s, br, :], b[:, 0:T], ACT.Identity, *freed(("dv", c, br, s)))
                for br in range(3):
                    for i in range(2):
                        b = take(("dq", c, br, i))
                        yield af(dq[:, u, 2 * br + i, :], b[:, 0:T], ACT.Identity, *freed(("dq", c, br, i)),
                                 scale=0.125)

            for _ in projected(0):
                pass

            def dil_exp(i):
                s, u = i % 2, i % 2
                n = 3 * P * (s + 1)
                reach(("db", i))
                act_.wait_ge(sem("dil_max"), i + 1)
                af(dsc[:, u, 0:n], dsc[:, u, 0:n], ACT.Exp, sem("dil_probs"), bias=dst[:, i % 4, 0:1],
                   accum_out=dst[:, i % 4, 1:2])

            dil_exp(0)
            for i in range(32):
                b = take(("dp", i, 0))
                if i >= 2:
                    act_.wait_ge(psum_ready, job_no["dy", i - 2] + 1)
                af(dpt[:, i % 2, 0:3, :], shaped(b[:, 0:384], 3, P), ACT.Identity, *freed(("dp", i, 0)))
                if i < 31:
                    dil_exp(i + 1)
                if i % 8 == 0:
                    coming = projected(i // 8 + 1) if i < 24 else iter(())
                for _ in range(proj_share(i)):
                    next(coming, None)
            for j in range(4):
                b = take(("dt", j))
                for k in range(2):
                    high_part(hn_hi[:, 2 * j + k, :], b[:, k * T:k * T + T])
                af(hn[:, 2 * j:2 * j + 2, :], shaped(b, 2, T), ACT.Identity, *freed(("dt", j)))
            squares(hn2, lambda k: gone(("dw", k)))
            root(8)
            modulate(4, hn, hn_hi, 72)
            ffn(2)
            squares(hn, lambda k: gone(("down", 2, k)))
            root(9)
            for s in range(2):
                b = take(("fin", 2 * s + 1))
                af(outt[:, s, 512:1024], b, ACT.Identity, *freed(("fin", 2 * s + 1)))


_INS = ['x', 'p', 'pre_mix_norm', 'post_mix_norm', 'pre_ffn_norm', 'post_ffn_norm', 'w_in', 'w_out', 'shift_mu',
        'rw_w0', 'rw_w2', 'rw_a0', 'rw_a2', 'rw_g2', 'rw_k_k', 'rw_k_a', 'rw_r_k', 'rw_gn_w', 'rw_gn_b', 'cmp_pe_k',
        'cmp_pe_v', 'cmp_w1_k', 'cmp_w2_k', 'cmp_w1_v', 'cmp_w2_v', 's5_lam_re', 's5_lam_im', 's5_log_dt', 's5_b_re',
        's5_b_im', 's5_c_re', 's5_c_im', 's5_d', 's5_w_glu', 'w_up', 'conv_w', 'conv_b', 'w_down', 'w_ple', 'ple_norm',
        'w_ple_gate', 'c_2', 'ada_w_2', 'ada_b_2', 'norm1_g_2', 'norm2_g_2', 'pool_w_in_2', 'pool_w_grp_2',
        'pool_scale_2', 'pool_w_out_2', 'kv_norm_g_2', 'kv_ada_w_2', 'kv_ada_b_2', 'w_kv_2', 'attn_w_q_2',
        'attn_w_o_2', 'ffn_w_up_2', 'ffn_conv_w_2', 'ffn_conv_b_2', 'ffn_w_down_2', 'final_g_2']


def kernel(**inputs):
    import numpy as _np
    import concourse.bacc as _bacc
    from concourse import mybir as _mybir
    from concourse.bass_utils import run_bass_kernel_spmd as _run

    nc = _bacc.Bacc("TRN2", target_bir_lowering=False, num_devices=1)
    arrays, args = {}, {}
    for name in _INS:
        a = _np.ascontiguousarray(inputs[name])
        arrays[f"in_{name}_dram"] = a
        args[name] = nc.dram_tensor(f"in_{name}_dram", a.shape, _mybir.dt.from_np(a.dtype), kind="ExternalInput").ap()
    out = nc.dram_tensor("out_0_dram", (1, T, D), _mybir.dt.float32, kind="ExternalOutput").ap()
    two_block_kernel(nc, args, out)
    r = _run(nc, [arrays], core_ids=[0])
    return r.results[0]["out_0_dram"]
```

```python
import math
from contextlib import ExitStack

import concourse.bass as bass
from concourse import mybir

F32 = mybir.dt.float32
F32R = mybir.dt.float32r
ALU = mybir.AluOpType
ACT = mybir.ActivationFunctionType
AX = mybir.AxisListType

P = 128
T = 256
D = 1024
KT = D // P
FF = 2816
FT = FF // P
HD = 64
BANKS = 8
SLOTS = 6
SLOT = 2048
HI_SLOTS = 4
FAR = 1.0e32
NCMP = 15
EPS = 1e-6
GN_EPS = 64e-5
MAGIC = 12582912.0
RW_TILES = 11
Q_COL, KC_COL, VC_COL, KS_COL, VS_COL, KW_COL, VW_COL, GATE_COL, U_COL = (
    1408, 1792, 1920, 2048, 2176, 2304, 2432, 2560, 2578)
N_IN = 2834


def nsa_slopes(n):
    def pow2(m):
        return [2.0 ** (-8.0 / m * (i + 1)) for i in range(m)]
    c = 2 ** math.floor(math.log2(n))
    return pow2(c) + pow2(2 * c)[0::2][: n - c]


def dilated_slopes(n):
    def pow2(m):
        start = 2.0 ** (-(2.0 ** -(math.log2(m) - 3)))
        return [start ** (i + 1) for i in range(m)]
    c = 2 ** math.floor(math.log2(n))
    s = pow2(n) if c == n else pow2(c) + pow2(2 * c)[0::2][: n - c]
    return sorted(s, reverse=True)


class Ledger:

    def __init__(self, eng, own):
        self.eng, self.own, self.count, self.open = eng, own, {}, {}

    def emit(self, ins, signal=None, value=None):
        signal = signal or self.own
        ins.then_inc(signal, 1)
        self.count[signal.name] = value or self.count.get(signal.name, 0) + 1
        self.open[signal.name] = (signal, self.count[signal.name])

    def settle(self):
        for signal, value in self.open.values():
            self.eng.wait_ge(signal, value)
        self.open = {}


def two_block_kernel(nc, a, out):
    ctx = ExitStack()
    with ctx:
        sems = {}

        def sem(name):
            if name not in sems:
                sems[name] = ctx.enter_context(nc.semaphore(name))
            return sems[name]

        def sb(name, cols, rows=P):
            return ctx.enter_context(nc.sbuf_tensor(name, [rows, cols], F32))

        def shaped(flat, *dims):
            names = "abcdef"[:len(dims)]
            return flat.rearrange(f"p ({' '.join(names)}) -> p {' '.join(names)}", **dict(zip(names, dims)))

        ident = sb("ident", P)
        ones_mean = sb("ones_mean", P)
        head_ones = sb("head_ones", P)
        head_mean = sb("head_mean", P)
        masks = shaped(sb("masks", 6 * P), 6, P)
        U8, L8M, L16M, L32M, U32S, U32I = (masks[:, i, :] for i in range(6))
        scan_keep = sb("scan_keep", T)
        dist = shaped(sb("dist", 2 * T), 2, T)
        late = sb("late", 10 * T)
        bdist = shaped(late[:, 0:6 * T], 3, 2, T)
        inv_count = shaped(late[:, 6 * T:10 * T], 4, T)
        sums = shaped(late[:, 0:1024], 2, 512)
        cond_wide = shaped(late[:, 1024:1280], KT, 32)
        cdist = shaped(sb("cdist", 30), 2, NCMP)
        cbias = shaped(sb("cbias", 180), 2, 6, NCMP)
        block3 = sb("block3", 3)
        block2 = sb("block2", 2)
        row_ok = sb("row_ok", 2)
        one_each = sb("one_each", 1)
        par = sb("par", 6 * P + 8)
        dt_rows = sb("dt_rows", 2)
        dt_wide = sb("dt_wide", P)
        drv = sb("drv", 32)
        cond = sb("cond", KT)
        mod = sb("mod", 112)
        gsc = sb("gsc", 40)
        pT = shaped(sb("pT", 2 * T), 2, T)
        h = shaped(sb("h", KT * T), KT, T)
        rs = shaped(sb("rs", 2 * T), 2, T)
        HN, ARENA0, ARENA = SLOTS * SLOT, SLOTS * SLOT + 2 * KT * T, 27520

        def place(name, off, dtype, *dims):
            with ExitStack() as brief:
                if off:
                    brief.enter_context(nc.sbuf_tensor(name + "_offset", [P, off], F32))
                flat = brief.enter_context(nc.sbuf_tensor(name, [P, math.prod(dims)], dtype))
            return shaped(flat, *dims)

        ring = place("ring", 0, F32, SLOTS, SLOT)
        ring_lo = place("ring_lo", 0, F32R, SLOTS, SLOT)
        hn = place("hn", HN, F32, KT, T)
        hn_lo = place("hn_lo", HN, F32R, KT, T)
        hn_hi = place("hn_hi", HN + KT * T, F32R, KT, T)
        arena = place("arena", ARENA0, F32, 1, ARENA)[:, 0, :]

        def at(off, *dims):
            n = math.prod(dims)
            assert off + n <= ARENA, (off, dims)
            flat = arena[:, off:off + n]
            return flat if len(dims) == 1 else shaped(flat, *dims)

        def parts(name, off, *dims):
            assert off + math.prod(dims) <= ARENA
            return place(name, ARENA0 + off, F32R, *dims)

        banks = ctx.enter_context(nc.psum_tensor("banks", [P, BANKS, 512], F32))

        xtok = at(0, 2, D)
        stage = at(2048, 6, P)
        ptok = at(2816, 2, T)
        zs = at(0, RW_TILES, T)
        kcs = at(2816, 4, T)
        kd = at(3840, 4, T)
        qT = at(4864, 3, T)
        vtok = at(5632, 2, T)
        gate = at(6144, 2, 18)
        uT = at(6208, 2, T)
        lora_w = at(6720, 384)
        g2_w = at(7104, 384)
        cw2 = at(7488, 3, HD)
        M0 = 7680
        tabC, tabS = at(M0, 8, T), at(M0 + 2048, 8, T)
        BT = at(M0 + 4096, 2, 2, P)
        CT = at(M0 + 4608, 2, 2, P)
        wglu = at(M0 + 5120, 2, 512)
        s5w = at(M0 + 6144, 2, 5, 2, T)
        s5v = at(M0 + 11264, 24, 8)
        bfull = at(M0 + 11456, 2, 8, 16)
        bmul = at(M0 + 11712, 2, 8, 16)
        bdup = at(M0 + 11968, 2, 8, 2, 16)
        cdup = at(M0 + 12480, 2, 2, P)
        ygel = at(M0 + 12992, 2, T)
        s5g = at(M0 + 13504, 2, T)
        powr = at(M0 + 14016, 2, 8)
        ptmp = at(M0 + 14032, 2, 8, P)
        assert M0 + 16080 <= ARENA
        nsc = at(M0 + 17664, 2, 2, T)
        npt = at(M0 + 18688, 2, 4, P)
        NB = M0 + 15312
        otok = at(M0 + 14480, 2, 384)
        chid = at(NB, P)
        hid = at(NB + 128, 2, 32)
        kcT = at(NB + 192, 2, NCMP)
        vbd = at(NB + 224, 2, 3, HD)
        csc = at(NB + 992, 2, 6, 32)
        cst = at(NB + 1376, 2, 4, 6)
        nst = at(NB + 1424, 4, 4, 2)
        cpt = at(M0 + 14032, 2, P)
        hidv = at(M0 + 14288, 2, 3, 32)
        W = [at(M0 + 768 * i, 3, T) for i in range(12)]
        tok4 = at(M0 + 9216, 4, 3, P)
        AM = at(M0 + 10752, 3, 2, P)
        AU = at(M0 + 11520, 3, 2, P)
        KEEP = [at(M0 + 12288 + 768 * i, 2, 3, P) for i in range(4)]
        TM = [at(M0 + 768 * i, 2, 3, P) for i in range(6)] + [at(M0 + 15360 + 768 * i, 2, 3, P) for i in range(3)]
        EB, HB = at(M0, 4, 3, P), at(M0 + 1536, 4, 3, P)
        ST = at(2816, 7, 3, P)
        Pend = at(5632, 3, 8)
        assert M0 + 17664 <= ARENA
        HI0 = ARENA - HI_SLOTS * SLOT
        ring_hi = parts("ring_hi", HI0, HI_SLOTS, SLOT)
        act = at(0, FT, T)
        act_lo, act_hi = parts("act_lo", 0, FT, T), parts("act_hi", 13312, FT, T)
        early_hi = parts("early_hi", M0 + 6144, 2, SLOT)
        eT_lo = parts("eT_lo", 8192, KT, T)
        assert 13312 + FT * T <= HI0
        ct = at(5632, 2, 2, T)
        eT = at(8192, KT, T)
        sqb, yb, eb = eT, at(10240, KT, T), at(0, KT, T)
        pu = at(10240, KT, T)
        pw = at(12288, 2, 2, T)
        dk, dv, dq = at(0, 2, 6, T), at(3072, 2, 2, 3, T), at(6144, 2, 6, T)
        dsc = at(9216, 2, 3 * T)
        dpt = at(10752, 2, 6, P)
        dotok = at(12288, 2, D)
        dst = at(14336, 4, 4)
        hn2 = at(14400, KT, T)
        hn2_lo, hn2_hi = parts("hn2_lo", 14400, KT, T), parts("hn2_hi", 16448, KT, T)
        assert 18496 <= HI0
        outt = at(0, 2, D)
        dint = at(12288, 2, T)

        def rows(x, pat, **k):
            return x.rearrange(pat, **k)
        vecs = [("pre_mix", rows(a["pre_mix_norm"], "l (j p) -> (l j) p", p=P)),
                ("post_mix", rows(a["post_mix_norm"], "l (j p) -> (l j) p", p=P)),
                ("pre_ffn", rows(a["pre_ffn_norm"], "l (j p) -> (l j) p", p=P)),
                ("post_ffn", rows(a["post_ffn_norm"], "l (j p) -> (l j) p", p=P)),
                ("ple_norm", rows(a["ple_norm"], "l (j p) -> (l j) p", p=P)),
                ("norm1", rows(a["norm1_g_2"], "l (j p) -> (l j) p", p=P)),
                ("norm2", rows(a["norm2_g_2"], "l (j p) -> (l j) p", p=P)),
                ("kv_norm", rows(a["kv_norm_g_2"], "(j p) -> j p", p=P)),
                ("final", rows(a["final_g_2"], "(j p) -> j p", p=P)),
                ("c", rows(a["c_2"], "l (j p) -> (l j) p", p=P)),
                ("pool_scale", rows(a["pool_scale_2"], "l (j p) -> (l j) p", p=P)),
                ("mu", rows(a["shift_mu"], "l (j p) -> (l j) p", p=P)),
                ("w0", rows(a["rw_w0"], "l (j p) -> (l j) p", p=P)),
                ("a0", rows(a["rw_a0"], "l (j p) -> (l j) p", p=P)),
                ("k_k", rows(a["rw_k_k"], "l (j p) -> (l j) p", p=P)),
                ("k_a", rows(a["rw_k_a"], "l (j p) -> (l j) p", p=P)),
                ("r_k", rows(a["rw_r_k"], "l (j p) -> (l j) p", p=P)),
                ("gn_w", rows(a["rw_gn_w"], "l (j p) -> (l j) p", p=P)),
                ("gn_b", rows(a["rw_gn_b"], "l (j p) -> (l j) p", p=P)),
                ("pe_k", rows(a["cmp_pe_k"], "l (j q) d -> (l j) (q d)", q=2)),
                ("pe_v", rows(a["cmp_pe_v"], "l (j q) d -> (l j) (q d)", q=2)),
                ("s5_d", rows(a["s5_d"], "l (j p) -> (l j) p", p=P)),
                ("lam_re", rows(a["s5_lam_re"], "l (j g) n -> (l j) (g n)", g=2)),
                ("lam_im", rows(a["s5_lam_im"], "l (j g) n -> (l j) (g n)", g=2)),
                ("ada_b", rows(a["ada_b_2"], "l (j p) -> (l j) p", p=P)),
                ("kv_ada_b", rows(a["kv_ada_b_2"], "(j p) -> j p", p=P)),
                ("conv_w", rows(a["conv_w"], "l w (j p) -> (l w j) p", p=P)),
                ("conv_b", rows(a["conv_b"], "l (j p) -> (l j) p", p=P)),
                ("fconv_w", rows(a["ffn_conv_w_2"], "l w (j p) -> (l w j) p", p=P)),
                ("fconv_b", rows(a["ffn_conv_b_2"], "l (j p) -> (l j) p", p=P))]
        row0, n = {}, 0
        for name, src in vecs:
            row0[name] = n
            n += src.shape[0]
        assert n <= 6 * P
        row0["log_dt"] = 6 * P

        def col(name, i=0):
            return par[:, row0[name] + i:row0[name] + i + 1]

        def cols(name, n, i=0):
            return par[:, row0[name] + i:row0[name] + i + n]

        omm, hw0, ha0, omka = (lambda i: drv[:, i:i + 1]), (lambda i: drv[:, 11 + i:12 + i]), \
            (lambda i: drv[:, 14 + i:15 + i]), (lambda i: drv[:, 17 + i:18 + i])
        eps_col = drv[:, 20:21]

        def mc(layer, which, i):
            j = 48 * layer + 8 * which + i
            return mod[:, j:j + 1]

        def kmaj(w, c0, c1, k0=0, k1=KT):
            return w.rearrange("(k p) n -> p k n", p=P)[:, k0:k1, c0:c1]

        def k256(w, i, k0=0, k1=KT):
            return [kmaj(w, 256 * i, 256 * i + 256, k0, k1)]

        chunk_src, early = {}, []
        w_in, w_out = a["w_in"][0], a["w_out"][0]
        for i in range(7):
            chunk_src["in", i] = k256(w_in, i)
        chunk_src["in", 7] = [kmaj(w_in, VS_COL, KW_COL), kmaj(w_in, VW_COL, GATE_COL)]
        for i, (c0, c1) in enumerate(((KC_COL, KC_COL + HD), (VC_COL, VC_COL + HD), (KS_COL, KS_COL + HD),
                                      (KW_COL, KW_COL + HD))):
            chunk_src["keys", i] = [kmaj(w_in, c, c + HD) for c in (c0, c0, c1, c1)]
        early = [("in", i) for i in range(8)] + [("keys", i) for i in range(4)] + [("gate", 0), ("u", 0)]
        chunk_src["gate", 0] = [kmaj(w_in, GATE_COL, U_COL)]
        chunk_src["u", 0] = [kmaj(w_in, U_COL, N_IN)]
        for i in range(28):
            w = a["ada_w_2"][i // 12] if i < 24 else a["kv_ada_w_2"]
            c = 512 * (i % 12 if i < 24 else i - 24)
            for f in range(2):
                chunk_src["ada", i, f] = [kmaj(w, c, c + 512, 4 * f, 4 * f + 4)]
        for f, nm in enumerate(("cmp_w1_k", "cmp_w1_v")):
            chunk_src["cmp", f] = [a[nm][0].rearrange("(k p) n -> p k n", p=P)]
        chunk_src["ple", 0] = [a["w_ple"][0].rearrange("(k p) n -> p k n", p=P)]
        chunk_src["pgrp", 0] = [a["pool_w_grp_2"][0].rearrange("g (k p) n -> p (g k) n", p=P)]
        split = set()
        for nm, w, n in (("out", w_out, 4), ("pin", a["pool_w_in_2"][0], 4), ("pout", a["pool_w_out_2"][0], 4),
                         ("pleg", a["w_ple_gate"][0], 4), ("kv", a["w_kv_2"], 24), ("dq", a["attn_w_q_2"][0], 12),
                         ("do", a["attn_w_o_2"][0], 4)):
            for i in range(n):
                chunk_src[nm, i] = k256(w, i)
                split.add((nm, i))
        ffn_up = [a["w_up"][0], a["ffn_w_up_2"][0], a["ffn_w_up_2"][1]]
        ffn_down = [a["w_down"][0], a["ffn_w_down_2"][0], a["ffn_w_down_2"][1]]
        for f in range(3):
            for i in range(11):
                for x, nm in enumerate(("ug", "uu")):
                    chunk_src[nm, f, i] = k256(ffn_up[f], 11 * x + i)
                    split.add((nm, f, i))
            for m in range(4):
                for i in range(3):
                    chunk_src["down", f, m, i] = k256(ffn_down[f], m, 8 * i, min(8 * i + 8, FT))
                    split.add(("down", f, m, i))
        chunk_no, split_no = {}, {}
        chunk_landed, chunk_used = {}, {}
        used_at = {}

        def chunk_flat(key):
            n = sum(src.shape[1] * src.shape[2] for src in chunk_src[key])
            s = chunk_no[key] % SLOTS
            if key in early:
                return ring[:, s, 0:n], ring_lo[:, s, 0:n], early_hi[:, early.index(key) % 2, 0:n]
            return (ring[:, s, 0:n], ring_lo[:, s, 0:n],
                    ring_hi[:, split_no[key] % HI_SLOTS, 0:n] if key in split_no else None)

        def chunk_view(key):
            flat = chunk_flat(key)[0]
            if len(chunk_src[key]) > 1:
                n = chunk_src[key][0].shape[2]
                whole = shaped(flat, KT, 256 // n, n)
                return [whole[:, :, i, :] for i in range(256 // n)]
            return [shaped(flat, *chunk_src[key][0].shape[1:])]

        job_no = {}
        psum_ready = sem("psum_ready")
        bank_free = [sem(f"bank_free{b}") for b in range(BANKS)]

        def bank_of(job):
            return banks[:, job_no[job] % BANKS, :]

        def freed(job):
            return bank_free[job_no[job] % BANKS], job_no[job] // BANKS + 1

        pieces = []
        for name, src in vecs:
            r, n, k = row0[name], src.shape[0], 0
            while k < n:
                m = min(n - k, P - (r + k) % P)
                pieces.append((r + k, m, src[k:k + m, :]))
                k += m
        soon = [x for x in pieces if x[0] + x[1] <= 3 * P]
        later = [x for x in pieces if x not in soon]
        assert row0["conv_w"] <= 3 * P
        soon_total, later_total = 16 * len(soon), 16 * len(later) + 16

        def proj_share(i):
            return (3, 3, 3, 3, 2, 2, 2, 0)[i % 8]

        conv_base = [0, 2 * FT, 3 * FT]

        landed = [sem(f"slot_landed{s}") for s in range(SLOTS)]
        setup_in, small_in = sem("setup_in"), sem("small_in")

        block = ctx.enter_context(nc.Block())


        INV = [("L2", 0, 1, None, 4), ("N2", 1, 0, None, 5), ("L4", 5, 4, None, 6), ("Y1", 4, 7, 7, 8),
               ("T8", 6, 8, 8, 0), ("T8t", 0, None, None, 1), ("Ya", 2, 0, None, 4), ("T16", 1, 4, 0, 5),
               ("T16t", 5, None, None, 6), ("Yb", 3, 5, None, 7), ("T32", 6, 7, 5, 9)]

        def tmat(i):
            return KEEP[3] if i == 9 else TM[i]

        @block.tensor
        def _(pe):
            landed_count = [0] * SLOTS
            current = [None]

            def opened(job):
                n = job_no[job] = len(job_no)
                if n >= BANKS:
                    pe.wait_ge(bank_free[n % BANKS], n // BANKS)
                current[0] = job
                return banks[:, n % BANKS, :]

            def opened_beside(job):
                before = current[0]
                b = opened(job)
                current[0] = before
                return b

            def chunk(key):
                if key not in chunk_no:
                    slot = len(chunk_no) % SLOTS
                    chunk_no[key] = len(chunk_no)
                    landed_count[slot] += 16 * len(chunk_src[key])
                    chunk_landed[key] = (landed[slot], landed_count[slot])
                    if key in early:
                        pe.wait_ge(sem("early_lo"), early.index(key) + 1)
                    elif key in split:
                        split_no[key] = len(split_no)
                        pe.wait_ge(sem("lo_ready"), split_no[key] + 1)
                    else:
                        pe.wait_ge(*chunk_landed[key])
                used_at[key] = job_no[current[0]]
                chunk_used[key] = (psum_ready, used_at[key] + 1)
                if key in split or key in early:
                    k = chunk_src[key][0].shape[1]
                    n = chunk_flat(key)[0].shape[1] // k
                    return [shaped(part, k, n) for part in chunk_flat(key)[1:]]
                return chunk_view(key)

            def copied(job):
                pe.wait_ge(*freed(job))

            def mm(o, l, r, start=True, stop=True, **k):
                return nc.tensor.matmul(o, l, r, start=start, stop=stop, **k)

            def close(ins):
                ins.then_inc(psum_ready, 1)

            def turn(job, pieces):
                b, off = opened(job), 0
                for src in pieces:
                    n, m = src.shape[0], src.shape[1]
                    last = nc.tensor.transpose(b[0:m, off:off + n], src, ident[0:n, 0:n])
                    off += n
                close(last)

            def tile(job, key, c0, rhs, part=0, kts=KT, m=P, first=None, n=T):
                b = opened(job)
                w = chunk(key)[part]
                for k in range(kts):
                    if first:
                        first(k)
                    l = w[:, k, c0:c0 + m]
                    last = mm(b[0:m, 0:n], l, rhs[:, k, :], start=(k == 0), stop=(k == kts - 1))
                close(last)

            def three_passes(o, w, x, start, stop):
                (w_lo, w_hi), (x_lo, x_hi) = w, x
                mm(o, w_hi, x_hi, start=start, stop=False)
                mm(o, w_hi, x_lo, start=False, stop=False)
                return mm(o, w_lo, x_hi, start=False, stop=stop)

            def split_tile(job, key, c0, x):
                b = opened(job)
                w = chunk(key)
                for k in range(KT):
                    last = three_passes(b[:, 0:T], [v[:, k, c0:c0 + P] for v in w], [v[:, k, :] for v in x],
                                        k == 0, k == KT - 1)
                close(last)

            def split_rows(job, outs, key, x):
                b = opened(job)
                w = chunk(key)
                for cols_, cut in outs:
                    for k in range(KT):
                        last = three_passes(b[:, cols_], [v[:, k, cut] for v in x], [v[:, k, :] for v in w],
                                            k == 0, k == KT - 1)
                close(last)

            def first_tiles(rnd, jobs, x, ks=tuple(range(KT))):
                low, high = x
                todo = []
                for job, key, c0 in jobs:
                    b = opened(job)[:, 0:T]
                    todo.append((b, [v[:, :, c0:c0 + P] for v in chunk(key)]))
                for t, (b, (w_lo, w_hi)) in enumerate(todo):
                    for n, k in enumerate(ks):
                        if t == 0:
                            pe.wait_ge(sem("x_high"), KT * (rnd + 1) + n + 1)
                        mm(b, w_hi[:, k, :], high[:, k, :], start=(n == 0), stop=False)
                        mm(b, w_lo[:, k, :], high[:, k, :], start=False, stop=False)
                for t, (b, (_, w_hi)) in enumerate(todo):
                    for n, k in enumerate(ks):
                        if t == 0:
                            pe.wait_ge(sem("x_split"), KT * (rnd + 1) + n + 1)
                        last = mm(b, w_hi[:, k, :], low[:, k, :], start=False, stop=(n == KT - 1))
                    close(last)

            def mean_square_of(i, b, sq, ks):
                for k in ks:
                    if k % 2 == 0:
                        pe.wait_ge(sem("squares"), 4 * i + k // 2 + 1)
                    last = mm(b[:, 0:T], ones_mean[:, :], sq[:, k, :], start=(k == 0), stop=(k == KT - 1))
                if ks[-1] == KT - 1:
                    close(last)

            def projection(rnd, name, key, x, ms=None, ks=tuple(range(KT))):
                tiles = [((name, m), (key, m // 2), 128 * (m % 2)) for m in range(8)]
                first_tiles(rnd, tiles[:4], x, ks)
                for t in tiles[4:7]:
                    split_tile(*t, x)
                if ms is None:
                    split_tile(*tiles[7], x)
                    return
                b = opened(tiles[7][0])
                b_ms = opened_beside(("ms", ms[0]))
                mean_square_of(ms[0], b_ms, ms[1], (0, 1, 2, 3))
                w = chunk(tiles[7][1])
                for k in range(KT):
                    last = three_passes(b[:, 0:T], [v[:, k, 128:256] for v in w], [v[:, k, :] for v in x],
                                        k == 0, k == KT - 1)
                close(last)
                mean_square_of(ms[0], b_ms, ms[1], (4, 5, 6, 7))

            def mean_square(i, sq):
                mean_square_of(i, opened(("ms", i)), sq, tuple(range(KT)))

            ada_left = list(range(28))

            ada_open = []

            def ada_columns():
                if ada_open:
                    i = ada_open.pop()
                    copied(("ada", i))
                    b = opened(("adc", i))
                    for m in range(4):
                        last = mm(b[:, m:m + 1], sums[:, i % 2, m * P:m * P + P], one_each[:, :])
                    close(last)

            def ada(n=1):
                for _ in range(n):
                    if ada_left:
                        i = ada_left.pop(0)
                        if i == 0:
                            pe.wait_ge(sem("cond_ready"), 1)
                        b = opened(("ada", i))
                        for k in range(KT):
                            w = chunk(("ada", i, k // 4))[0]
                            q = 32 * (k % 4)
                            last = mm(b[q:q + 32, :], cond_wide[:, k, :], w[:, k % 4, :], start=(k < 4), stop=(k >= 4),
                                      tile_position=(0, q))
                        close(last)
                        ada_columns()
                        ada_open.append(i)

            pe.wait_ge(sem("ident_ready"), 2)
            pe.wait_ge(setup_in, 32)
            for j in range(4):
                turn(("xT", j), [xtok[:, s, (2 * j + k) * P:(2 * j + k + 1) * P] for k in range(2) for s in range(2)])
            pe.wait_ge(sem("mean_ready"), 1)
            mean_square(0, hn)
            pe.wait_ge(sem("stage_clear"), 2)
            pe.wait_ge(sem("soon_in"), soon_total)
            turn(("par", 0), [stage[:, i, :] for i in range(3)])
            xz = (hn_lo, hn_hi)
            zt = [(("rw", i) if i < 11 else ("q", i - 11), ("in", i // 2), 128 * (i % 2)) for i in range(14)]
            first_tiles(-1, zt[:2], xz)
            pe.wait_ge(sem("later_in"), later_total)
            pe.wait_ge(sem("dt_spread"), 1)
            turn(("par", 1), [stage[:, 3 + i, :] for i in range(3)] + [dt_wide[0:8, :]])
            turn(("pT",), [ptok[:, s, k * P:k * P + P] for k in range(2) for s in range(2)])
            for t in zt[2:]:
                split_tile(*t, xz)
            for s in range(2):
                split_rows(("vtok", s), [(slice(0, T), slice(s * P, s * P + P))], ("in", 7), xz)
            for x, nm in enumerate(("kc", "kd")):
                for i in range(4):
                    split_tile((nm, i), ("keys", 2 * x + i // 2), 128 * (i % 2), xz)
            split_rows(("gtok",), [(slice(s * 18, s * 18 + 18), slice(s * P, s * P + P)) for s in range(2)],
                       ("gate", 0), xz)
            for i in range(2):
                split_tile(("u", i), ("u", 0), 128 * i, xz)

            pe.wait_ge(sem("consts"), 1)
            pe.wait_ge(sem("b_ready"), 1)
            turn(("bT",), [bdup[:, r, 4 * f:4 * f + 4, :, :].rearrange("p a b c -> p (a b c)")
                           for r in range(2) for f in range(2)])
            turn(("cT",), [cdup[:, r, f, :] for r in range(2) for f in range(2)])
            copied(("bT",))
            copied(("cT",))
            for i in range(2):
                copied(("u", i))

            def bu(j):
                b, q = opened(("bu", j)), 32 * (j % 4)
                for r in range(2):
                    last = mm(b[:, r * T:r * T + T], BT[q:q + 32, r, j // 4, :], uT[q:q + 32, j // 4, :])
                close(last)

            def y5(j):
                b, q, r2 = opened(("y5", j)), 32 * (j % 4), j % 2
                pe.wait_ge(sem("s5_states"), j + 1)
                for r in range(2):
                    last = mm(b[q:q + 32, 0:T], CT[:, r, j // 4, q:q + 32], s5w[:, r2, 4, r, :],
                              start=(r == 0), stop=(r == 1))
                close(last)

            def compressed_hidden():
                b = opened(("cmq",))
                w1 = [chunk(("cmp", v))[0] for v in range(2)]
                for i in range(4):
                    copied(("kc", i))
                for lp in range(16):
                    for x in (0, 1):
                        for i in range(4):
                            v, g = i // 2, i % 2
                            pos = col("pe_v" if v else "pe_k", lp).broadcast_to([P, NCMP])
                            last = mm(b[32 * i:32 * i + NCMP, 0:P], pos if x else kcs[:, 2 * v + g, 2 * lp:2 * lp + 225:16],
                                      w1[v][:, lp, :], start=(lp == x == 0), stop=(lp == 15 and x == 1),
                                      tile_position=(0, 32 * i))
                close(last)

            def s5_gate():
                pe.wait_ge(sem("ygel_ready"), 2)
                for m in range(4):
                    b = opened(("glu", m))
                    for k in range(2):
                        last = mm(b[:, 0:T], wglu[:, k, m * P:m * P + P], ygel[:, k, :], start=(k == 0), stop=(k == 1))
                    close(last)

            def compressed_keys():
                copied(("cmph",))
                b = opened(("kcT",))
                close(mm(b[:, 0:30], cw2[:, 0:2, :].rearrange("p a b -> p (a b)"), hid[:, 0:2, 0:NCMP]))
                b = opened(("vc",))
                for g in range(2):
                    last = mm(b[0:96, g * HD:g * HD + HD], hidv[:, g, :, :].rearrange("p a b -> p (a b)"), cw2[:, 2, :])
                close(last)

            def compressed_scores():
                copied(("kcT",))
                for i in range(3):
                    copied(("q", i))
                for s in range(2):
                    for x in range(2):
                        b = opened(("cs", s, x))
                        for i in range(3):
                            hh = x + 2 * i
                            last = mm(b[:, 32 * i:32 * i + NCMP], qT[64 * x:64 * x + 64, hh // 2, s * P:s * P + P],
                                      kcT[64 * x:64 * x + 64, hh // 3, :])
                        close(last)

            def nsa_scores(i):
                s, hh = i // 6, i % 6
                x, g, nk = hh % 2, hh // 3, P * (s + 1)
                b = opened(("ns", i))
                for br in range(2):
                    last = mm(b[:, T * br:T * br + nk], qT[64 * x:64 * x + 64, hh // 2, s * P:s * P + P],
                              kd[64 * x:64 * x + 64, 2 * br + g, 0:nk])
                close(last)

            def nsa_turn(i):
                s = i // 6
                pe.wait_ge(sem("nsa_probs"), i + 1)
                b = opened(("np", i))
                for br in range(2):
                    for kt in range(s + 1):
                        o = (2 * br + kt) * P
                        last = nc.tensor.transpose(b[:, o:o + P], nsc[:, i % 2, br, kt * P:kt * P + P], ident[:, :])
                close(last)

            def nsa_values(i):
                s, g = i // 6, (i % 6) // 3
                copied(("np", i))
                b = opened(("nv", i))
                for br in range(2):
                    for kt in range(s + 1):
                        last = mm(b[:, br * HD:br * HD + HD], npt[:, i % 2, 2 * br + kt, :],
                                  vtok[:, kt, br * P + g * HD:br * P + g * HD + HD], start=(kt == 0), stop=(kt == s))
                close(last)

            def compressed_values():
                for s in range(2):
                    pe.wait_ge(sem("cmp_probs"), s + 1)
                    turn(("ct", s), [csc[:, s, 3 * g:3 * g + 3, :].rearrange("p a b -> p (a b)") for g in range(2)])
                    copied(("ct", s))
                    copied(("vc",))
                    b = opened(("cpv", s))
                    for g in range(2):
                        last = mm(b[:, 192 * g:192 * g + 192], cpt[0:96, g, :],
                                  vbd[0:96, g, :, :].rearrange("p a b -> p (a b)"))
                    close(last)

            def nsa_round(i):
                if i < 11:
                    nsa_scores(i + 1)
                if i > 0:
                    nsa_values(i - 1)
                nsa_turn(i)

            bu(0)
            for j in range(8):
                if j < 7:
                    bu(j + 1)
                if j == 0:
                    compressed_hidden()
                elif j == 1:
                    copied(("cmq",))
                    turn(("cmph",), [chid])
                elif j == 2:
                    compressed_keys()
                elif j == 3:
                    compressed_scores()
                    for i in range(4):
                        copied(("kd", i))
                    nsa_scores(0)
                elif j == 4:
                    compressed_values()
                else:
                    nsa_round(j - 5)
                ada()
                y5(j)
            for i in range(3, 12):
                nsa_round(i)
                ada()
                if i == 5:
                    s5_gate()
                if i == 6:
                    pe.wait_ge(sem("lora_tanh"), 2)
                    for c in range(3):
                        b = opened(("wp", c))
                        close(mm(b[:, 0:T], lora_w[0:64, c * P:c * P + P], zs[0:64, 9, :]))
                elif i == 7:
                    for c in range(3):
                        b = opened(("ap", c))
                        close(mm(b[:, 0:T], lora_w[64:128, c * P:c * P + P], zs[64:128, 9, :]))
                    pe.wait_ge(sem("lora_in"), 1)
                    for c in range(3):
                        b = opened(("gp", c))
                        close(mm(b[:, 0:T], g2_w[:, c * P:c * P + P], zs[:, 10, :]))
                elif i == 8:
                    pe.wait_ge(sem("kk_sq"), 1)
                    for c in range(3):
                        b = opened(("kks", c))
                        close(mm(b[:, 0:T], head_ones[:, :], W[5][:, c, :]))
                elif i == 10:
                    pe.wait_ge(sem("bonus_in"), 1)
                    for c in range(3):
                        b = opened(("bon", c))
                        close(mm(b[:, 0:T], head_ones[:, :], W[5][:, c, :]))
            nsa_values(11)
            ada()
            pe.wait_ge(sem("otok_ready"), 1)
            for c in range(3):
                turn(("oT", c), [otok[:, s, c * P:c * P + P] for s in range(2)])

            pe.wait_ge(sem("gram_in"), 1)
            for s in range(2):
                cut = slice(s * P, s * P + P)
                for x, src in enumerate((W[6], W[7], W[8], zs[:, 6:9, :])):
                    turn(("tk", s, x), [src[:, c, cut] for c in range(3)])
                for name, lw, rw in (("N", 7, 6), ("L", 6, 7), ("MT", 8, 6), ("Rb", 7, 9), ("Rk", 8, 9)):
                    for p in range(2):
                        b, q = opened((name, s, p)), slice(64 * p, 64 * p + 64)
                        for c in range(3):
                            last = mm(b[:, c * P:c * P + P], W[lw][q, c, cut], W[rw][q, c, cut])
                        close(last)
                for p in range(2):
                    copied(("N", s, p))
                    copied(("L", s, p))
                pe.wait_ge(sem("tri_ready"), s + 1)
                for k, (name, lw, rw, add, dst) in enumerate(INV):
                    for p in range(2):
                        if k:
                            copied((INV[k - 1][0], s, p))
                        b = opened((name, s, p))
                        for c in range(3):
                            o = b[:, c * P:c * P + P]
                            if rw is None:
                                last = nc.tensor.transpose(o, tmat(lw)[:, p, c, :], ident[:, :])
                            else:
                                last = mm(o, tmat(lw)[:, p, c, :], tmat(rw)[:, p, c, :])
                        close(last)
                    if k % 2:
                        ada()
                for p in range(2):
                    copied(("MT", s, p))
                for x in range(4):
                    copied(("tk", s, x))
                b = opened(("mv", s))
                for c in range(3):
                    for p in range(2):
                        o = c * P + p * HD
                        last = mm(b[:, o:o + HD], KEEP[0][:, p, c, :], tok4[:, 3, c, p * HD:p * HD + HD])
                close(last)
                copied(("mv", s))
                for p in range(2):
                    copied(("T32", s, p))
                    b = opened(("au", s, p))
                    for c in range(3):
                        last = mm(b[:, c * P:c * P + P], KEEP[3][:, p, c, :], AM[:, c, :, p * HD:p * HD + HD])
                    close(last)
                for p in range(2):
                    copied(("au", s, p))
                for r in range(4):
                    q = slice(32 * r, 32 * r + 32)
                    if 4 * s + r < 7:
                        b = opened(("H", s, r))
                        for c in range(3):
                            o = b[:, c * P:c * P + P]
                            mm(o, tok4[q, 1, c, :], AU[q, c, 1, :], stop=False)
                            last = mm(o, tok4[q, 2, c, :], tok4[q, 3, c, :], start=False)
                        close(last)
                    if 0 < 4 * s + r < 7:
                        b = opened(("E", s, r))
                        for c in range(3):
                            last = mm(b[:, c * P:c * P + P], AU[q, c, 0, :], tok4[q, 1, c, :])
                        close(last)
                for p in range(2):
                    copied(("Rb", s, p))
                    copied(("Rk", s, p))
                b = opened(("rt", s))
                for p in range(2):
                    for c in range(3):
                        last = mm(b[64 * p:64 * p + 64, c * P:c * P + P], AU[:, c, 0, p * HD:p * HD + HD],
                                  KEEP[1][:, p, c, :])
                close(last)
                for r in range(4):
                    q = 4 * s + r
                    if 0 < q < 7:
                        copied(("E", s, r))
                        copied(("H", 0, 0) if q == 1 else ("st", q - 1))
                        b = opened(("st", q))
                        for c in range(3):
                            o = b[:, c * P:c * P + P]
                            last = mm(o, EB[:, r, c, :], ST[:, q - 1, c, :])
                        close(last)
                b = opened(("ol", s))
                for c in range(3):
                    for p in range(2):
                        last = mm(b[64 * p:64 * p + 64, c * P:c * P + P], AU[:, c, 1, p * HD:p * HD + HD],
                                  KEEP[1][:, p, c, :], start=(c == 0), stop=False, skip_group_check=True)
                for c in range(3):
                    for p in range(2):
                        last = mm(b[64 * p:64 * p + 64, c * P:c * P + P], tok4[:, 3, c, p * HD:p * HD + HD],
                                  KEEP[2][:, p, c, :], start=False, stop=False, skip_group_check=True)
                copied(("st", 3 if s == 0 else 6))
                copied(("rt", s))
                for q in range(max(1, 4 * s), 4 * s + 4):
                    for c in range(3):
                        o = c * P + 32 * (q % 4)
                        last = mm(b[:, o:o + 32], ST[:, q - 1, c, :], W[9][:, c, 32 * q:32 * q + 32],
                                  start=False, stop=(q == 4 * s + 3), skip_group_check=True)
                close(last)
            for s in range(2):
                copied(("ol", s))
            for c in range(3):
                b = opened(("gm", c))
                close(mm(b[:, 0:T], head_mean[:, :], zs[:, c, :]))
            for c in range(3):
                pe.wait_ge(sem("gn_sq"), c + 1)
                b = opened(("gv", c))
                close(mm(b[:, 0:T], head_mean[:, :], zs[:, 3 + c, :]))
            ada(28)
            ada_columns()

            for i in range(2):
                copied(("glu", i))
            for c in range(3):
                copied(("oT", c))
            projection(0, "out", "out", (hn_lo, hn_hi), (1, sqb), (3, 4, 5, 6, 7, 0, 1, 2))

            down_used = [0]

            def ffn(f, first, ms):
                tiles = [((nm, f, j), (nm, f, j // 2), 128 * (j % 2)) for j in range(FT) for nm in ("ug", "uu")]
                first_tiles(first, tiles[:4], (hn_lo, hn_hi))
                for t in tiles[4:]:
                    split_tile(*t, (hn_lo, hn_hi))
                for m in range(4):
                    outs = [opened(("down", f, 2 * m + i)) for i in range(2)]
                    if m == 3:
                        b_ms = opened_beside(("ms", ms[0]))
                    for c in range(3):
                        if m == 3 and c:
                            mean_square_of(ms[0], b_ms, ms[1], (2 * c - 2, 2 * c - 1))
                        key = ("down", f, m, c)
                        w = chunk(key)
                        n = chunk_src[key][0].shape[1]
                        for i in range(2):
                            for k in range(n):
                                t = 8 * c + k
                                if m == 0 and i == 0:
                                    pe.wait_ge(sem("act_split"), FT * f + t + 1)
                                last = three_passes(outs[i][:, 0:T], [v[:, k, i * P:i * P + P] for v in w],
                                                    (act_lo[:, t, :], act_hi[:, t, :]), t == 0, t == FT - 1)
                            if c == 2:
                                close(last)
                        if c < 2:
                            last.then_inc(sem("down_used"), 1)
                            down_used[0] += 1
                            chunk_used[key] = (sem("down_used"), down_used[0])
                            used_at[key] = job_no["down", f, 2 * m] - 0.5
                mean_square_of(ms[0], b_ms, ms[1], (4, 5, 6, 7))

            mean_square(2, hn)
            ffn(0, 1, (3, sqb))
            for m in range(8):
                tile(("pl", m), ("ple", 0), 128 * m, pT, kts=2)
            mean_square(4, sqb)
            projection(2, "pg", "pleg", (hn_lo, hn_hi))

            mean_square(5, hn)
            projection(3, "pi", "pin", (hn_lo, hn_hi))
            for m in range(8):
                b = opened(("pp", m))
                w = chunk(("pgrp", 0))[0]
                for k in range(2):
                    t = 2 * (m // 2) + k
                    pe.wait_ge(sem("pooled"), t + 1)
                    last = mm(b[:, 0:T], w[:, t, (m % 2) * P:(m % 2) * P + P], pu[:, t, :], start=(k == 0), stop=(k == 1))
                close(last)
            projection(4, "po", "pout", (eT_lo, hn_hi), (6, hn))
            ffn(1, 5, (7, hn))


            def projections(c):
                if c == 0:
                    yield first_tiles(6, [(("dk", c, br, i), ("kv", 4 * br + c), 128 * i) for br in range(2)
                                          for i in range(2)], (hn_lo, hn_hi))
                for br in range(2 if c == 0 else 0, 3):
                    for i in range(2):
                        yield split_tile(("dk", c, br, i), ("kv", 4 * br + c), 128 * i, (hn_lo, hn_hi))
                for br in range(3):
                    for s in range(2):
                        b = opened(("dv", c, br, s))
                        w = chunk(("kv", 12 + 4 * br + c))
                        for k in range(KT):
                            last = three_passes(b[:, 0:T], [v[:, k, s * P:s * P + P] for v in (hn_lo, hn_hi)],
                                                [v[:, k, :] for v in w], k == 0, k == KT - 1)
                        yield close(last)
                if c == 0:
                    pe.wait_ge(sem("x_split"), KT * 9)
                for br in range(3):
                    for i in range(2):
                        yield split_tile(("dq", c, br, i), ("dq", 4 * br + c), 128 * i, (hn2_lo, hn2_hi))

            def dil_scores(i):
                hh, s = i // 2, i % 2
                c = i // 8
                nk, q = P * (s + 1), slice(64 * (hh % 2), 64 * (hh % 2) + 64)
                if i % 8 == 0:
                    for br in range(3):
                        for x in range(2):
                            copied(("dk", c, br, x))
                            copied(("dq", c, br, x))
                for job, brs in (("da", (0, 1)), ("db", (2,))):
                    b = opened((job, i))
                    for br in brs:
                        t = 2 * br + hh // 2 % 2
                        last = mm(b[:, T * (br % 2):T * (br % 2) + nk], dq[q, c % 2, t, s * P:s * P + P],
                                  dk[q, c % 2, t, 0:nk])
                    close(last)

            def dil_turn(i):
                s = i % 2
                pe.wait_ge(sem("dil_probs"), i + 1)
                n = 3 * (s + 1)
                src = dsc[:, i % 2, 0:n * P]
                turn(("dp", i, 0), [src[:, k * P:k * P + P] for k in range(3)])
                if s:
                    turn(("dp", i, 1), [src[:, k * P:k * P + P] for k in range(3, 6)])

            def dil_values(i):
                hh, s = i // 2, i % 2
                for x in range(s + 1):
                    copied(("dp", i, x))
                if i % 8 == 0:
                    for br in range(3):
                        for x in range(2):
                            copied(("dv", i // 8, br, x))
                b = opened(("dy", i))
                n = 3 * (s + 1)
                for k in range(n):
                    br, kt = k // (s + 1), k % (s + 1)
                    c = HD * (hh % 4)
                    last = mm(b[:, 0:HD], dpt[:, i % 2, k, :], dv[:, i // 8 % 2, kt, br, c:c + HD], start=(k == 0), stop=(k == n - 1))
                close(last)

            for _ in projections(0):
                pass
            dil_scores(0)
            for i in range(32):
                if i < 31:
                    dil_scores(i + 1)
                if i > 0:
                    dil_values(i - 1)
                dil_turn(i)
                if i % 8 == 0:
                    coming = projections(i // 8 + 1) if i < 24 else iter(())
                for _ in range(proj_share(i)):
                    next(coming, None)
            dil_values(31)
            copied(("dy", 30))
            copied(("dy", 31))
            for j in range(4):
                turn(("dt", j), [dotok[:, s, (2 * j + k) * P:(2 * j + k + 1) * P] for k in range(2) for s in range(2)])
            projection(8, "dw", "do", (hn_lo, hn_hi), (8, hn2))
            ffn(2, 9, (9, hn))
            for s in range(2):
                for f in range(2):
                    for k in range(4):
                        if s == 0:
                            pe.wait_ge(sem("hn_ready"), 16 + 4 * f + k + 1)
                    turn(("fin", 2 * s + f), [hn[:, 4 * f + k, s * P:s * P + P] for k in range(4)])

        def taker(eng):
            def take(job):
                eng.wait_ge(psum_ready, job_no[job] + 1)
                return bank_of(job)
            return take

        SMALL = 16 * 13

        def stage_rows(eng, some, signal):
            for r, m, src in some:
                eng.dma_start(stage[r % P:r % P + m, r // P, :], src).then_inc(signal, 16)

        def small_inputs(eng):
            eng.dma_start(lora_w[0:64, :], a["rw_w2"][0]).then_inc(small_in, 16)
            eng.dma_start(lora_w[64:128, :], a["rw_a2"][0]).then_inc(small_in, 16)
            eng.dma_start(g2_w, a["rw_g2"][0]).then_inc(small_in, 16)
            eng.dma_start(cw2[:, 0, :], a["cmp_w2_k"][0]).then_inc(small_in, 16)
            eng.dma_start(cw2[:, 1, :], a["cmp_w2_k"][0]).then_inc(small_in, 16)
            eng.dma_start(cw2[:, 2, :], a["cmp_w2_v"][0]).then_inc(small_in, 16)
            eng.dma_start(wglu, a["s5_w_glu"][0].rearrange("(k p) n -> p k n", p=P)).then_inc(small_in, 16)
            for ri, nm in enumerate(("s5_b_re", "s5_b_im")):
                eng.dma_start(bfull[:, ri], a[nm][0].rearrange("(j g) n c -> (g n) j c", g=2)).then_inc(small_in, 16)
            for ri, nm in enumerate(("s5_c_re", "s5_c_im")):
                for x in range(2):
                    eng.dma_start(cdup[:, ri, :, HD * x:HD * x + HD],
                                   a[nm][0].rearrange("(f g) c n -> (g c) f n", f=2)).then_inc(small_in, 16)

        @block.sync
        def _(sp):
            sp.dma_start(xtok, a["x"][0].rearrange("(s p) d -> p s d", p=P)).then_inc(setup_in, 16)
            sp.dma_start(ptok, a["p"][0, 0].rearrange("(s p) d -> p s d", p=P)).then_inc(setup_in, 16)
            sp.wait_ge(sem("stage_clear"), 2)
            stage_rows(sp, soon[0::2], sem("soon_in"))
            stage_rows(sp, later[0::2], sem("later_in"))
            order = sorted(chunk_no, key=chunk_no.get)
            for n, key in enumerate(order):
                if n >= SLOTS:
                    sp.wait_ge(*chunk_used[order[n - SLOTS]])
                if n == SLOTS:
                    small_inputs(sp)
                for dst, src in zip(chunk_view(key), chunk_src[key]):
                    sp.dma_start(dst, src).then_inc(landed[n % SLOTS], 16)
            for s in range(2):
                for f in range(2):
                    sp.wait_ge(*freed(("fin", 2 * s + f)))
                    sp.dma_start(out[0, s * P:s * P + P, 512 * f:512 * f + 512],
                                 outt[:, s, 512 * f:512 * f + 512]).then_inc(sem("out_done"), 16)
            sp.wait_ge(sem("out_done"), 64)

        @block.gpsimd
        def _(pool):
            led = Ledger(pool, sem("pool_own"))
            g = nc.gpsimd

            def keep_if(o, op, base, cm, pattern, fill=0.0, signal=None):
                led.settle()
                led.emit(g.affine_select(out=o, in_=o, compare_op=op, fill=fill, base=base, pattern=pattern,
                                         channel_multiplier=cm), signal)

            def on_blocks(o, size, nb, width):
                v = o if width == 1 else o.rearrange("p (b c) -> p b c", b=nb)
                pat = [[-size, nb]] + ([[0, width]] if width > 1 else [])
                neg = [[size, nb]] + ([[0, width]] if width > 1 else [])
                keep_if(v, ALU.is_ge, 0, 1, pat)
                keep_if(v, ALU.is_ge, size - 1, -1, neg)

            led.emit(g.memset(ident[:, :], 0.0), sem("ident_ready"))
            keep_if(ident[:, :], ALU.not_equal, 0, 1, [[-1, P]], 1.0, sem("ident_ready"))
            led.emit(g.memset(ones_mean[:, :], 1.0 / D), sem("mean_ready"))
            led.emit(g.memset(head_ones[:, :], 1.0))
            led.emit(g.memset(head_mean[:, :], 1.0 / HD))
            led.emit(g.memset(masks[:, :, :], 1.0))
            led.emit(g.memset(scan_keep[:, :], 1.0))
            led.emit(g.memset(block3[:, :], 1.0))
            led.emit(g.memset(block2[:, :], 1.0))
            led.emit(g.memset(row_ok[:, :], 1.0))
            on_blocks(head_ones[:, :], HD, 2, HD)
            on_blocks(head_mean[:, :], HD, 2, HD)
            on_blocks(block3[:, :], 32, 3, 1)
            on_blocks(block2[:, :], HD, 2, 1)
            for m, size in ((U8, 8), (L8M, 8), (L16M, 16), (L32M, 32), (U32S, 32), (U32I, 32)):
                on_blocks(m, size, P // size, size)
            for m, up, strict in ((U8, 1, 1), (L8M, 0, 1), (L16M, 0, 1), (L32M, 0, 1), (U32S, 1, 1), (U32I, 1, 0)):
                keep_if(m, ALU.is_ge, -strict, -1 if up else 1, [[1 if up else -1, P]])
            led.settle()
            led.emit(g.tensor_tensor(L32M, L32M, L16M, ALU.subtract))
            led.settle()
            led.emit(g.tensor_tensor(L16M, L16M, L8M, ALU.subtract))
            keep_if(row_ok[:, :], ALU.is_ge, -31, 1, [[P, 2]])
            led.emit(g.memset(shaped(scan_keep[:, :], 8, 32)[:, :, 0], 0.0))
            led.emit(g.iota(dist[:, :, :], pattern=[[P, 2], [-1, T]], base=0, channel_multiplier=1,
                            allow_small_or_imprecise_dtypes=True))
            led.emit(g.iota(cdist[:, :, :], pattern=[[P, 2], [-16, NCMP]], base=-31, channel_multiplier=1,
                            allow_small_or_imprecise_dtypes=True))
            keep_if(dist[:, :, :], ALU.is_ge, 0, 1, [[P, 2], [-1, T]], FAR)
            keep_if(cdist[:, :, :], ALU.is_ge, -31, 1, [[P, 2], [-16, NCMP]], FAR)
            led.emit(g.memset(one_each[:, :], 0.0))
            for q in (0, 32, 64, 96):
                keep_if(one_each[:, :], ALU.not_equal, -q, 1, [[0, 1]], 1.0)
            led.settle()
            for hh, sl in enumerate(nsa_slopes(6)):
                led.emit(g.tensor_scalar(cbias[:, :, hh, :], cdist[:, :, :], -sl, None, ALU.mult))
            led.settle()
            led.emit(g.memset(hid[:, :, :], 0.0))
            led.emit(g.memset(csc[:, :, :, :], 0.0), sem("consts"))
            led.emit(g.memset(tabC[:, :, 0:1], 1.0))
            led.emit(g.memset(tabS[:, :, 0:1], 0.0))

            pool.wait_ge(sem("theta_ready"), 2)
            led.emit(g.tensor_copy(powr[:, 0, :], s5v[:, 8, :]))
            led.emit(g.tensor_copy(powr[:, 1, :], s5v[:, 7, :]))
            n = 1
            while n < T:
                led.settle()
                pc, ps = (powr[:, x, :].unsqueeze(2).broadcast_to([P, 8, n]) for x in range(2))
                lo, hi = slice(0, n), slice(n, 2 * n)
                for tab, (x, y), op in ((tabC, (tabC, tabS), ALU.subtract), (tabS, (tabS, tabC), ALU.add)):
                    led.settle()
                    led.emit(g.tensor_tensor(ptmp[:, 0, :, lo], x[:, :, lo], pc, ALU.mult))
                    led.emit(g.tensor_tensor(ptmp[:, 1, :, lo], y[:, :, lo], ps, ALU.mult))
                    led.settle()
                    led.emit(g.tensor_tensor(tab[:, :, hi], ptmp[:, 0, :, lo], ptmp[:, 1, :, lo], op))
                n *= 2
                if n < T:
                    led.settle()
                    led.emit(g.tensor_tensor(s5v[:, 18, :], powr[:, 0, :], powr[:, 0, :], ALU.mult))
                    led.emit(g.tensor_tensor(s5v[:, 19, :], powr[:, 1, :], powr[:, 1, :], ALU.mult))
                    led.emit(g.tensor_tensor(s5v[:, 20, :], powr[:, 0, :], powr[:, 1, :], ALU.mult))
                    led.settle()
                    led.emit(g.tensor_tensor(powr[:, 0, :], s5v[:, 18, :], s5v[:, 19, :], ALU.subtract))
                    led.emit(g.tensor_scalar(powr[:, 1, :], s5v[:, 20, :], 2.0, None, ALU.mult))
            led.settle()
            led.emit(g.memset(chid, 0.0), sem("tables"))
            led.emit(g.memset(hidv[:, :, :, :], 0.0), sem("tables"))

            def turned_in(j):
                w = s5w[:, j % 2]
                pool.wait_ge(*freed(("bu", j)))
                led.emit(g.tensor_tensor(w[:, 2, 0, :], w[:, 0, 0, :], w[:, 1, 1, :], ALU.add))
                led.emit(g.tensor_tensor(w[:, 2, 1, :], w[:, 0, 1, :], w[:, 1, 0, :], ALU.subtract), sem("s5_in"))

            turned_in(0)
            for j in range(8):
                if j < 7:
                    turned_in(j + 1)
                w = s5w[:, j % 2]
                pool.wait_ge(sem("s5_out"), j + 1)
                if j >= 2:
                    pool.wait_ge(psum_ready, job_no["y5", j - 2] + 1)
                led.emit(g.tensor_tensor(w[:, 4, 0, :], w[:, 0, 0, :], w[:, 1, 1, :], ALU.subtract))
                led.emit(g.tensor_tensor(w[:, 4, 1, :], w[:, 0, 1, :], w[:, 1, 0, :], ALU.add), sem("s5_states"))

            def low_parts(keys):
                for key in keys:
                    raw, low, high = chunk_flat(key)
                    pool.wait_ge(sem("hi_ready"), split_no[key] + 1)
                    led.emit(g.tensor_tensor(low, raw, high.bitcast(F32), ALU.subtract), sem("lo_ready"))

            order = sorted(split_no, key=split_no.get)
            low_parts(order[:10])
            pool.wait_ge(sem("gains"), 5)
            led.emit(g.iota(dint.bitcast(mybir.dt.int32), pattern=[[P, 2], [-1, T]], base=0, channel_multiplier=1))
            led.emit(g.iota(inv_count[:, :, :], pattern=[[0, 4], [1, T]], base=1, channel_multiplier=0,
                            allow_small_or_imprecise_dtypes=True))
            led.emit(g.tensor_copy(bdist[:, 0, :, :], dist[:, :, :]))
            keep_if(bdist[:, 0, :, :], ALU.is_ge, P, -1, [[-P, 2], [1, T]], FAR)
            for w in range(4):
                led.emit(g.tensor_scalar(inv_count[:, w, :], inv_count[:, w, :], float(2 ** (w + 1)), None, ALU.min),
                         sem("late_consts") if w == 3 else None)
            low_parts(order[10:])

        @block.vector
        def _(dve):
            led = Ledger(dve, sem("dve_own"))
            v = nc.vector
            take0 = taker(dve)
            ada_jobs = sorted((n, job) for job, n in job_no.items() if job[0] == "adc")

            def modulation_before(job):
                while ada_jobs and ada_jobs[0][0] < job_no[job]:
                    aj = ada_jobs.pop(0)[1]
                    b, i = take0(aj), aj[1]
                    led.emit(v.tensor_tensor(mod[:, 4 * i:4 * i + 4], b[:, 0:4], cols("ada_b", 4, 4 * i), ALU.add),
                             *freed(aj))

            def take(job):
                modulation_before(job)
                return take0(job)

            def placed(job):
                modulation_before(job)
                dve.wait_ge(*freed(job))

            def tt(o, x, y, op, signal=None, value=None):
                led.emit(v.tensor_tensor(o, x, y, op), signal, value)

            def ts(o, x, s1, op0, s2=None, op1=ALU.bypass, signal=None, value=None):
                led.emit(v.tensor_scalar(o, x, s1, s2, op0, op1) if s2 is not None else
                         v.tensor_scalar(o, x, s1, None, op0), signal, value)

            def stt(o, x, s, y, op0, op1, signal=None, value=None):
                led.emit(v.scalar_tensor_tensor(out=o, in0=x, scalar=s, in1=y, op0=op0, op1=op1), signal, value)

            def copy(o, x, signal=None, value=None):
                led.emit(v.tensor_copy(o, x), signal, value)

            def rec(o, x, signal=None):
                led.emit(v.reciprocal(o, x), signal)

            settle = led.settle
            MUL, ADD, SUB = ALU.mult, ALU.add, ALU.subtract

            def low_part(n, low, x, high):
                dve.wait_ge(sem("x_high"), KT + n + 1)
                tt(low, x, high.bitcast(F32), SUB, sem("x_split"))

            led.emit(v.memset(stage[:, :, :], 0.0), sem("stage_clear"))
            led.emit(v.memset(eps_col, EPS), sem("stage_clear"))
            def norm_scale(i):
                placed(("ms", i))
                rec(rs[:, 1, :], rs[:, 0, :])
                settle()

            for j in range(4):
                b = take(("xT", j))
                copy(h[:, 2 * j:2 * j + 2, :], shaped(b, 2, T), *freed(("xT", j)))
            def early_low(c):
                raw, low, high = chunk_flat(early[c])
                dve.wait_ge(sem("early_hi"), c + 1)
                tt(low, raw, high.bitcast(F32), SUB, sem("early_lo"))

            early_low(0)
            norm_scale(0)
            b = take(("par", 0))
            copy(par[:, 0:384], b[:, 0:384], *freed(("par", 0)))
            settle()
            for k in range(KT):
                stt(hn[:, k, :], h[:, k, :], col("pre_mix", k), rs[:, 1, :], MUL, MUL, sem("hn_ready"))

            for k in range(KT):
                low_part(k - KT, hn_lo[:, k, :], hn[:, k, :], hn_hi[:, k, :])

            early_low(1)
            settle()
            ts(drv[:, 0:11], cols("mu", 11), -1.0, MUL, 1.0, ADD)
            ts(drv[:, 11:14], cols("w0", 3), 0.5, MUL)
            ts(drv[:, 14:17], cols("a0", 3), 0.5, MUL)
            ts(drv[:, 17:20], cols("k_a", 3), -1.0, MUL, 1.0, ADD, signal=sem("derived"))
            dve.wait_ge(sem("later_in"), later_total)
            copy(shaped(dt_wide[0:8, :], 2, HD), dt_rows[0:8, :].unsqueeze(2).broadcast_to([8, 2, HD]), sem("dt_spread"))
            b = take(("par", 1))
            copy(par[:, 384:6 * P + 8], b[:, 0:392], *freed(("par", 1)))
            b = take(("pT",))
            copy(pT[:, :, :], shaped(b, 2, T), *freed(("pT",)))
            dve.wait_ge(sem("cond_tanh"), 1)
            stt(cond[:, :], cond[:, :], 1.0, cols("c", 8), ADD, MUL)
            settle()
            ts(cond_wide[:, :, :], cond[:, :].unsqueeze(2).broadcast_to([P, KT, 32]), 0.5, MUL, signal=sem("cond_ready"))

            def z(i):
                return s5v[:, i, :]
            lre, lim = cols("lam_re", 8), cols("lam_im", 8)
            dve.wait_ge(sem("s5_dt"), 1)
            tt(z(1), lre, z(0), MUL)
            tt(z(3), lim, z(0), MUL, sem("s5_lr"))
            settle()
            ts(z(4), z(3), 1.0 / (2 * math.pi), MUL, MAGIC, ADD)
            settle()
            ts(z(4), z(4), MAGIC, SUB)
            settle()
            stt(z(5), z(4), -6.28125, z(3), MUL, ADD)
            settle()
            stt(z(5), z(4), -(2 * math.pi - 6.28125), z(5), MUL, ADD)
            settle()
            ts(z(5), z(5), 3.1415925, ALU.min, -3.1415925, ALU.max)
            settle()
            ts(z(6), z(5), math.pi / 2, ALU.is_gt, -2 * math.pi, MUL)
            settle()
            stt(z(6), z(5), math.pi / 2, z(6), ADD, ADD)
            settle()
            ts(z(6), z(6), 3.1415925, ALU.min, -3.1415925, ALU.max, signal=sem("s5_angle"))
            tt(z(11), lre, lre, MUL)
            tt(z(12), lim, lim, MUL)
            settle()
            tt(z(11), z(11), z(12), ADD)
            settle()
            rec(z(12), z(11))
            dve.wait_ge(sem("theta_ready"), 2)
            tt(z(9), z(2), z(8), MUL)
            tt(z(10), z(2), z(7), MUL)
            settle()
            ts(z(15), z(9), 1.0, SUB)
            settle()
            tt(z(13), z(15), lre, MUL)
            tt(z(16), z(10), lim, MUL)
            tt(z(14), z(10), lre, MUL)
            tt(z(17), z(15), lim, MUL)
            settle()
            tt(z(13), z(13), z(16), ADD)
            tt(z(14), z(14), z(17), SUB)
            settle()
            tt(z(13), z(13), z(12), MUL)
            tt(z(14), z(14), z(12), MUL)
            settle()
            for i in range(RW_TILES):
                if i % 2 == 0:
                    early_low(i // 2 + 2)
                b = take(("rw", i))
                dve.wait_ge(sem("shift_own"), i + 1)
                stt(zs[:, i, 1:T], b[:, 0:T - 1], col("mu", i), zs[:, i, 1:T], MUL, ADD, *freed(("rw", i)))
            dve.wait_ge(sem("consts"), 1)
            dve.wait_ge(small_in, SMALL)
            fre, fim = (z(i).unsqueeze(2).broadcast_to([P, 8, 16]) for i in (13, 14))
            for ri, (x, y, op) in enumerate(((0, 1, SUB), (1, 0, ADD))):
                tt(bmul[:, ri], bfull[:, x], fre, MUL)
                tt(bdup[:, ri, :, 0, :], bfull[:, y], fim, MUL)
                settle()
                tt(bmul[:, ri], bmul[:, ri], bdup[:, ri, :, 0, :], op)
                settle()
                for bb in range(2):
                    ts(bdup[:, ri, :, bb, :], bmul[:, ri], block2[:, bb:bb + 1], MUL,
                       signal=sem("b_ready") if ri and bb else None)
            for c in range(8, len(early)):
                early_low(c)
            placed(("gtok",))
            ts(gate[:, :, :], gate[:, :, :], 0.5, MUL, 0.5, ADD)

            b = take(("bT",))
            copy(BT[:, :, :, :].rearrange("p a b c -> p (a b c)"), b, *freed(("bT",)))
            b = take(("cT",))
            pb = shaped(b, 2, 2, 4, 2, 16)
            for ri in range(2):
                for bb in range(2):
                    last = ri == 1 and bb == 1
                    o = CT[:, ri].rearrange("p f (a b c) -> p f a b c", a=4, b=2)[:, :, :, bb, :]
                    ts(o, pb[:, ri, :, :, bb, :], block2[:, bb:bb + 1], MUL, -1.0 if ri else 1.0, MUL,
                       signal=freed(("cT",))[0] if last else None, value=freed(("cT",))[1] if last else None)
            dve.wait_ge(sem("tables"), 2)

            def s5_in(j):
                b = shaped(take(("bu", j)), 2, T)
                w = s5w[:, j % 2]
                if j >= 2:
                    dve.wait_ge(sem("s5_states"), j - 1)
                tt(w[:, 0], b, tabC[:, j, :].unsqueeze(1).broadcast_to([P, 2, T]), MUL)
                tt(w[:, 1], b, tabS[:, j, :].unsqueeze(1).broadcast_to([P, 2, T]), MUL, *freed(("bu", j)))

            def s5_scan(j):
                w = s5w[:, j % 2]
                dve.wait_ge(sem("s5_in"), j + 1)
                for x in range(2):
                    led.emit(v.tensor_tensor_scan(w[:, 3, x, :], z(2)[:, j:j + 1].broadcast_to([P, T]), w[:, 2, x, :],
                                                  0.0, MUL, ADD))
                settle()
                tt(w[:, 0], w[:, 3], tabC[:, j, :].unsqueeze(1).broadcast_to([P, 2, T]), MUL)
                tt(w[:, 1], w[:, 3], tabS[:, j, :].unsqueeze(1).broadcast_to([P, 2, T]), MUL, sem("s5_out"))

            def s5_y(j):
                b, q = take(("y5", j)), slice(32 * (j % 4), 32 * (j % 4) + 32)
                f = j // 4
                stt(ygel[q, f, :], uT[q, f, :], par[q, row0["s5_d"] + f:row0["s5_d"] + f + 1], b[q, 0:T], MUL, ADD,
                    *freed(("y5", j)))

            slopes6 = nsa_slopes(6)

            def nsa_bias(i):
                s, hh, u = i // 6, i % 6, i % 2
                nk = P * (s + 1)
                b = shaped(take(("ns", i)), 2, T)
                if i >= 2:
                    dve.wait_ge(psum_ready, job_no["np", i - 2] + 1)
                stt(nsc[:, u, :, 0:nk], dist[:, s, 0:nk].unsqueeze(1).broadcast_to([P, 2, nk]), -slopes6[hh],
                    b[:, :, 0:nk], MUL, ADD, *freed(("ns", i)))
                settle()
                led.emit(v.tensor_reduce(nst[:, i % 4, 0, :], nsc[:, u, :, 0:nk], AX.X, ALU.max, negate=True),
                         sem("nsa_max"))

            def nsa_out(i):
                s, hh, u = i // 6, i % 6, i % 2
                dve.wait_ge(sem("nsa_probs"), i + 1)
                rec(nst[:, i % 4, 2, :], nst[:, i % 4, 1, :])
                settle()
                tt(nst[:, i % 4, 3, :], nst[:, i % 4, 2, :], gate[:, s, 3 * hh + 1:3 * hh + 3], MUL)
                b = take(("nv", i))
                o = otok[:, s, HD * hh:HD * hh + HD]
                settle()
                stt(o, b[:, 0:HD], nst[:, i % 4, 3, 0:1], o, MUL, ADD)
                settle()
                stt(o, b[:, HD:2 * HD], nst[:, i % 4, 3, 1:2], o, MUL, ADD, *freed(("nv", i)))

            rr, kk_, vv = zs[:, 0:3, :], zs[:, 3:6, :], zs[:, 6:9, :]

            def nsa_round(i):
                if i < 11:
                    nsa_bias(i + 1)
                if i > 0:
                    nsa_out(i - 1)

            s5_in(0)
            for j in range(8):
                if j < 7:
                    s5_in(j + 1)
                s5_scan(j)
                if j:
                    s5_y(j - 1)
                if j == 2:
                    b = take(("vc",))
                    for x in range(3):
                        ts(vbd[0:96, :, x, :], shaped(b[0:96, 0:P], 2, HD), block3[0:96, x:x + 1], MUL,
                           signal=freed(("vc",))[0] if x == 2 else None, value=freed(("vc",))[1] if x == 2 else None)
                elif j == 3:
                    for s in range(2):
                        for x in range(2):
                            b = take(("cs", s, x))
                            tt(csc[:, s, x::2, 0:NCMP], shaped(b[:, 0:96], 3, 32)[:, :, 0:NCMP], cbias[:, s, x::2, :], ADD,
                               *freed(("cs", s, x)))
                    settle()
                    for s in range(2):
                        led.emit(v.tensor_reduce(cst[:, s, 0, :], csc[:, s, :, 0:NCMP], AX.X, ALU.max))
                    settle()
                    for s in range(2):
                        tt(csc[:, s, :, 0:NCMP], csc[:, s, :, 0:NCMP], cst[:, s, 0, :].unsqueeze(2).broadcast_to([P, 6, NCMP]),
                           SUB, sem("cmp_shifted"))
                    nsa_bias(0)
                elif j == 4:
                    for s in range(2):
                        dve.wait_ge(sem("cmp_exp"), s + 1)
                        led.emit(v.tensor_reduce(cst[:, s, 1, :], csc[:, s, :, 0:NCMP], AX.X, ADD))
                    settle()
                    for s in range(2):
                        rec(cst[:, s, 2, :], cst[:, s, 1, :])
                    settle()
                    for s in range(2):
                        stt(cst[:, s, 3, :], cst[:, s, 2, :], row_ok[:, s:s + 1], gate[:, s, 0::3], MUL, MUL)
                    settle()
                    for s in range(2):
                        tt(csc[:, s, :, 0:NCMP], csc[:, s, :, 0:NCMP], cst[:, s, 3, :].unsqueeze(2).broadcast_to([P, 6, NCMP]),
                           MUL, sem("cmp_probs"))
        
                    for s in range(2):
                        b = take(("ct", s))
                        if s:
                            dve.wait_ge(psum_ready, job_no["cpv", 0] + 1)
                        copy(cpt[0:96, :, :], shaped(b[0:96, 0:T], 2, P), *freed(("ct", s)))
                        b = take(("cpv", s))
                        copy(otok[:, s, :], b[:, 0:384], *freed(("cpv", s)))
                elif j > 4:
                    nsa_round(j - 5)
            s5_y(7)
            for i in range(3, 12):
                nsa_round(i)
                if i == 5:
                    for m in range(2):
                        placed(("glu", 2 + m))
                        ts(s5g[:, m, :], s5g[:, m, :], 0.5, MUL, 0.5, ADD)
                    settle()
                    for m in range(2):
                        b = take(("glu", m))
                        tt(hn[:, 6 + m, :], b[:, 0:T], s5g[:, m, :], MUL, *freed(("glu", m)))
        
                elif i == 6:
                    dve.wait_ge(sem("lora_tanh"), 2)
                    ts(zs[:, 10, :], zs[:, 10, :], 0.5, MUL, 0.5, ADD, signal=sem("lora_in"))
                    for c in range(3):
                        placed(("wp", c))
                    ts(W[0], W[0], -0.5 * math.exp(-0.5), MUL, -0.5 * math.exp(-0.5), ADD)
                    settle()
                    for c in range(3):
                        led.emit(v.tensor_tensor_scan(W[1][:, c, :], scan_keep[:, :], W[0][:, c, :], 0.0, MUL, ADD))
                    settle()
                    tt(W[0], W[1], W[0], SUB, sem("logs"))
                    for c in range(3):
                        ts(W[4][:, c, :], kk_[:, c, :], col("k_k", c), MUL)
                    settle()
                    tt(W[5], W[4], W[4], MUL, sem("kk_sq"))
                elif i == 7:
                    for c in range(3):
                        placed(("ap", c))
                    ts(W[3], W[3], 0.5, MUL, 0.5, ADD)
                    settle()
                    for c in range(3):
                        ts(W[11][:, c, :], W[3][:, c, :], col("k_a", c), MUL, omka(c), ADD)
                    settle()
                    tt(kk_, kk_, W[11], MUL)
                elif i == 8:
                    for c in range(3):
                        b = take(("kks", c))
                        ts(W[5][:, c, :], b[:, 0:T], 1e-24, ALU.max, signal=freed(("kks", c))[0], value=freed(("kks", c))[1])
                    settle()
                    rec(W[5], W[5], sem("kk_rec"))
                elif i == 9:
                    dve.wait_ge(sem("exps"), 3)
                    tt(W[8], kk_, W[2], MUL)
                    tt(W[9], rr, W[1], MUL)
                    copy(Pend[:, :, :], W[1][:, :, 31::32])
                    dve.wait_ge(sem("kk_root"), 1)
                    tt(W[4], W[4], W[5], MUL)
                    settle()
                    for c in range(3):
                        stt(W[5][:, c, :], rr[:, c, :], col("r_k", c), kk_[:, c, :], MUL, MUL,
                            sem("bonus_in") if c == 2 else None)
                    tt(W[7], W[4], W[3], MUL)
                    stt(W[6].rearrange("p a b -> p (a b)"), W[4].rearrange("p a b -> p (a b)"), -1.0,
                        W[0].rearrange("p a b -> p (a b)"), MUL, MUL)
                    settle()
                    tt(W[7], W[7], W[2], MUL, sem("gram_in"))
                elif i == 10:
                    for c in range(3):
                        b = take(("bon", c))
                        tt(W[11][:, c, :], b[:, 0:T], vv[:, c, :], MUL, *freed(("bon", c)))
        

            nsa_out(11)
            settle()
            led.emit(v.memset(nst[:, 0, 0, :], 0.0), sem("otok_ready"))

            def over3(m):
                return m.unsqueeze(1).broadcast_to([P, 3, P])

            def three(b):
                return shaped(b[:, 0:384], 3, P)

            for s in range(2):
                cut = slice(s * P, s * P + P)
                for p in range(2):
                    b = take(("N", s, p))
                    tt(TM[0][:, p], three(b), over3(U8), MUL, *freed(("N", s, p)))
                for p in range(2):
                    b = take(("L", s, p))
                    tt(TM[1][:, p], three(b), over3(L8M), MUL)
                    tt(TM[2][:, p], three(b), over3(L16M), MUL)
                    tt(TM[3][:, p], three(b), over3(L32M), MUL, *freed(("L", s, p)))
                settle()
                for p in range(2):
                    tt(TM[7][:, p], TM[0][:, p], over3(ident[:, :]), ADD, sem("tri_ready") if p else None)
                for name, k, m in (("MT", 0, U32S), ("Rb", 1, U32I), ("Rk", 2, U32I)):
                    for p in range(2):
                        b = take((name, s, p))
                        tt(KEEP[k][:, p], three(b), over3(m), MUL, *freed((name, s, p)))
                for name, _l, _r, add, to in INV:
                    b = take((name, s, 0))
                    if add is None:
                        copy(tmat(to)[:, 0], three(b), *freed((name, s, 0)))
                    else:
                        tt(tmat(to)[:, 0], three(b), tmat(add)[:, 0], ADD, *freed((name, s, 0)))
                        b = take((name, s, 1))
                        tt(tmat(to)[:, 1], three(b), tmat(add)[:, 1], ADD, *freed((name, s, 1)))
                if s == 0:
                    for k in range(3, 8):
                        low_part(k - 3, hn_lo[:, k, :], hn[:, k, :], hn_hi[:, k, :])
                b = take(("mv", s))
                copy(AM[:, :, 1, :], three(b), *freed(("mv", s)))
                b = take(("au", s, 0))
                copy(AU[:, :, :, 0:HD], shaped(b[:, 0:384], 3, 2, HD), *freed(("au", s, 0)))
                for r in range(4):
                    q = 4 * s + r
                    if q < 7:
                        b = three(take(("H", s, r)))
                        for c in range(3):
                            o = ST[:, 0, c, :] if q == 0 else HB[:, r, c, :]
                            stt(o, b[:, c, :], Pend[:, c, q:q + 1], head_ones[:, :], MUL, MUL,
                                *(freed(("H", s, r)) if c == 2 else (None, None)))
                    if 0 < q < 7:
                        b = three(take(("E", s, r)))
                        tt(EB[:, r], b, over3(head_ones[:, :]), MUL)
                        settle()
                        tt(EB[:, r], EB[:, r], over3(ident[:, :]), ADD, *freed(("E", s, r)))
                b = take(("rt", s))
                tt(W[9][:, :, cut], three(b), W[9][:, :, cut], ADD, *freed(("rt", s)))
                settle()
                for r in range(4):
                    q = 4 * s + r
                    if 0 < q < 7:
                        b = three(take(("st", q)))
                        for c in range(3):
                            stt(ST[:, q, c, :], b[:, c, :], Pend[:, c, q:q + 1], HB[:, r, c, :], MUL, ADD,
                                *(freed(("st", q)) if c == 2 else (None, None)))
            for s in range(2):
                placed(("ol", s))
            for c in range(3):
                b = take(("gm", c))
                tt(zs[:, c, :], zs[:, c, :], b[:, 0:T], SUB, *freed(("gm", c)))
            for c in range(3):
                b = take(("gv", c))
                ts(zs[:, 6 + c, :], b[:, 0:T], GN_EPS, ADD, signal=freed(("gv", c))[0], value=freed(("gv", c))[1])
                settle()
                rec(zs[:, 6 + c, :], zs[:, 6 + c, :], sem("gn_rec"))
            for c in range(3):
                dve.wait_ge(sem("gn_root"), c + 1)
                stt(zs[:, c, :], zs[:, c, :], col("gn_w", c), zs[:, 6 + c, :], MUL, MUL)
                settle()
                stt(zs[:, c, :], zs[:, c, :], col("gn_b", c), W[11][:, c, :], ADD, ADD)
                settle()
                tt(hn[:, c, :], zs[:, c, :], W[10][:, c, :], MUL, sem("mix_rw"))
            for c in range(3):
                low_part(5 + c, hn_lo[:, c, :], hn[:, c, :], hn_hi[:, c, :])

            def add_normed(i, gain, y):
                norm_scale(i)
                for k in range(KT + 2):
                    settle()
                    if k < KT:
                        stt(y[:, k, :], y[:, k, :], col(gain, k), rs[:, 1, :], MUL, MUL)
                    if k >= 2:
                        tt(h[:, k - 2, :], h[:, k - 2, :], y[:, k - 2, :], ADD, sem("h_ready"))

            def ffn(f):
                W0, B0, n = (row0["conv_w"], row0["conv_b"], 44) if f == 0 else \
                    (row0["fconv_w"] + 66 * (f - 1), row0["fconv_b"] + 22 * (f - 1), 22)

                def product(j):
                    u = j % 2
                    dve.wait_ge(sem("gate_act"), FT * f + j + 1)
                    other = ct[:, u, 1, :] if f == 0 else take(("uu", f, j))[:, 0:T]
                    tt(act[:, j, :], other, ct[:, u, 0, :], MUL)
                    tt(act_hi[:, j, :], other, ct[:, u, 0, :], MUL, *((sem("act_ready"),) if f == 0 else freed(("uu", f, j))))

                def act_low(j):
                    tt(act_lo[:, j, :], act[:, j, :], act_hi[:, j, :].bitcast(F32), SUB, sem("act_split"))

                parts = ("ug", "uu") if f == 0 else ("ug",)
                for j in range(FT):
                    bs = []
                    for x, nm in enumerate(parts):
                        bs.append(take((nm, f, j)))
                        dve.wait_ge(sem("conv_own"), conv_base[f] + len(parts) * j + x + 1)
                        t = ct[:, j % 2, x, :]
                        w = W0 + n + 22 * x + j
                        stt(t[:, 1:T], bs[x][:, 0:T - 1], par[:, w:w + 1], t[:, 1:T], MUL, ADD)
                    settle()
                    for x, nm in enumerate(parts):
                        t = ct[:, j % 2, x, :]
                        w = W0 + 22 * x + j
                        stt(t[:, 2:T], bs[x][:, 0:T - 2], par[:, w:w + 1], t[:, 2:T], MUL, ADD, *freed((nm, f, j)))
                    if j > 1:
                        act_low(j - 2)
                    if j:
                        product(j - 1)
                settle()
                act_low(FT - 2)
                product(FT - 1)
                settle()
                act_low(FT - 1)
                if f:
                    for m in range(8):
                        b = take(("down", f, m))
                        stt(h[:, m, :], b[:, 0:T], mc(f - 1, 5, m), h[:, m, :], MUL, ADD, *freed(("down", f, m)))

            def modulated(n, rnd, x, low, high, shift):
                for k in range(KT):
                    stt(x[:, k, :], h[:, k, :], gsc[:, 8 * n + k:8 * n + k + 1], rs[:, 1, :], MUL, MUL, sem("x_scaled"))
                for k in range(KT):
                    dve.wait_ge(sem("x_high"), KT * (rnd + 1) + k + 1)
                    stt(low[:, k, :], x[:, k, :], mod[:, shift + k:shift + k + 1], high[:, k, :].bitcast(F32), ADD, SUB,
                        sem("x_split"))

            add_normed(1, "post_mix", yb)
            norm_scale(2)
            for k in range(KT):
                stt(hn[:, k, :], h[:, k, :], col("pre_ffn", k), rs[:, 1, :], MUL, MUL, sem("hn_ready"))
            for k in range(KT):
                low_part(8 + k, hn_lo[:, k, :], hn[:, k, :], hn_hi[:, k, :])
            for n, (l, sc, gn) in enumerate(((0, 1, cols("norm1", 8)), (0, 4, cols("norm2", 8)), (2, 1, cols("kv_norm", 8)),
                                             (1, 1, cols("norm1", 8, 8)), (1, 4, cols("norm2", 8, 8)))):
                c0 = 48 * l + 8 * sc
                stt(gsc[:, 8 * n:8 * n + 8], mod[:, c0:c0 + 8], 1.0, gn, ADD, MUL, sem("gains"))
            ffn(0)
            dve.wait_ge(sem("late_consts"), 1)
            rec(inv_count[:, :, :], inv_count[:, :, :])
            for br, low in ((1, 3), (2, 15)):
                m = bdist[:, br, :, :]
                led.emit(v.tensor_scalar(m.bitcast(mybir.dt.int32), dint.bitcast(mybir.dt.int32), low, None,
                                         ALU.bitwise_and))
            settle()
            for br in (1, 2):
                m = bdist[:, br, :, :]
                ts(m, m.bitcast(mybir.dt.int32), 1.0, ALU.min, FAR, MUL)
            settle()
            for br in (1, 2):
                tt(bdist[:, br, :, :], bdist[:, br, :, :], dist[:, :, :], ALU.max)
            add_normed(3, "post_ffn", yb)
            for k in range(KT):
                low_part(16 + k, hn_lo[:, k, :], h[:, k, :], hn_hi[:, k, :])
            norm_scale(4)
            for k in range(KT):
                stt(eb[:, k, :], eb[:, k, :], col("ple_norm", k), rs[:, 1, :], MUL, MUL)
            settle()
            for m in range(8):
                placed(("pg", m))
                stt(yb[:, m, :], yb[:, m, :], 1.0, eb[:, m, :], ADD, MUL)
            settle()
            for m in range(8):
                stt(h[:, m, :], yb[:, m, :], 0.5, h[:, m, :], MUL, ADD, sem("h_ready"))

            norm_scale(5)
            modulated(0, 3, hn, hn_lo, hn_hi, 0)
            for gq in range(4):
                for i in range(2):
                    placed(("pi", 2 * gq + i))
                src = pu[:, 2 * gq:2 * gq + 2, :]
                for l in range(gq + 1):
                    sh, o = 2 ** l, pw[:, l % 2]
                    copy(o[:, :, 0:sh], src[:, :, 0:sh])
                    tt(o[:, :, sh:T], src[:, :, sh:T], src[:, :, 0:T - sh], ADD)
                    settle()
                    src = o
                tt(src, src, inv_count[:, gq, :].unsqueeze(1).broadcast_to([P, 2, T]), MUL)
                settle()
                for i in range(2):
                    tt(pu[:, 2 * gq + i, :], src[:, i, :], pu[:, 2 * gq + i, :], SUB, sem("pooled"))
                settle()
            for m in range(8):
                placed(("pp", m))
                low_part(32 + m, eT_lo[:, m, :], eT[:, m, :], hn_hi[:, m, :])
            for m in range(8):
                b = take(("po", m))
                stt(h[:, m, :], b[:, 0:T], mc(0, 2, m), h[:, m, :], MUL, ADD, *freed(("po", m)))
            settle()
            norm_scale(6)
            modulated(1, 5, hn, hn_lo, hn_hi, 24)
            ffn(1)
            settle()
            norm_scale(7)
            modulated(2, 6, hn, hn_lo, hn_hi, 96)
            modulated(3, 7, hn2, hn2_lo, hn2_hi, 48)

            slopes48 = dilated_slopes(48)

            def dil_bias(i):
                hh, s, u = i // 2, i % 2, i % 2
                nk = P * (s + 1)
                if i >= 2:
                    dve.wait_ge(psum_ready, job_no["dp", i - 2, s] + 1)
                for job, brs in (("da", (0, 1)), ("db", (2,))):
                    b = take((job, i))
                    for br in brs:
                        last = br != 0
                        o = T * (br % 2)
                        stt(dsc[:, u, br * nk:br * nk + nk], bdist[:, br, s, 0:nk], -float(slopes48[16 * br + hh]),
                            b[:, o:o + nk], MUL, ADD, *(freed((job, i)) if last else (None, None)))
                settle()
                led.emit(v.tensor_reduce(dst[:, i % 4, 0:1], dsc[:, u, 0:3 * nk], AX.X, ALU.max, negate=True),
                         sem("dil_max"))

            def dil_out(i):
                hh, s, u = i // 2, i % 2, i % 2
                if s:
                    b = take(("dp", i, 1))
                    if i >= 2:
                        dve.wait_ge(psum_ready, job_no["dy", i - 2] + 1)
                    copy(dpt[:, u, 3:6, :], three(b), *freed(("dp", i, 1)))
                dve.wait_ge(sem("dil_probs"), i + 1)
                rec(dst[:, i % 4, 2:3], dst[:, i % 4, 1:2])
                settle()
                b = take(("dy", i))
                ts(dotok[:, s, HD * hh:HD * hh + HD], b[:, 0:HD], dst[:, i % 4, 2:3], MUL,
                   signal=freed(("dy", i))[0], value=freed(("dy", i))[1])

            dil_bias(0)
            for i in range(32):
                if i < 31:
                    dil_bias(i + 1)
                dil_out(i)
            for m in range(8):
                placed(("dt", m // 2))
                low_part(64 + m, hn_lo[:, m, :], hn[:, m, :], hn_hi[:, m, :])
            for m in range(8):
                b = take(("dw", m))
                stt(h[:, m, :], b[:, 0:T], mc(1, 2, m), h[:, m, :], MUL, ADD, *freed(("dw", m)))
            settle()
            norm_scale(8)
            modulated(4, 9, hn, hn_lo, hn_hi, 72)
            ffn(2)
            settle()
            norm_scale(9)
            for k in range(KT):
                stt(hn[:, k, :], h[:, k, :], col("final", k), rs[:, 1, :], MUL, MUL, sem("hn_ready"))
            for s in range(2):
                b = take(("fin", 2 * s))
                copy(outt[:, s, 0:512], b, *freed(("fin", 2 * s)))

        @block.scalar
        def _(act_):
            led = Ledger(act_, sem("act_own"))
            take0 = taker(act_)
            sum_jobs = sorted((n, job) for job, n in job_no.items() if job[0] == "ada")
            settle = led.settle

            def af(o, x, func=ACT.Identity, signal=None, value=None, **k):
                led.emit(nc.scalar.activation(o, x, func, **k), signal, value)

            def sums_before(job):
                while sum_jobs and sum_jobs[0][0] < job_no[job]:
                    aj = sum_jobs.pop(0)[1]
                    b = take0(aj)
                    if aj[1] >= 2:
                        act_.wait_ge(psum_ready, job_no["adc", aj[1] - 2] + 1)
                    af(sums[:, aj[1] % 2, :], b, ACT.Identity, *freed(aj))

            split_order = sorted(split_no, key=split_no.get)
            chunk_order = sorted(chunk_no, key=chunk_no.get)
            high_done = [0]

            def reach(job):
                sums_before(job)
                while high_done[0] < len(split_order):
                    n = high_done[0]
                    key = split_order[n]
                    before = [split_order[n - HI_SLOTS]] if n >= HI_SLOTS else []
                    earlier = before + chunk_order[max(0, chunk_no[key] - SLOTS):max(0, chunk_no[key] - SLOTS + 1)]
                    if any(used_at[x] >= job_no[job] for x in earlier) or job_no[job] <= job_no["ol", 1]:
                        break
                    if n == 0:
                        act_.wait_ge(psum_ready, job_no["ol", 1] + 1)
                    for x in before:
                        act_.wait_ge(*chunk_used[x])
                    act_.wait_ge(*chunk_landed[key])
                    raw, _, high = chunk_flat(key)
                    af(high, raw, ACT.Identity, sem("hi_ready"))
                    high_done[0] += 1

            def take(job):
                reach(job)
                return take0(job)

            def gone(job):
                reach(job)
                act_.wait_ge(*freed(job))

            def high_part(x_hi, x, **k):
                af(x_hi, x, ACT.Identity, sem("x_high"), **k)

            act_.wait_ge(sem("stage_clear"), 2)
            stage_rows(act_, soon[1::2], sem("soon_in"))

            def sqrt_table():
                settle()
                af(drv[:, 21:22], eps_col, ACT.Sqrt)

            def squares(dst_, after):
                sqrt_table()
                for f in range(4):
                    after(2 * f)
                    after(2 * f + 1)
                    af(dst_[:, 2 * f:2 * f + 2, :], h[:, 2 * f:2 * f + 2, :], ACT.Square, sem("squares"))

            def root(i):
                b = take(("ms", i))
                af(rs[:, 0, :], b[:, 0:T], ACT.Sqrt, *freed(("ms", i)), bias=eps_col)

            squares(hn, lambda k: act_.wait_ge(*freed(("xT", k // 2))))
            def early_high(c):
                if c >= 2:
                    act_.wait_ge(*chunk_used[early[c - 2]])
                act_.wait_ge(*chunk_landed[early[c]])
                raw, _, high = chunk_flat(early[c])
                af(high, raw, ACT.Identity, sem("early_hi"))

            stage_rows(act_, later[1::2], sem("later_in"))
            act_.dma_start(dt_rows[0:8, :], a["s5_log_dt"].rearrange("l (j g) -> (l j) g", g=2)).then_inc(sem("later_in"), 16)
            early_high(0)
            early_high(1)
            root(0)
            for k in range(KT):
                act_.wait_ge(sem("hn_ready"), k + 1)
                high_part(hn_hi[:, k, :], hn[:, k, :])
            af(cond[:, :], cols("c", 8), ACT.Tanh, sem("cond_tanh"), scale=0.5)
            act_.wait_ge(*freed(("par", 1)))
            af(s5v[:, 0, :], cols("log_dt", 8), ACT.Exp, sem("s5_dt"))
            act_.wait_ge(sem("s5_lr"), 1)
            af(s5v[:, 2, :], s5v[:, 1, :], ACT.Exp)
            act_.wait_ge(sem("s5_angle"), 1)
            af(s5v[:, 7, :], s5v[:, 5, :], ACT.Sin, sem("theta_ready"))
            af(s5v[:, 8, :], s5v[:, 6, :], ACT.Sin, sem("theta_ready"))
            act_.wait_ge(sem("derived"), 1)

            def rw(i):
                b = take(("rw", i))
                af(zs[:, i, :], b[:, 0:T], ACT.Identity, sem("shift_own"), scale=omm(i))

            def q_(i):
                b = take(("q", i))
                af(qT[:, i, :], b[:, 0:T], ACT.Identity, *freed(("q", i)), scale=0.125)

            def vtok_(s):
                b = take(("vtok", s))
                af(vtok[:, s, :], b[:, 0:T], ACT.Identity, *freed(("vtok", s)))

            def kc_(i):
                b = take(("kc", i))
                af(kcs[0:64, i, :], b[0:64, 0:T])
                af(kcs[64:128, i, 0:T - 1], b[64:128, 1:T], ACT.Identity, *freed(("kc", i)))

            def kd_(i):
                b = take(("kd", i))
                af(kd[:, i, :], b[:, 0:T], ACT.Identity, *freed(("kd", i)))

            def u_(i):
                b = take(("u", i))
                af(uT[:, i, :], b[:, 0:T], ACT.Identity, *freed(("u", i)))

            def gtok_(_):
                b = take(("gtok",))
                af(gate[:, :, :].rearrange("p a b -> p (a b)"), b[:, 0:36], ACT.Tanh, *freed(("gtok",)), scale=0.5)

            jobs = [(rw, i) for i in range(11)] + [(q_, i) for i in range(3)]
            by_chunk = [jobs[2 * c:2 * c + 2] for c in range(7)] + [[(vtok_, 0), (vtok_, 1)]] + \
                [[(kc_, 0), (kc_, 1)], [(kc_, 2), (kc_, 3)], [(kd_, 0), (kd_, 1)], [(kd_, 2), (kd_, 3)]] + \
                [[(gtok_, 0)], [(u_, 0), (u_, 1)]]
            for c, readers in enumerate(by_chunk):
                if 1 <= c < len(early) - 1:
                    early_high(c + 1)
                for reader, i in readers:
                    reader(i)
            act_.wait_ge(*freed(("rw", 9)))
            af(zs[0:64, 9, :], zs[0:64, 9, :], ACT.Tanh, sem("lora_tanh"))
            act_.wait_ge(*freed(("rw", 10)))
            af(zs[:, 10, :], zs[:, 10, :], ACT.Tanh, sem("lora_tanh"), scale=0.5)
            b = take(("cmq",))
            act_.wait_ge(sem("tables"), 2)
            for i in range(4):
                q = slice(32 * i, 32 * i + NCMP)
                af(chid[q, :], b[q, 0:P], ACT.Identity, *(freed(("cmq",)) if i == 3 else (None, None)))
            b = shaped(take(("cmph",))[:, 0:P], 4, 32)[:, :, 0:NCMP]
            af(hid[:, 0:2, 0:NCMP], b[:, 0:2, :], ACT.Gelu_apprx_tanh)
            af(hidv[:, :, :, 0:NCMP], b[:, 2:4, :].unsqueeze(2).broadcast_to([P, 2, 3, NCMP]), ACT.Gelu_apprx_tanh,
               *freed(("cmph",)))
            b = take(("kcT",))
            af(kcT[:, :, :], shaped(b[:, 0:30], 2, NCMP), ACT.Identity, *freed(("kcT",)))
            for s in range(2):
                reach(("cs", 1, 1))
                act_.wait_ge(sem("cmp_shifted"), s + 1)
                af(csc[:, s, :, 0:NCMP], csc[:, s, :, 0:NCMP], ACT.Exp, sem("cmp_exp"))

            def nsa_exp(i):
                s, u = i // 6, i % 2
                nk = P * (s + 1)
                reach(("ns", i))
                act_.wait_ge(sem("nsa_max"), i + 1)
                for br in range(2):
                    af(nsc[:, u, br, 0:nk], nsc[:, u, br, 0:nk], ACT.Exp, sem("nsa_probs") if br else None,
                       bias=nst[:, i % 4, 0, br:br + 1], accum_out=nst[:, i % 4, 1, br:br + 1])

            def nsa_copy(i):
                s, u = i // 6, i % 2
                b = take(("np", i))
                if i >= 2:
                    act_.wait_ge(psum_ready, job_no["nv", i - 2] + 1)
                af(npt[:, u].rearrange("p (a b) c -> p a b c", a=2)[:, :, 0:s + 1, :],
                   shaped(b, 2, 2, P)[:, :, 0:s + 1, :], ACT.Identity, *freed(("np", i)))

            nsa_exp(0)
            for i in range(12):
                nsa_copy(i)
                if i < 11:
                    nsa_exp(i + 1)
                if i == 2:
                    for f in range(2):
                        for j in range(4 * f, 4 * f + 4):
                            reach(("y5", j))
                            act_.wait_ge(*freed(("y5", j)))
                        af(ygel[:, f, :], ygel[:, f, :], ACT.Gelu_apprx_tanh, sem("ygel_ready"))
                elif i == 5:
                    for m in range(2):
                        b = take(("glu", 2 + m))
                        af(s5g[:, m, :], b[:, 0:T], ACT.Tanh, *freed(("glu", 2 + m)), scale=0.5)
                elif i == 6:
                    for c in range(3):
                        b = take(("wp", c))
                        af(W[0][:, c, :], b[:, 0:T], ACT.Tanh, *freed(("wp", c)), scale=0.5, bias=hw0(c))
                elif i == 7:
                    for c in range(3):
                        b = take(("ap", c))
                        af(W[3][:, c, :], b[:, 0:T], ACT.Tanh, *freed(("ap", c)), scale=0.5, bias=ha0(c))
                    for c in range(3):
                        b = take(("gp", c))
                        af(W[10][:, c, :], b[:, 0:T], ACT.Identity, *freed(("gp", c)))
                    reach(("gp", 2))
                    act_.wait_ge(sem("logs"), 1)
                    af(W[2], W[1], ACT.Exp, sem("exps"), scale=-1.0)
                    af(W[0], W[0], ACT.Exp, sem("exps"))
                    af(W[1], W[1], ACT.Exp, sem("exps"))
                elif i == 8:
                    reach(("kks", 2))
                    act_.wait_ge(sem("kk_rec"), 1)
                    af(W[5], W[5], ACT.Sqrt, sem("kk_root"))
            for c in range(3):
                b = take(("oT", c))
                high_part(hn_hi[:, 3 + c, :], b[:, 0:T])
                af(hn[:, 3 + c, :], b[:, 0:T], ACT.Identity, *freed(("oT", c)))
            for m in range(2):
                gone(("glu", m))
                high_part(hn_hi[:, 6 + m, :], hn[:, 6 + m, :])

            for s in range(2):
                for x in range(4):
                    b = take(("tk", s, x))
                    o = AM[:, :, 0, :] if x == 0 else tok4[:, x]
                    af(o, shaped(b[:, 0:384], 3, P), ACT.Identity, *freed(("tk", s, x)))
                for name, _l, _r, add, dst_ in INV:
                    if add is not None:
                        continue
                    b = take((name, s, 1))
                    af(tmat(dst_)[:, 1], shaped(b[:, 0:384], 3, P), ACT.Identity, *freed((name, s, 1)))
                b = take(("au", s, 1))
                af(AU[:, :, :, HD:P], shaped(b[:, 0:384], 3, 2, HD), ACT.Identity, *freed(("au", s, 1)))
                b = take(("ol", s))
                af(zs[:, 0:3, s * P:s * P + P], shaped(b[:, 0:384], 3, P), ACT.Identity, *freed(("ol", s)))
            for c in range(3):
                reach(("gm", c))
                act_.wait_ge(*freed(("gm", c)))
                af(zs[:, 3 + c, :], zs[:, c, :], ACT.Square, sem("gn_sq"))
            reach(("gv", 2))
            for c in range(3):
                act_.wait_ge(sem("gn_rec"), c + 1)
                af(zs[:, 6 + c, :], zs[:, 6 + c, :], ACT.Sqrt, sem("gn_root"))

            reach(("gv", 2))
            for c in range(3):
                act_.wait_ge(sem("mix_rw"), c + 1)
                high_part(hn_hi[:, c, :], hn[:, c, :])

            def out_squares(jobs, y):
                sqrt_table()
                for k, job in enumerate(jobs):
                    b = take(job)
                    af(sqb[:, k, :], b[:, 0:T], ACT.Square, sem("squares") if k % 2 else None)
                    af(y[:, k, :], b[:, 0:T], ACT.Identity, *freed(job))

            def h_at(n):
                return lambda k: act_.wait_ge(sem("h_ready"), 8 * n + k + 1)

            def modulate(n, high, x, sh):
                for k in range(KT):
                    act_.wait_ge(sem("x_scaled"), 8 * n + k + 1)
                    high_part(high[:, k, :], x[:, k, :], bias=mod[:, sh + k:sh + k + 1])

            def ffn(f):
                W0, B0, n = (row0["conv_w"], row0["conv_b"], 44) if f == 0 else \
                    (row0["fconv_w"] + 66 * (f - 1), row0["fconv_b"] + 22 * (f - 1), 22)
                parts = ("ug", "uu") if f == 0 else ("ug",)

                def own(j):
                    for x, nm in enumerate(parts):
                        b = take((nm, f, j))
                        if j >= 2:
                            act_.wait_ge(*((sem("act_ready"), j - 1) if f == 0 else freed(("uu", f, j - 2))))
                        w, bc = W0 + 2 * n + 22 * x + j, B0 + 22 * x + j
                        af(ct[:, j % 2, x, :], b[:, 0:T], ACT.Identity, sem("conv_own"), scale=par[:, w:w + 1],
                           bias=par[:, bc:bc + 1])

                def gated(j):
                    act_.wait_ge(*freed(("ug", f, j)))
                    t = ct[:, j % 2, 0, :]
                    af(t, t, ACT.Gelu_apprx_tanh if f == 0 else ACT.Silu, sem("gate_act"))

                for j in range(FT):
                    own(j)
                    if j:
                        gated(j - 1)
                gated(FT - 1)

            out_squares([("out", m) for m in range(8)], yb)
            root(1)
            squares(hn, h_at(0))
            root(2)
            for k in range(KT):
                act_.wait_ge(sem("hn_ready"), 8 + k + 1)
                high_part(hn_hi[:, k, :], hn[:, k, :])
            ffn(0)
            out_squares([("down", 0, m) for m in range(8)], yb)
            root(3)
            for k in range(KT):
                act_.wait_ge(sem("h_ready"), 8 + k + 1)
                high_part(hn_hi[:, k, :], h[:, k, :])
            out_squares([("pl", m) for m in range(8)], eb)
            root(4)
            for m in range(8):
                b = take(("pg", m))
                af(yb[:, m, :], b[:, 0:T], ACT.Tanh, *freed(("pg", m)), scale=0.5)
            squares(hn, h_at(2))
            root(5)
            modulate(0, hn_hi, hn, 0)
            for m in range(8):
                b = take(("pi", m))
                af(pu[:, m, :], b[:, 0:T], ACT.Identity, *freed(("pi", m)))
            for m in range(8):
                b = take(("pp", m))
                high_part(hn_hi[:, m, :], b[:, 0:T], scale=col("pool_scale", m))
                af(eT[:, m, :], b[:, 0:T], ACT.Identity, *freed(("pp", m)), scale=col("pool_scale", m))
            squares(hn, lambda k: gone(("po", k)))
            root(6)
            modulate(1, hn_hi, hn, 24)
            ffn(1)
            squares(hn, lambda k: gone(("down", 1, k)))
            root(7)
            modulate(2, hn_hi, hn, 96)
            modulate(3, hn2_hi, hn2, 48)

            def projected(c):
                u = c % 2
                for br in range(3):
                    for i in range(2):
                        b = take(("dk", c, br, i))
                        yield af(dk[:, u, 2 * br + i, :], b[:, 0:T], ACT.Identity, *freed(("dk", c, br, i)))
                for br in range(3):
                    for s in range(2):
                        b = take(("dv", c, br, s))
                        yield af(dv[:, u, s, br, :], b[:, 0:T], ACT.Identity, *freed(("dv", c, br, s)))
                for br in range(3):
                    for i in range(2):
                        b = take(("dq", c, br, i))
                        yield af(dq[:, u, 2 * br + i, :], b[:, 0:T], ACT.Identity, *freed(("dq", c, br, i)),
                                 scale=0.125)

            for _ in projected(0):
                pass

            def dil_exp(i):
                s, u = i % 2, i % 2
                n = 3 * P * (s + 1)
                reach(("db", i))
                act_.wait_ge(sem("dil_max"), i + 1)
                af(dsc[:, u, 0:n], dsc[:, u, 0:n], ACT.Exp, sem("dil_probs"), bias=dst[:, i % 4, 0:1],
                   accum_out=dst[:, i % 4, 1:2])

            dil_exp(0)
            for i in range(32):
                b = take(("dp", i, 0))
                if i >= 2:
                    act_.wait_ge(psum_ready, job_no["dy", i - 2] + 1)
                af(dpt[:, i % 2, 0:3, :], shaped(b[:, 0:384], 3, P), ACT.Identity, *freed(("dp", i, 0)))
                if i < 31:
                    dil_exp(i + 1)
                if i % 8 == 0:
                    coming = projected(i // 8 + 1) if i < 24 else iter(())
                for _ in range(proj_share(i)):
                    next(coming, None)
            for j in range(4):
                b = take(("dt", j))
                for k in range(2):
                    high_part(hn_hi[:, 2 * j + k, :], b[:, k * T:k * T + T])
                af(hn[:, 2 * j:2 * j + 2, :], shaped(b, 2, T), ACT.Identity, *freed(("dt", j)))
            squares(hn2, lambda k: gone(("dw", k)))
            root(8)
            modulate(4, hn_hi, hn, 72)
            ffn(2)
            squares(hn, lambda k: gone(("down", 2, k)))
            root(9)
            for s in range(2):
                b = take(("fin", 2 * s + 1))
                af(outt[:, s, 512:1024], b, ACT.Identity, *freed(("fin", 2 * s + 1)))


_INS = ['x', 'p', 'pre_mix_norm', 'post_mix_norm', 'pre_ffn_norm', 'post_ffn_norm', 'w_in', 'w_out', 'shift_mu',
        'rw_w0', 'rw_w2', 'rw_a0', 'rw_a2', 'rw_g2', 'rw_k_k', 'rw_k_a', 'rw_r_k', 'rw_gn_w', 'rw_gn_b', 'cmp_pe_k',
        'cmp_pe_v', 'cmp_w1_k', 'cmp_w2_k', 'cmp_w1_v', 'cmp_w2_v', 's5_lam_re', 's5_lam_im', 's5_log_dt', 's5_b_re',
        's5_b_im', 's5_c_re', 's5_c_im', 's5_d', 's5_w_glu', 'w_up', 'conv_w', 'conv_b', 'w_down', 'w_ple', 'ple_norm',
        'w_ple_gate', 'c_2', 'ada_w_2', 'ada_b_2', 'norm1_g_2', 'norm2_g_2', 'pool_w_in_2', 'pool_w_grp_2',
        'pool_scale_2', 'pool_w_out_2', 'kv_norm_g_2', 'kv_ada_w_2', 'kv_ada_b_2', 'w_kv_2', 'attn_w_q_2',
        'attn_w_o_2', 'ffn_w_up_2', 'ffn_conv_w_2', 'ffn_conv_b_2', 'ffn_w_down_2', 'final_g_2']


def kernel(**inputs):
    import numpy as _np
    import concourse.bacc as _bacc
    from concourse import mybir as _mybir
    from concourse.bass_utils import run_bass_kernel_spmd as _run

    nc = _bacc.Bacc("TRN2", target_bir_lowering=False, num_devices=1)
    arrays, args = {}, {}
    for name in _INS:
        a = _np.ascontiguousarray(inputs[name])
        arrays[f"in_{name}_dram"] = a
        args[name] = nc.dram_tensor(f"in_{name}_dram", a.shape, _mybir.dt.from_np(a.dtype), kind="ExternalInput").ap()
    out = nc.dram_tensor("out_0_dram", (1, T, D), _mybir.dt.float32, kind="ExternalOutput").ap()
    two_block_kernel(nc, args, out)
    r = _run(nc, [arrays], core_ids=[0])
    return r.results[0]["out_0_dram"]
```
